# Optimizing a Trainium2 kernel written in Bass

```python
import jax, jax.numpy as jnp
from jax import lax
import numpy as np

D_MODEL = 1024
BATCH = 1
SEQ = 2048
DEPTH = 1

EPS = 1e-6
HEAD_DIM = 64
LRU_WIDTH = 384
LRU_BLOCKS = 6
LRU_BLOCK = LRU_WIDTH // LRU_BLOCKS
CONV_WIDTH = 4
LRU_C = 8.0
FOX_HEADS = 6
FOX_WIDTH = FOX_HEADS * HEAD_DIM
Q_BLOCK = 128
GLA_HEADS = 4
GLA_DK = 64
GLA_DV = 64
GLA_KW = GLA_HEADS * GLA_DK
GLA_VW = GLA_HEADS * GLA_DV
GLA_RANK = 16
GLA_TAU = 16.0
GLA_CHUNK = 64
D_MIX = LRU_WIDTH + FOX_WIDTH + GLA_VW
SPLIT_SIZES = (LRU_WIDTH, LRU_WIDTH, FOX_WIDTH, FOX_WIDTH, FOX_WIDTH, FOX_HEADS,
               GLA_KW, GLA_KW, GLA_VW, GLA_RANK, GLA_VW)
D_IN = sum(SPLIT_SIZES)
D_FF = -(-8 * D_MODEL // (3 * 256)) * 256
N_MOD = 6

kernel_name = 'hybrid_rglru_fox_gla_block'

def rms_norm(x, gain):
    xf = x.astype(jnp.float32)
    y = xf * lax.rsqrt(jnp.mean(xf * xf, axis=-1, keepdims=True) + EPS)
    return (y * gain.astype(jnp.float32)).astype(x.dtype)

def causal_depthwise_conv(x, w, b):
    S = x.shape[1]
    K = w.shape[0]
    xp = jnp.pad(x, ((0, 0), (K - 1, 0), (0, 0)))
    out = xp[:, K - 1:K - 1 + S] * w[K - 1] + b
    for j in range(K - 1):
        out = out + xp[:, j:j + S] * w[j]
    return out

def rg_lru(x, w_r, b_r, w_i, b_i, lam):
    B, S, _ = x.shape
    xb = x.reshape(B, S, LRU_BLOCKS, LRU_BLOCK)
    r = jax.nn.sigmoid(jnp.einsum('bsnd,nde->bsne', xb, w_r).reshape(B, S, LRU_WIDTH) + b_r)
    i = jax.nn.sigmoid(jnp.einsum('bsnd,nde->bsne', xb, w_i).reshape(B, S, LRU_WIDTH) + b_i)
    log_a = (-LRU_C * r.astype(jnp.float32) * jax.nn.softplus(-lam.astype(jnp.float32)))
    a = jnp.exp(log_a)
    mult = jnp.sqrt(-jnp.expm1(2.0 * log_a))
    u = mult * (i * x).astype(jnp.float32)

    def combine(left, right):
        a1, b1 = left
        a2, b2 = right
        return a1 * a2, a2 * b1 + b2

    _, h = lax.associative_scan(combine, (a, u), axis=1)
    return h.astype(x.dtype)

def forgetting_attention(q, k, v, f_logit, b_f, q_gain, k_gain):
    B, S, _ = q.shape
    q = rms_norm(q.reshape(B, S, FOX_HEADS, HEAD_DIM), q_gain).transpose(0, 2, 1, 3)
    k = rms_norm(k.reshape(B, S, FOX_HEADS, HEAD_DIM), k_gain).transpose(0, 2, 1, 3)
    v = v.reshape(B, S, FOX_HEADS, HEAD_DIM).transpose(0, 2, 1, 3)
    log_f = jax.nn.log_sigmoid((f_logit + b_f).astype(jnp.float32))
    cum = jnp.cumsum(log_f, axis=1).transpose(0, 2, 1)
    scale = HEAD_DIM ** -0.5
    k_pos = jnp.arange(S)

    def one_block(start):
        qb = lax.dynamic_slice_in_dim(q, start, Q_BLOCK, axis=2)
        cb = lax.dynamic_slice_in_dim(cum, start, Q_BLOCK, axis=2)
        s = (jnp.einsum('bhqd,bhkd->bhqk', qb, k).astype(jnp.float32) * scale
             + cb[..., :, None] - cum[..., None, :])
        q_pos = start + jnp.arange(Q_BLOCK)
        s = jnp.where(k_pos[None, :] <= q_pos[:, None], s, -jnp.inf)
        p = jax.nn.softmax(s, axis=-1)
        return jnp.einsum('bhqk,bhkd->bhqd', p.astype(v.dtype), v)

    starts = jnp.arange(S // Q_BLOCK) * Q_BLOCK
    o = lax.map(one_block, starts)
    return o.transpose(1, 0, 3, 2, 4).reshape(B, S, FOX_WIDTH)

def gated_linear_attention(q, k, v, low, g, w_alpha, b_alpha, out_gain):
    B, S, _ = q.shape
    nc = S // GLA_CHUNK

    def to_chunks(t, d):
        return t.reshape(B, nc, GLA_CHUNK, GLA_HEADS, d).transpose(0, 3, 1, 2, 4).astype(jnp.float32)

    log_alpha = jax.nn.log_sigmoid((low @ w_alpha + b_alpha).astype(jnp.float32)) / GLA_TAU
    qh = to_chunks(q, GLA_DK) * (GLA_DK ** -0.5)
    kh = to_chunks(k, GLA_DK)
    vh = to_chunks(v, GLA_DV)
    la = to_chunks(log_alpha, GLA_DK)
    bcum = jnp.cumsum(la, axis=3)
    b_last = bcum[..., -1:, :]
    q_dec = qh * jnp.exp(bcum)
    k_dec = kh * jnp.exp(-bcum)
    k_to_end = kh * jnp.exp(b_last - bcum)
    att = jnp.einsum('bhnid,bhnjd->bhnij', q_dec, k_dec)
    att = jnp.where(jnp.tril(jnp.ones((GLA_CHUNK, GLA_CHUNK), dtype=bool)), att, 0.0)
    o_intra = jnp.einsum('bhnij,bhnjv->bhniv', att, vh)
    kv = jnp.einsum('bhnjd,bhnjv->bhndv', k_to_end, vh)
    decay = jnp.exp(b_last[..., 0, :])

    def step(state, inp):
        dec, kv_n = inp
        return dec[..., None] * state + kv_n, state

    init = jnp.zeros((B, GLA_HEADS, GLA_DK, GLA_DV), jnp.float32)
    _, s_prev = lax.scan(step, init, (decay.transpose(2, 0, 1, 3), kv.transpose(2, 0, 1, 3, 4)))
    s_prev = s_prev.transpose(1, 2, 0, 3, 4)
    o_inter = jnp.einsum('bhnid,bhndv->bhniv', q_dec, s_prev)
    o = (o_intra + o_inter).transpose(0, 2, 3, 1, 4).reshape(B, S, GLA_HEADS, GLA_DV)
    o = rms_norm(o, out_gain).reshape(B, S, GLA_VW)
    return (o * jax.nn.silu(g.astype(jnp.float32))).astype(q.dtype)

def hybrid_layer(x, c_act, norm1_gain, norm2_gain, w_mod, b_mod, w_in, conv_w, conv_b,
                 lru_w_r, lru_b_r, lru_w_i, lru_b_i, lru_lambda, fox_b_f, fox_q_gain,
                 fox_k_gain, gla_w_alpha, gla_b_alpha, gla_out_gain, w_out,
                 ffn_w_gate_up, ffn_w_down):
    mod = (c_act @ w_mod + b_mod)[:, None, :]
    shift1, scale1, gate1, shift2, scale2, gate2 = jnp.split(mod, N_MOD, axis=-1)

    h = rms_norm(x, norm1_gain) * (1.0 + scale1) + shift1
    proj = h @ w_in
    (xa, ya, fq, fk, fv, ff, gq, gk, gv, glow, gg) = jnp.split(
        proj, np.cumsum(SPLIT_SIZES)[:-1].tolist(), axis=-1)
    xa = causal_depthwise_conv(xa, conv_w, conv_b)
    out_a = rg_lru(xa, lru_w_r, lru_b_r, lru_w_i, lru_b_i, lru_lambda) * jax.nn.gelu(ya)
    out_b = forgetting_attention(fq, fk, fv, ff, fox_b_f, fox_q_gain, fox_k_gain)
    out_c = gated_linear_attention(gq, gk, gv, glow, gg, gla_w_alpha, gla_b_alpha, gla_out_gain)
    mix = jnp.concatenate([out_a, out_b, out_c], axis=-1) @ w_out
    x = x + gate1 * mix

    h = rms_norm(x, norm2_gain) * (1.0 + scale2) + shift2
    gt, up = jnp.split(h @ ffn_w_gate_up, 2, axis=-1)
    x = x + gate2 * ((jax.nn.silu(gt) * up) @ ffn_w_down)
    return x

def setup_inputs(seed: int = 0) -> dict:
    key = jax.random.key(seed)
    ks = jax.random.split(key, 24)
    f32 = jnp.float32
    L = DEPTH

    def nrm(k, shape, fan_in, mult=1.0):
        return (jax.random.normal(k, shape, f32) * (mult * fan_in ** -0.5)).astype(f32)

    def gain(k, shape):
        return 1.0 + 0.02 * jax.random.normal(k, shape, f32)

    def small(k, shape):
        return 0.01 * jax.random.normal(k, shape, f32)

    a0 = jax.random.uniform(ks[12], (L, LRU_WIDTH), f32, minval=0.9, maxval=0.999)
    return {
        'x': jax.random.normal(ks[0], (BATCH, SEQ, D_MODEL), f32),
        'c': jax.random.normal(ks[1], (BATCH, D_MODEL), f32),
        'norm1_gain': gain(ks[2], (L, D_MODEL)),
        'norm2_gain': gain(ks[3], (L, D_MODEL)),
        'w_mod': nrm(ks[4], (L, D_MODEL, N_MOD * D_MODEL), D_MODEL, 0.5),
        'b_mod': small(ks[5], (L, N_MOD * D_MODEL)),
        'w_in': nrm(ks[6], (L, D_MODEL, D_IN), D_MODEL),
        'conv_w': nrm(ks[7], (L, CONV_WIDTH, LRU_WIDTH), CONV_WIDTH),
        'conv_b': small(ks[8], (L, LRU_WIDTH)),
        'lru_w_r': nrm(ks[9], (L, LRU_BLOCKS, LRU_BLOCK, LRU_BLOCK), LRU_BLOCK),
        'lru_b_r': small(ks[10], (L, LRU_WIDTH)),
        'lru_w_i': nrm(ks[11], (L, LRU_BLOCKS, LRU_BLOCK, LRU_BLOCK), LRU_BLOCK),
        'lru_b_i': small(ks[13], (L, LRU_WIDTH)),
        'lru_lambda': jnp.log(a0) - jnp.log1p(-a0),
        'fox_b_f': jax.random.uniform(ks[14], (L, FOX_HEADS), f32, minval=1.0, maxval=4.0),
        'fox_q_gain': gain(ks[15], (L, HEAD_DIM)),
        'fox_k_gain': gain(ks[16], (L, HEAD_DIM)),
        'gla_w_alpha': nrm(ks[17], (L, GLA_RANK, GLA_KW), GLA_RANK),
        'gla_b_alpha': small(ks[18], (L, GLA_KW)),
        'gla_out_gain': gain(ks[19], (L, GLA_DV)),
        'w_out': nrm(ks[20], (L, D_MIX, D_MODEL), D_MIX),
        'ffn_w_gate_up': nrm(ks[21], (L, D_MODEL, 2 * D_FF), D_MODEL),
        'ffn_w_down': nrm(ks[22], (L, D_FF, D_MODEL), D_FF),
    }

def reference(x, c, norm1_gain, norm2_gain, w_mod, b_mod, w_in, conv_w, conv_b,
              lru_w_r, lru_b_r, lru_w_i, lru_b_i, lru_lambda, fox_b_f, fox_q_gain,
              fox_k_gain, gla_w_alpha, gla_b_alpha, gla_out_gain, w_out,
              ffn_w_gate_up, ffn_w_down):
    c_act = jax.nn.silu(c)
    for l in range(DEPTH):
        x = hybrid_layer(x, c_act, norm1_gain[l], norm2_gain[l], w_mod[l], b_mod[l], w_in[l],
                         conv_w[l], conv_b[l], lru_w_r[l], lru_b_r[l], lru_w_i[l], lru_b_i[l],
                         lru_lambda[l], fox_b_f[l], fox_q_gain[l], fox_k_gain[l],
                         gla_w_alpha[l], gla_b_alpha[l], gla_out_gain[l], w_out[l],
                         ffn_w_gate_up[l], ffn_w_down[l])
    return x


_drawn_inputs = setup_inputs


def setup_inputs(seed=0):
    import zlib

    import numpy as np

    out = dict(_drawn_inputs(seed))
    spreads = {}
    factors = {'norm1_gain': 8.0,
     'norm2_gain': 30.571,
     'b_mod': 4.809,
     'conv_b': 47.222,
     'lru_b_r': 58.62,
     'lru_b_i': 54.409,
     'fox_q_gain': 53.002,
     'fox_k_gain': 42.829,
     'gla_w_alpha': 2.673,
     'gla_b_alpha': 64.0,
     'gla_out_gain': 23.784,
     'fox_b_f': 3.896}
    for name, (base, spread) in spreads.items():
        noise = np.random.default_rng([zlib.crc32(name.encode()), seed]).standard_normal(out[name].shape)
        drawn = base * np.exp(spread * noise) if base else spread * noise
        out[name] = __import__('jax').numpy.asarray(drawn.astype(out[name].dtype))
    for name, factor in factors.items():
        out[name] = (out[name] * factor).astype(out[name].dtype)
    return out
```

```python
from contextlib import ExitStack

import numpy as np

import concourse.bass as bass
from concourse import mybir

F32 = mybir.dt.float32
F32R = mybir.dt.float32r
U32 = mybir.dt.uint32
ALU = mybir.AluOpType
ACT = mybir.ActivationFunctionType
AX = mybir.AxisListType

P = 128
D_MODEL = 1024
SEQ = 2048
EPS = 1e-6
HEAD_DIM = 64
LRU_WIDTH = 384
CONV_WIDTH = 4
LRU_C = 8.0
FOX_HEADS = 6
GLA_HEADS = 4
GLA_RANK = 16
GLA_TAU = 16.0
GLA_CHUNK = 64
D_FF = 2816

KD = D_MODEL // P
KF = D_FF // P
BLK = 512
NBLK = SEQ // BLK
LRU_T = LRU_WIDTH // P
FOX_T = FOX_HEADS * HEAD_DIM // P
GLA_T = GLA_HEADS * HEAD_DIM // P
T_XA, T_YA = 0, LRU_T
T_FQ = T_YA + LRU_T
T_FK, T_FV = T_FQ + FOX_T, T_FQ + 2 * FOX_T
T_GQ = T_FV + FOX_T
T_GK, T_GV, T_GG = T_GQ + GLA_T, T_GQ + 2 * GLA_T, T_GQ + 3 * GLA_T
T_MISC = T_GG + GLA_T
N_PROJ = T_MISC + 1
FF_ROW = 32
MIX_T = LRU_T + FOX_T + GLA_T
MASKED = -1.0e30

C_MEAN, C_HEAD, C_IDENT, C_CAUSAL, C_CHUNK = range(5)
N_CONST = 5

C_MEAN, C_HEAD, C_IDENT, C_CAUSAL, C_CHUNK = range(5)
N_CONST = 5

C_MEAN, C_HEAD, C_IDENT, C_CAUSAL, C_CHUNK = range(5)
N_CONST = 5

VEC = {}
_at = 0
for _name, _n in (("c", KD), ("g1", KD), ("g2", KD), ("b_mod", 6 * KD), ("conv_w", CONV_WIDTH * LRU_T),
                  ("conv_b", LRU_T), ("b_r", LRU_T), ("b_i", LRU_T), ("lam", LRU_T), ("q_gain", 1),
                  ("k_gain", 1), ("b_alpha", GLA_T), ("out_gain", 1), ("b_f", 1)):
    VEC[_name] = _at
    _at += _n
N_VEC = _at

MOD_COLS = 256
MOD_CHUNKS = 6 * D_MODEL // MOD_COLS
SHIFT1, SCALE1, GATE1, SHIFT2, SCALE2, GATE2 = (i * KD for i in range(6))


def split_products(nc, out, hi, lo, act_hi, act_lo, first, last):
    nc.tensor.matmul(out, hi, act_hi, start=first, stop=False)
    nc.tensor.matmul(out, hi, act_lo, start=False, stop=False)
    return nc.tensor.matmul(out, lo, act_hi, start=False, stop=last)


def project_in(nc, vec, mod, xT, w_mod, w_in, consts, vec_in, proj):
    with ExitStack() as ctx:
        sb = lambda n, s, d=F32: ctx.enter_context(nc.sbuf_tensor(n, s, d))
        ps = lambda n, s, d=F32: ctx.enter_context(nc.psum_tensor(n, s, d))
        sem = lambda n: ctx.enter_context(nc.semaphore(n))
        two = lambda n: [sem(n + "_even"), sem(n + "_odd")]

        h_hi = sb("h_hi", [P, KD, SEQ], F32R)
        h_lo = sb("h_lo", [P, KD, SEQ], F32R)
        x_blk = sb("x_blk", [P, 2, KD * BLK])
        shared = sb("shared", [P, 2 * KD * MOD_COLS])
        w_hi = sb("w_hi", [P, 2, KD, P], F32R)
        w_lo = sb("w_lo", [P, 2, KD, P], F32R)
        mod_acc = sb("mod_acc", [P, 2, MOD_COLS])
        mean_ones = sb("mean_ones", [P, P])
        ones_col = sb("ones_col", [P, 1])
        c_act = sb("c_act", [P, KD])
        rstd = sb("rstd", [P, BLK])
        rms = sb("rms", [P, BLK])
        eps = sb("eps", [P, 1])
        ssum = sb("ssum", [P, BLK])
        scale_a = sb("scale_a", [P, KD])
        banks = ps("banks", [P, 8, BLK])

        mod_w = shared[:, :].rearrange("p (s k n) -> p s k n", s=2, k=KD)
        squares = shared[:, :].rearrange("p (k n) -> p k n", k=KD)
        w_raw = shared[:, 0:2 * KD * P].rearrange("p (s n) -> p s n", s=2)
        x_kt = x_blk[:, :, :].rearrange("p s (k n) -> p s k n", k=KD)
        stage = x_blk[:, :, 0:SEQ]
        mod_ps = banks[:, 7, 0:6 * KD]
        norm_ps = banks[:, 0, :]
        flat = lambda t: t.rearrange("p k n -> p (k n)")

        params_in, c_ready, ones_ready = sem("params_in"), sem("c_ready"), sem("ones_ready")
        modw_in, modacc_ready, partial, mod_done, mod_ready = two("modw_in"), sem("modacc_ready"), sem("partial"), sem("mod_done"), sem("mod_ready")
        x_in, sq_ready, ssum_ready, norm_sum, rms_ready, rstd_ready = two("x_in"), sem("sq_ready"), sem("ssum_ready"), sem("norm_sum"), sem("rms_ready"), sem("rstd_ready")
        xn_ready, h_hi_ready, h_full, h_ready = sem("xn_ready"), sem("h_hi_ready"), sem("h_full"), sem("h_ready")
        w_in_sem, hi_ready, lo_ready = two("w_in_sem"), sem("hi_ready"), sem("lo_ready")
        tile_done, staged, stored = sem("tile_done"), sem("staged"), two("stored")

        with nc.Block() as block:
            @block.sync
            def _(sp):
                sp.dma_start(vec[:], vec_in).then_inc(params_in, 16)
                sp.dma_start(mean_ones[:], consts[:, C_MEAN * P:(C_MEAN + 1) * P]).then_inc(params_in, 16)
                for n in range(2):
                    sp.dma_start(mod_w[:, n], w_mod[n]).then_inc(modw_in[n], 16)
                with sp.Fori(1, MOD_CHUNKS // 2) as i:
                    for s in range(2):
                        sp.wait_ge(modacc_ready, 2 * i + (s - 1))
                        sp.dma_start(mod_w[:, s], w_mod[bass.ds(2 * i + s, 1)].rearrange("o p k n -> (o p) k n")).then_inc(modw_in[s], 16)
                sp.wait_ge(ssum_ready, NBLK)
                for n in range(2):
                    sp.dma_start(w_raw[:, n], w_in[n]).then_inc(w_in_sem[n], 16)
                with sp.Fori(1, N_PROJ // 2) as i:
                    for s in range(2):
                        sp.wait_ge(lo_ready, 2 * i + (s - 1))
                        sp.dma_start(w_raw[:, s], w_in[bass.ds(2 * i + s, 1)].rearrange("o p n -> (o p) n")).then_inc(w_in_sem[s], 16)

            @block.gpsimd
            def _(pool):
                nc.gpsimd.memset(eps[:], EPS).then_inc(ones_ready, 1)
                nc.gpsimd.memset(ones_col[:], 1.0).then_inc(ones_ready, 1)
                for n in range(NBLK):
                    if n >= 2:
                        pool.wait_ge(h_ready, n - 1)
                    pool.dma_start(x_kt[:, n % 2], xT[:, :, n * BLK:(n + 1) * BLK]).then_inc(x_in[n % 2], 16)
                with pool.Fori(0, N_PROJ // 2) as i:
                    for s in range(2):
                        pool.wait_ge(hi_ready, 2 * i + (s + 1))
                        nc.gpsimd.tensor_tensor(flat(w_lo[:, s]), w_raw[:, s], flat(w_hi[:, s]).bitcast(F32), ALU.subtract).then_inc(lo_ready, 1)

            @block.scalar
            def _(act):
                act.wait_ge(params_in, 32)
                act.wait_ge(ones_ready, 2)
                nc.scalar.activation(c_act[:], vec[:, VEC["c"]:VEC["c"] + KD], ACT.Silu).then_inc(c_ready, 1)
                act.wait_ge(mod_ready, 1)
                for n in range(NBLK):
                    act.wait_ge(x_in[n % 2], 16 * (n // 2 + 1))
                    if n >= 1:
                        act.wait_ge(ssum_ready, n)
                    nc.scalar.activation(squares, x_kt[:, n % 2], ACT.Square).then_inc(sq_ready, 1)
                    act.wait_ge(norm_sum, n + 1)
                    if n >= 1:
                        act.wait_ge(rstd_ready, n)
                    nc.scalar.activation(rms[:], norm_ps, ACT.Sqrt, bias=eps[:]).then_inc(rms_ready, 1)
                    act.wait_ge(xn_ready, n + 1)
                    for k in range(KD):
                        last = nc.scalar.activation(h_hi[:, k, n * BLK:(n + 1) * BLK], x_kt[:, n % 2, k], ACT.Identity,
                                                    bias=mod[:, SHIFT1 + k:SHIFT1 + k + 1], scale=scale_a[:, k:k + 1])
                    last.then_inc(h_hi_ready, 1)

                for s in range(2):
                    act.sem_inc(stored[s], 16)
                for n in range(2):
                    act.wait_ge(w_in_sem[n], 16)
                    nc.scalar.activation(flat(w_hi[:, n]), w_raw[:, n], ACT.Copy).then_inc(hi_ready, 1)
                with act.Fori(1, N_PROJ // 2) as i:
                    for s in range(2):
                        act.wait_ge(w_in_sem[s], 16 * i + 16)
                        act.wait_ge(tile_done, 2 * i + (s - 1))
                        nc.scalar.activation(flat(w_hi[:, s]), w_raw[:, s], ACT.Copy).then_inc(hi_ready, 1)
                        act.wait_ge(staged, 2 * i + (s + 1))
                        act.dma_start(proj[bass.ds(2 * i + (s - 2), 1)].rearrange("o p n -> (o p) n"), stage[:, s]).then_inc(stored[s], 16)
                for n in (N_PROJ - 2, N_PROJ - 1):
                    act.wait_ge(staged, n + 3)
                    act.dma_start(proj[n], stage[:, n % 2]).then_inc(stored[n % 2], 16)
                for s in range(2):
                    act.wait_ge(stored[s], 16 + 8 * N_PROJ)

            @block.vector
            def _(dve):
                dve.wait_ge(c_ready, 1)
                with dve.Fori(0, MOD_CHUNKS // 2) as i:
                    for s in range(2):
                        dve.wait_ge(modw_in[s], 16 * i + 16)
                        dve.wait_ge(mod_done, 2 * i + (s + 1))
                        nc.vector.tensor_scalar(mod_acc[:, s], mod_w[:, s, 0], c_act[:, 0:1], None, ALU.mult).then_inc(partial, 1)
                        for k in range(1, KD):
                            dve.wait_ge(partial, 2 * (KD - 1) * i + ((KD - 1) * s + k))
                            nc.vector.scalar_tensor_tensor(out=mod_acc[:, s], in0=mod_w[:, s, k], scalar=c_act[:, k:k + 1], in1=mod_acc[:, s],
                                                           op0=ALU.mult, op1=ALU.add).then_inc(partial if k < KD - 1 else modacc_ready, 1)
                dve.wait_ge(mod_done, MOD_CHUNKS + 2)
                nc.vector.tensor_tensor(mod[:], mod_ps, vec[:, VEC["b_mod"]:VEC["b_mod"] + 6 * KD], ALU.add).then_inc(partial, 1)
                dve.wait_ge(partial, (KD - 1) * MOD_CHUNKS + 1)
                nc.vector.scalar_tensor_tensor(out=scale_a[:], in0=mod[:, SCALE1:SCALE1 + KD], scalar=1.0, in1=vec[:, VEC["g1"]:VEC["g1"] + KD],
                                               op0=ALU.add, op1=ALU.mult).then_inc(mod_ready, 1)
                dve.wait_ge(mod_ready, 1)
                for n in range(NBLK):
                    xb, cols = x_kt[:, n % 2], slice(n * BLK, (n + 1) * BLK)
                    dve.wait_ge(sq_ready, n + 1)
                    nc.vector.tensor_reduce(ssum[:], squares.rearrange("p k n -> p n k"), AX.X, ALU.add).then_inc(ssum_ready, 1)
                    dve.wait_ge(rms_ready, n + 1)
                    nc.vector.reciprocal(rstd[:], rms[:]).then_inc(rstd_ready, 1)
                    dve.wait_ge(rstd_ready, n + 1)
                    nc.vector.tensor_tensor(xb, xb, rstd[:, None, :].to_broadcast([P, KD, BLK]), ALU.mult).then_inc(xn_ready, 1)
                    dve.wait_ge(h_hi_ready, n + 1)
                    for k in range(KD):
                        last = nc.vector.tensor_scalar(xb[:, k], xb[:, k], scale_a[:, k:k + 1], mod[:, SHIFT1 + k:SHIFT1 + k + 1], ALU.mult, ALU.add)
                    last.then_inc(h_full, 1)
                    dve.wait_ge(h_full, n + 1)
                    nc.vector.tensor_tensor(h_lo[:, :, cols], xb, h_hi[:, :, cols].bitcast(F32), ALU.subtract).then_inc(h_ready, 1)

                dve.wait_ge(h_ready, NBLK)
                with dve.Fori(0, N_PROJ // 2) as i:
                    for s in range(2):
                        dve.wait_ge(tile_done, 2 * i + (s + 1))
                        dve.wait_ge(stored[s], 16 * i + 16)
                        nc.vector.tensor_copy(stage[:, s], banks[:, 4 * s:4 * s + 4].rearrange("p b n -> p (b n)")).then_inc(staged, 1)

            @block.tensor
            def _(pe):
                pe.sem_inc(mod_done, 2)
                pe.wait_ge(ones_ready, 2)
                pe.wait_ge(params_in, 32)
                with pe.Fori(0, MOD_CHUNKS // 2) as i:
                    for s in range(2):
                        pe.wait_ge(modacc_ready, 2 * i + (s + 1))
                        for j in range(MOD_COLS // P):
                            last = nc.tensor.matmul(mod_ps[:, bass.ds(4 * i + (2 * s + j), 1)], mod_acc[:, s, j * P:(j + 1) * P], ones_col[:], start=True, stop=True)
                        last.then_inc(mod_done, 1)
                for n in range(NBLK):
                    pe.wait_ge(ssum_ready, n + 1)
                    if n >= 1:
                        pe.wait_ge(rms_ready, n)
                    nc.tensor.matmul(norm_ps, mean_ones[:], ssum[:], start=True, stop=True).then_inc(norm_sum, 1)
                pe.wait_ge(h_ready, NBLK)
                pe.wait_ge(rms_ready, NBLK)
                pe.sem_inc(staged, 2)
                with pe.Fori(0, N_PROJ // 2) as i:
                    for s in range(2):
                        pe.wait_ge(lo_ready, 2 * i + (s + 1))
                        pe.wait_ge(staged, 2 * i + (s + 1))
                        for k in range(KD):
                            for b in range(NBLK):
                                cols = slice(b * BLK, (b + 1) * BLK)
                                last = split_products(nc, banks[:, 4 * s + b], w_hi[:, s, k], w_lo[:, s, k], h_hi[:, k, cols], h_lo[:, k, cols],
                                                      k == 0, k == KD - 1)
                        last.then_inc(tile_done, 1)


def recurrent_branch(nc, vec, w_gates, proj, mix):
    with ExitStack() as ctx:
        sb = lambda n, s, d=F32: ctx.enter_context(nc.sbuf_tensor(n, s, d))
        ps = lambda n, s, d=F32: ctx.enter_context(nc.psum_tensor(n, s, d))
        sem = lambda n: ctx.enter_context(nc.semaphore(n))
        PAD = CONV_WIDTH - 1
        xa = sb("lru_xa", [P, LRU_T, PAD + SEQ])
        ya = sb("lru_ya", [P, LRU_T, SEQ])
        gates = sb("lru_gates", [P, 2, LRU_T, P])
        conv = sb("lru_conv", [P, SEQ])
        r_gate, i_gate = sb("lru_r", [P, SEQ]), sb("lru_i", [P, SEQ])
        decay, tanh_y, inv = sb("lru_decay", [P, SEQ]), sb("lru_tanh", [P, SEQ]), sb("lru_inv", [P, SEQ])
        u_in, state, gelu_y = sb("lru_u", [P, SEQ]), sb("lru_state", [P, SEQ]), sb("lru_gelu", [P, SEQ])
        out = sb("lru_out", [P, LRU_T, SEQ])
        sp_abs, sp_exp, sp_one, sp_ln, sp_rec, sp_err = (sb("lru_sp%d" % i, [P, LRU_T]) for i in range(6))
        rate, neg_rate = sb("lru_rate", [P, LRU_T]), sb("lru_neg_rate", [P, LRU_T])
        gate_ps = ps("lru_gate_ps", [P, 2, SEQ])
        loaded, pool_done, link, sp_act, rate_ready = sem("lru_loaded"), sem("lru_pool_done"), sem("lru_link"), sem("lru_sp_act"), sem("lru_rate_ready")
        conv_ready, gates_done, act_done, out_ready, stored = sem("lru_conv_ready"), sem("lru_gates_done"), sem("lru_act_done"), sem("lru_out_ready"), sem("lru_stored")
        lam = vec[:, VEC["lam"]:VEC["lam"] + LRU_T]
        wcol = lambda name, i: vec[:, VEC[name] + i:VEC[name] + i + 1]
        FIRST, EACH = 5, PAD - 1 + 6

        with nc.Block() as block:
            @block.sync
            def _(sp):
                sp.dma_start(xa[:, :, PAD:], proj[T_XA:T_XA + LRU_T].rearrange("t p n -> p t n")).then_inc(loaded, 16)
                sp.dma_start(ya[:], proj[T_YA:T_YA + LRU_T].rearrange("t p n -> p t n")).then_inc(loaded, 16)
                sp.dma_start(gates[:], w_gates.rearrange("g t p n -> p g t n")).then_inc(loaded, 16)
                for t in range(LRU_T):
                    sp.wait_ge(out_ready, t + 1)
                    sp.dma_start(mix[t], out[:, t]).then_inc(stored, 16)
                sp.wait_ge(stored, 16 * LRU_T)

            @block.gpsimd
            def _(pool):
                nc.gpsimd.memset(xa[:, :, 0:PAD], 0.0).then_inc(pool_done, 1)
                for t in range(LRU_T):
                    pool.wait_ge(act_done, 5 * t + 2)
                    if t >= 1:
                        pool.wait_ge(link, FIRST + EACH * t)
                    nc.gpsimd.tensor_tensor(u_in[:], i_gate[:], conv[:], ALU.mult).then_inc(pool_done, 1)

            @block.scalar
            def _(act):
                nc.scalar.activation(sp_abs[:], lam, ACT.Abs).then_inc(sp_act, 1)
                act.wait_ge(sp_act, 1)
                nc.scalar.activation(sp_exp[:], sp_abs[:], ACT.Exp, scale=-1.0).then_inc(sp_act, 1)
                act.wait_ge(link, 1)
                nc.scalar.activation(sp_ln[:], sp_one[:], ACT.Ln).then_inc(sp_act, 1)
                for t in range(LRU_T):
                    act.wait_ge(gates_done, t + 1)
                    if t >= 1:
                        act.wait_ge(out_ready, t)
                    nc.scalar.activation(r_gate[:], gate_ps[:, 0], ACT.Sigmoid, bias=wcol("b_r", t)).then_inc(act_done, 1)
                    nc.scalar.activation(i_gate[:], gate_ps[:, 1], ACT.Sigmoid, bias=wcol("b_i", t)).then_inc(act_done, 1)
                    act.wait_ge(act_done, 5 * t + 2)
                    act.wait_ge(rate_ready, 1)
                    nc.scalar.activation(tanh_y[:], r_gate[:], ACT.Tanh, scale=rate[:, t:t + 1]).then_inc(act_done, 1)
                    nc.scalar.activation(decay[:], r_gate[:], ACT.Exp, scale=neg_rate[:, t:t + 1]).then_inc(act_done, 1)
                    nc.scalar.activation(gelu_y[:], ya[:, t], ACT.Gelu_apprx_tanh).then_inc(act_done, 1)
                    act.wait_ge(link, FIRST + EACH * t + PAD + 3)
                    nc.scalar.activation(inv[:], inv[:], ACT.Sqrt).then_inc(sp_act, 1)

            @block.vector
            def _(dve):
                dve.wait_ge(sp_act, 2)
                nc.vector.tensor_scalar(sp_one[:], sp_exp[:], 1.0, None, ALU.add).then_inc(link, 1)
                dve.wait_ge(link, 1)
                nc.vector.reciprocal(sp_rec[:], sp_one[:])
                nc.vector.scalar_tensor_tensor(out=sp_err[:], in0=sp_one[:], scalar=-1.0, in1=sp_exp[:], op0=ALU.add, op1=ALU.subtract).then_inc(link, 1)
                dve.wait_ge(link, 2)
                nc.vector.tensor_tensor(sp_err[:], sp_err[:], sp_rec[:], ALU.mult).then_inc(link, 1)
                dve.wait_ge(link, 3)
                dve.wait_ge(sp_act, 3)
                nc.vector.tensor_tensor(sp_ln[:], sp_ln[:], sp_err[:], ALU.subtract).then_inc(link, 1)
                nc.vector.tensor_scalar(sp_abs[:], lam, 0.0, None, ALU.min)
                dve.wait_ge(link, 4)
                nc.vector.tensor_scalar(sp_ln[:], sp_ln[:], LRU_C, None, ALU.mult).then_inc(link, 1)
                dve.wait_ge(link, 5)
                nc.vector.scalar_tensor_tensor(out=rate[:], in0=sp_abs[:], scalar=-LRU_C, in1=sp_ln[:], op0=ALU.mult, op1=ALU.add).then_inc(rate_ready, 1)
                dve.wait_ge(rate_ready, 1)
                nc.vector.tensor_scalar(neg_rate[:], rate[:], -1.0, None, ALU.mult).then_inc(rate_ready, 1)
                at = FIRST
                dve.wait_ge(loaded, 48)
                dve.wait_ge(pool_done, 1)
                for t in range(LRU_T):
                    tap = lambda j: xa[:, t, j:j + SEQ]
                    if t >= 1:
                        dve.wait_ge(pool_done, t + 1)
                        dve.wait_ge(gates_done, t)
                    nc.vector.tensor_scalar(conv[:], tap(PAD), wcol("conv_w", PAD * LRU_T + t), wcol("conv_b", t), ALU.mult, ALU.add).then_inc(link, 1)
                    at += 1
                    for j in range(PAD):
                        dve.wait_ge(link, at)
                        nc.vector.scalar_tensor_tensor(out=conv[:], in0=tap(j), scalar=wcol("conv_w", j * LRU_T + t), in1=conv[:],
                                                       op0=ALU.mult, op1=ALU.add).then_inc(link if j < PAD - 1 else conv_ready, 1)
                        at += j < PAD - 1
                    dve.wait_ge(act_done, 5 * t + 3)
                    nc.vector.tensor_scalar(inv[:], tanh_y[:], 1.0, None, ALU.add).then_inc(link, 1)
                    at += 1
                    dve.wait_ge(link, at)
                    nc.vector.reciprocal(inv[:], inv[:]).then_inc(link, 1)
                    at += 1
                    dve.wait_ge(link, at)
                    nc.vector.scalar_tensor_tensor(out=inv[:], in0=tanh_y[:], scalar=2.0, in1=inv[:], op0=ALU.mult, op1=ALU.mult).then_inc(link, 1)
                    at += 1
                    dve.wait_ge(pool_done, t + 2)
                    dve.wait_ge(sp_act, 4 + t)
                    nc.vector.tensor_tensor(u_in[:], u_in[:], inv[:], ALU.mult).then_inc(link, 1)
                    at += 1
                    dve.wait_ge(link, at)
                    dve.wait_ge(act_done, 5 * t + 5)
                    nc.vector.tensor_tensor_scan(state[:], decay[:], u_in[:], 0.0, ALU.mult, ALU.add).then_inc(link, 1)
                    at += 1
                    dve.wait_ge(link, at)
                    nc.vector.tensor_tensor(out[:, t], state[:], gelu_y[:], ALU.mult).then_inc(out_ready, 1)

            @block.tensor
            def _(pe):
                pe.wait_ge(loaded, 48)
                for t in range(LRU_T):
                    pe.wait_ge(conv_ready, t + 1)
                    if t >= 1:
                        pe.wait_ge(act_done, 5 * t - 3)
                    for g in range(2):
                        for b in range(NBLK):
                            last = nc.tensor.matmul(gate_ps[:, g, b * BLK:(b + 1) * BLK], gates[:, g, t], conv[:, b * BLK:(b + 1) * BLK], start=True, stop=True)
                    last.then_inc(gates_done, 1)


def fox_operands(nc, vec, consts, fox_rows, proj, q_split, k_split, bias_split, v_nat):
    HEADS2 = 2 * FOX_HEADS
    TILES = 2 * FOX_T
    with ExitStack() as ctx:
        sb = lambda n, s, d=F32: ctx.enter_context(nc.sbuf_tensor(n, s, d))
        ps = lambda n, s, d=F32: ctx.enter_context(nc.psum_tensor(n, s, d))
        sem = lambda n: ctx.enter_context(nc.semaphore(n))
        qk = sb("fp_qk", [P, TILES, SEQ])
        v_raw = sb("fp_v", [P, FOX_T, SEQ])
        squares = sb("fp_squares", [P, SEQ])
        hi = sb("fp_hi", [P, SEQ], F32R)
        lo = sb("fp_lo", [P, SEQ], F32R)
        ident = sb("fp_ident", [P, P])
        rows_sel = sb("fp_rows_sel", [P, TILES, HEADS2])
        back_sel = sb("fp_back_sel", [HEADS2, TILES, P])
        rows = [sb("fp_rows%d" % i, [FF_ROW + FOX_HEADS, SEQ]) for i in range(5)]
        mean, rstd, newton = (r[0:HEADS2] for r in rows[:3])
        logit, e_neg, log1p, err, recip = (r[FF_ROW:FF_ROW + FOX_HEADS] for r in rows)
        bias_hi, bias_lo = (t[FF_ROW:FF_ROW + FOX_HEADS] for t in (hi, lo))
        ones_col = sb("fp_ones_col", [FF_ROW + FOX_HEADS, 1])
        ones_row = ones_col[FF_ROW:FF_ROW + FOX_HEADS].to_broadcast([FOX_HEADS, SEQ])
        gains = sb("fp_gains", [P, 2])
        banks = ps("fp_banks", [P, 8, BLK])
        loaded, v_loaded, squared, summed, mean_out = sem("fp_loaded"), sem("fp_v_loaded"), sem("fp_squared"), sem("fp_summed"), sem("fp_mean_out")
        ln_done, rstd_done, spread, normed, hi_done, lo_done = sem("fp_ln_done"), sem("fp_rstd_done"), sem("fp_spread"), sem("fp_normed"), sem("fp_hi_done"), sem("fp_lo_done")
        hi_out, lo_out, v_t, v_hi_done, v_lo_done = sem("fp_hi_out"), sem("fp_lo_out"), sem("fp_v_t"), sem("fp_v_hi_done"), sem("fp_v_lo_done")
        f_act, f_link, f_hi, f_out, chain, consts_in = sem("fp_f_act"), sem("fp_f_link"), sem("fp_f_hi"), sem("fp_f_out"), sem("fp_chain"), sem("fp_consts_in")
        v4 = v_nat[:, :, :, :].rearrange("p h t (w d) -> p h t w d", w=2)
        with nc.Block() as block:
            @block.sync
            def _(sp):
                sp.dma_start(ident[:], consts[:, C_IDENT * P:(C_IDENT + 1) * P]).then_inc(consts_in, 16)
                sp.dma_start(rows_sel[:], fox_rows[:, 0:TILES * HEADS2].rearrange("p (t h) -> p t h", t=TILES)).then_inc(consts_in, 16)
                sp.dma_start(back_sel[:], fox_rows[0:HEADS2, TILES * HEADS2:].rearrange("h (t p) -> h t p", t=TILES)).then_inc(consts_in, 16)
                sp.dma_start(qk[:], proj[T_FQ:T_FQ + TILES].rearrange("t p n -> p t n")).then_inc(loaded, 16)
                sp.dma_start(v_raw[:], proj[T_FV:T_FV + FOX_T].rearrange("t p n -> p t n")).then_inc(v_loaded, 16)
                for t in range(TILES):
                    split, j = (q_split, k_split)[t // FOX_T], t % FOX_T
                    sp.wait_ge(hi_done, t + 1)
                    for h in range(2):
                        sp.dma_start(split[2 * j + h, 0], hi[HEAD_DIM * h:HEAD_DIM * (h + 1)].bitcast(F32)).then_inc(hi_out, 16)
                    sp.wait_ge(lo_done, t + 1)
                    for h in range(2):
                        sp.dma_start(split[2 * j + h, 1], lo[HEAD_DIM * h:HEAD_DIM * (h + 1)].bitcast(F32)).then_inc(lo_out, 16)
                sp.wait_ge(hi_out, 32 * TILES)
                sp.wait_ge(lo_out, 32 * TILES)

            @block.gpsimd
            def _(pool):
                pool.dma_start(logit, proj[T_MISC, FF_ROW:FF_ROW + FOX_HEADS]).then_inc(f_out, 16)
                nc.gpsimd.memset(ones_col[:], 1.0).then_inc(f_act, 1)
                pool.wait_ge(f_hi, 2)
                pool.dma_start(bias_split[:, 0], bias_hi.bitcast(F32)).then_inc(f_out, 16)
                pool.dma_start(bias_split[:, 1], bias_lo.bitcast(F32)).then_inc(f_out, 16)
                pool.wait_ge(f_out, 48)
                for t in range(TILES):
                    pool.wait_ge(hi_done, t + 1)
                    if t >= 1:
                        pool.wait_ge(lo_out, 32 * t)
                    nc.gpsimd.tensor_tensor(lo[:], qk[:, t], hi[:].bitcast(F32), ALU.subtract).then_inc(lo_done, 1)

            @block.scalar
            def _(act):
                act.wait_ge(loaded, 16)
                for t in range(TILES):
                    if t >= 1:
                        act.wait_ge(summed, t)
                    nc.scalar.activation(squares[:], qk[:, t], ACT.Square).then_inc(squared, 1)
                act.wait_ge(mean_out, 1)
                nc.scalar.activation(rstd, mean, ACT.Ln).then_inc(ln_done, 1)
                act.wait_ge(ln_done, 1)
                nc.scalar.activation(rstd, rstd, ACT.Exp, scale=-0.5).then_inc(ln_done, 1)
                act.wait_ge(f_link, 1)
                nc.scalar.activation(e_neg, logit, ACT.Abs).then_inc(ln_done, 1)
                act.wait_ge(ln_done, 3)
                nc.scalar.activation(e_neg, e_neg, ACT.Exp, scale=-1.0).then_inc(ln_done, 1)
                act.wait_ge(f_link, 2)
                nc.scalar.activation(log1p, err, ACT.Ln).then_inc(ln_done, 1)
                act.wait_ge(f_out, 48)
                for t in range(TILES):
                    act.wait_ge(normed, t + 1)
                    if t >= 1:
                        act.wait_ge(lo_done, t)
                        act.wait_ge(hi_out, 32 * t)
                    nc.scalar.activation(hi[:], qk[:, t], ACT.Copy).then_inc(hi_done, 1)
                for n in range(4 * FOX_T):
                    j, g = n // 4, n % 4
                    act.wait_ge(v_t, n + 1)
                    nc.scalar.activation(v4[:, 2 * j:2 * j + 2, 4 * g:4 * g + 4, 0].rearrange("p h t d -> p t h d"),
                                         banks[:, 4 + n % 4].rearrange("p (t h d) -> p t h d", t=4, h=2), ACT.Copy).then_inc(v_hi_done, 1)

            @block.vector
            def _(dve):
                nc.vector.tensor_scalar(gains[:, 0:1], vec[:, VEC["q_gain"]:VEC["q_gain"] + 1], HEAD_DIM ** -0.5, None, ALU.mult)
                nc.vector.tensor_copy(gains[:, 1:2], vec[:, VEC["k_gain"]:VEC["k_gain"] + 1])
                dve.wait_ge(f_out, 16)
                nc.vector.tensor_scalar(logit, logit, vec[FF_ROW:FF_ROW + FOX_HEADS, VEC["b_f"]:VEC["b_f"] + 1], None, ALU.add).then_inc(f_link, 1)
                dve.wait_ge(summed, TILES)
                nc.vector.tensor_scalar(mean, banks[0:HEADS2, 0:4].rearrange("p b n -> p (b n)"), EPS, None, ALU.add).then_inc(mean_out, 1)
                dve.wait_ge(ln_done, 2)
                nc.vector.tensor_tensor(newton, rstd, rstd, ALU.mult).then_inc(chain, 1)
                dve.wait_ge(chain, 1)
                nc.vector.tensor_tensor(newton, newton, mean, ALU.mult).then_inc(chain, 1)
                dve.wait_ge(chain, 2)
                nc.vector.tensor_scalar(newton, newton, -0.5, 1.5, ALU.mult, ALU.add).then_inc(chain, 1)
                dve.wait_ge(chain, 3)
                nc.vector.tensor_tensor(rstd, rstd, newton, ALU.mult).then_inc(rstd_done, 1)
                dve.wait_ge(ln_done, 4)
                nc.vector.tensor_scalar(err, e_neg, 1.0, None, ALU.add).then_inc(f_link, 1)
                dve.wait_ge(ln_done, 5)
                nc.vector.reciprocal(recip, err).then_inc(f_link, 1)
                nc.vector.scalar_tensor_tensor(out=err, in0=err, scalar=-1.0, in1=e_neg, op0=ALU.add, op1=ALU.subtract).then_inc(f_link, 1)
                dve.wait_ge(f_link, 4)
                nc.vector.tensor_tensor(err, err, recip, ALU.mult).then_inc(f_link, 1)
                dve.wait_ge(f_link, 5)
                nc.vector.tensor_scalar(recip, logit, 0.0, None, ALU.min).then_inc(f_link, 1)
                nc.vector.tensor_tensor(log1p, log1p, err, ALU.subtract).then_inc(f_link, 1)
                dve.wait_ge(f_link, 7)
                nc.vector.tensor_tensor(err, log1p, recip, ALU.subtract).then_inc(f_link, 1)
                dve.wait_ge(f_link, 8)
                dve.wait_ge(f_act, 1)
                nc.vector.tensor_tensor_scan(log1p, ones_row, err, 0.0, ALU.mult, ALU.add).then_inc(f_link, 1)
                dve.wait_ge(f_link, 9)
                nc.vector.tensor_copy(bias_hi, log1p).then_inc(f_hi, 1)
                dve.wait_ge(f_hi, 1)
                nc.vector.tensor_tensor(bias_lo, log1p, bias_hi.bitcast(F32), ALU.subtract).then_inc(f_hi, 1)
                for t in range(TILES):
                    dve.wait_ge(spread, t + 1)
                    nc.vector.scalar_tensor_tensor(out=qk[:, t], in0=qk[:, t], scalar=gains[:, t // FOX_T:t // FOX_T + 1],
                                                   in1=banks[:, 0:4].rearrange("p b n -> p (b n)"), op0=ALU.mult, op1=ALU.mult).then_inc(normed, 1)
                for n in range(4 * FOX_T):
                    j, g = n // 4, n % 4
                    dve.wait_ge(v_hi_done, n + 1)
                    for h in range(2):
                        last = nc.vector.tensor_tensor(v4[:, 2 * j + h, 4 * g:4 * g + 4, 1],
                                                       banks[:, 4 + n % 4].rearrange("p (t h d) -> p t h d", t=4, h=2)[:, :, h],
                                                       v4[:, 2 * j + h, 4 * g:4 * g + 4, 0].bitcast(F32), ALU.subtract)
                    last.then_inc(v_lo_done, 1)

            @block.tensor
            def _(pe):
                pe.wait_ge(consts_in, 48)
                for t in range(TILES):
                    pe.wait_ge(squared, t + 1)
                    for b in range(NBLK):
                        last = nc.tensor.matmul(banks[0:HEADS2, b], rows_sel[:, t], squares[:, b * BLK:(b + 1) * BLK], start=(t == 0), stop=(t == TILES - 1))
                    last.then_inc(summed, 1)
                pe.wait_ge(v_loaded, 16)

                def transpose_v(n):
                    for t in range(4):
                        o = (4 * (n % 4) + t) * P
                        last = nc.tensor.transpose(banks[:, 4 + n % 4, t * P:(t + 1) * P], v_raw[:, n // 4, o:o + P], ident[:])
                    last.then_inc(v_t, 1)

                for n in range(4):
                    transpose_v(n)
                pe.wait_ge(rstd_done, 1)
                for t in range(TILES):
                    if t >= 1:
                        pe.wait_ge(normed, t)
                    for b in range(NBLK):
                        last = nc.tensor.matmul(banks[:, b], back_sel[:, t], rstd[:, b * BLK:(b + 1) * BLK], start=True, stop=True)
                    last.then_inc(spread, 1)
                for n in range(4, 4 * FOX_T):
                    pe.wait_ge(v_lo_done, n - 3)
                    transpose_v(n)


def forgetting_attention(nc, consts, q_split, k_split, bias_split, v_nat, mix):
    NQ = SEQ // P
    CH = [(i, c, min(4, i + 1 - 4 * c)) for i in range(NQ) for c in range(i // 4 + 1)]
    NCH = len(CH)
    first = {i: min(m for m, x in enumerate(CH) if x[0] == i) for i in range(NQ)}
    last_of = {i: max(m for m, x in enumerate(CH) if x[0] == i) for i in range(NQ)}

    def ahead(m, by):
        i, c, _ = CH[m]
        if i + by >= NQ:
            return []
        mine = list(range(first[i + by], last_of[i + by] + 1))
        return mine[c:] if m == last_of[i] else mine[c:c + 1]

    mix_heads = mix[LRU_T:LRU_T + FOX_T].rearrange("t (w d) n -> (t w) d n", w=2)
    with ExitStack() as ctx:
        sb = lambda n, s, d=F32: ctx.enter_context(nc.sbuf_tensor(n, s, d))
        ps = lambda n, s, d=F32: ctx.enter_context(nc.psum_tensor(n, s, d))
        sem = lambda n: ctx.enter_context(nc.semaphore(n))
        QS = 4
        k_a = sb("fa_k_a", [P, FOX_HEADS, SEQ], F32R)
        k_b = sb("fa_k_b", [HEAD_DIM + 2, FOX_HEADS, SEQ], F32R)
        q_a = sb("fa_q_a", [P, QS, P], F32R)
        q_b = sb("fa_q_b", [HEAD_DIM + 2, QS, P], F32R)
        ident = sb("fa_ident", [P, P])
        ident_r = sb("fa_ident_r", [P, P], F32R)
        causal_r = sb("fa_causal_r", [P, P], F32R)
        scores = sb("fa_scores", [P, 2, SEQ])
        probs = sb("fa_probs", [P, 2, SEQ])
        p_hi = sb("fa_p_hi", [P, 2, BLK], F32R)
        p_lo = sb("fa_p_lo", [P, 2, BLK], F32R)
        ch_max = sb("fa_ch_max", [P, 2, 4])
        neg_max = sb("fa_neg_max", [P, 2])
        ch_sum = sb("fa_ch_sum", [P, 4, 4])
        row_sum, inv_sum = sb("fa_row_sum", [P, 1]), sb("fa_inv_sum", [P, 1])
        part = sb("fa_part", [P, HEAD_DIM])
        o_nat = sb("fa_o_nat", [P, 4, P])
        o_t = sb("fa_o_t", [HEAD_DIM, 2, BLK])
        s_ps = ps("fa_s_ps", [P, 3, BLK])
        t_ps = ps("fa_t_ps", [P, 2, BLK])
        o_ps = ps("fa_o_ps", [P, 2, BLK])
        ot_ps = ps("fa_ot_ps", [P, BLK])

        k_in, const_in, made, filled = sem("fa_k_in"), sem("fa_const_in"), sem("fa_made"), sem("fa_filled")
        q_in = [sem("fa_q_in%d" % s) for s in range(QS)]
        s_done, max_done, neg_done, exp_done = sem("fa_s_done"), sem("fa_max_done"), sem("fa_neg_done"), sem("fa_exp_done")
        t_done, hi_done, lo_done, pv_done = sem("fa_t_done"), sem("fa_hi_done"), sem("fa_lo_done"), sem("fa_pv_done")
        fin_link, fin_done, ot_done, ot_copied = sem("fa_fin_link"), sem("fa_fin_done"), sem("fa_ot_done"), sem("fa_ot_copied")
        stored = [sem("fa_stored0"), sem("fa_stored1")]

        with nc.Block() as block:
            @block.sync
            def _(sp):
                sp.dma_start(ident[:], consts[:, C_IDENT * P:(C_IDENT + 1) * P]).then_inc(const_in, 16)
                sp.dma_start(scores[:, 0, 0:P], consts[:, C_CAUSAL * P:(C_CAUSAL + 1) * P]).then_inc(const_in, 16)
                for half in range(2):
                    sp.dma_start(k_a[HEAD_DIM * half:HEAD_DIM * (half + 1)].bitcast(F32), k_split[:, 0].rearrange("h d n -> d h n")).then_inc(k_in, 16)
                sp.dma_start(k_b[0:HEAD_DIM].bitcast(F32), k_split[:, 1].rearrange("h d n -> d h n")).then_inc(k_in, 16)
                for w in range(2):
                    sp.dma_start(k_b[HEAD_DIM + w:HEAD_DIM + w + 1].bitcast(F32), bias_split[:, w].rearrange("(o h) n -> o h n", o=1)).then_inc(k_in, 16)
                with sp.Fori(0, FOX_HEADS) as h:
                    for i in range(NQ):
                        sp.wait_ge(s_done, NCH * h + (last_of[i - QS] + 2 if i >= QS else 1))
                        cols = slice(i * P, (i + 1) * P)
                        sp.dma_start(q_a[:, i % QS].bitcast(F32), q_split[bass.ds(h, 1), :, :, cols].rearrange("o w d n -> (o w d) n")).then_inc(q_in[i % QS], 16)
                        sp.dma_start(q_b[0:HEAD_DIM, i % QS].bitcast(F32), q_split[bass.ds(h, 1), 0, :, cols].rearrange("o d n -> (o d) n")).then_inc(q_in[i % QS], 16)

            @block.gpsimd
            def _(pool):
                nc.gpsimd.memset(o_nat[:], 0.0).then_inc(filled, 1)
                pool.wait_ge(filled, 1)
                nc.gpsimd.memset(q_b[HEAD_DIM:HEAD_DIM + 2].bitcast(F32), 1.0).then_inc(filled, 1)

            @block.scalar
            def _(act):
                for s in range(2):
                    act.sem_inc(stored[s], 16)
                act.sem_inc(exp_done, 1)
                act.sem_inc(ot_copied, 1)
                with act.Fori(0, FOX_HEADS) as h:
                    def exponentials(m):
                        i, c, w = CH[m]
                        if c == 0:
                            act.wait_ge(neg_done, NQ * h + (i + 1))
                            act.wait_ge(t_done, NCH * h + (last_of[i - 2] + 2 if i >= 2 else 1))
                            act.wait_ge(fin_done, NQ * h + (i + 1))
                        cols = slice(c * BLK, c * BLK + w * P)
                        nc.scalar.activation(probs[:, i % 2, cols], scores[:, i % 2, cols], ACT.Exp, bias=neg_max[:, i % 2:i % 2 + 1],
                                             accum_out=ch_sum[:, i % 4, c:c + 1]).then_inc(exp_done, 1)

                    def copy_out(g):
                        act.wait_ge(ot_done, 4 * h + (g + 1))
                        act.wait_ge(stored[g % 2], 32 * h + (16 * (g // 2) + 16))
                        nc.scalar.activation(o_t[:, g % 2], ot_ps[0:HEAD_DIM], ACT.Copy).then_inc(ot_copied, 1)
                        act.wait_ge(ot_copied, 4 * h + (g + 2))
                        act.dma_start(mix_heads[bass.ds(h, 1), :, g * BLK:(g + 1) * BLK].rearrange("o d n -> (o d) n"), o_t[:, g % 2]).then_inc(stored[g % 2], 16)

                    exponentials(0)
                    for m, (i, c, w) in enumerate(CH):
                        for n in ahead(m, 1):
                            exponentials(n)
                        act.wait_ge(t_done, NCH * h + (m + 2))
                        act.wait_ge(pv_done, NCH * h + (m + 1))
                        nc.scalar.activation(p_hi[:, m % 2, 0:w * P], t_ps[:, m % 2, 0:w * P], ACT.Copy).then_inc(hi_done, 1)
                        if m > 0 and m == last_of[i] and i % 4 == 1 and i > 4:
                            copy_out(i // 4 - 1)
                    copy_out(NQ // 4 - 1)
                for s in range(2):
                    act.wait_ge(stored[s], 16 + 16 * (NQ // 8) * FOX_HEADS)

            @block.vector
            def _(dve):
                dve.wait_ge(const_in, 32)
                nc.vector.tensor_copy(ident_r[:], ident[:]).then_inc(made, 1)
                nc.vector.tensor_copy(causal_r[:], scores[:, 0, 0:P]).then_inc(made, 1)
                dve.wait_ge(made, 2)
                dve.wait_ge(filled, 2)
                dve.sem_inc(max_done, 3)
                dve.sem_inc(lo_done, 2)
                dve.sem_inc(fin_done, 4)
                with dve.Fori(0, FOX_HEADS) as h:
                    def maxima(m):
                        i, c, w = CH[m]
                        if c == 0:
                            dve.wait_ge(exp_done, NCH * h + (last_of[i - 2] + 2 if i >= 2 else 1))
                        dve.wait_ge(s_done, NCH * h + (m + 2))
                        nc.vector.tensor_scalar(scores[:, i % 2, c * BLK:c * BLK + w * P], s_ps[:, m % 3, 0:w * P], 1.0, None, ALU.mult, ALU.max,
                                                accum_out=ch_max[:, i % 2, c:c + 1]).then_inc(max_done, 1)
                        if m == last_of[i]:
                            dve.wait_ge(max_done, NCH * h + (m + 4))
                            nc.vector.tensor_reduce(neg_max[:, i % 2:i % 2 + 1], ch_max[:, i % 2, 0:c + 1], AX.X, ALU.max, negate=True).then_inc(neg_done, 1)

                    def finish(i):
                        n = i // 4 + 1
                        dve.wait_ge(pv_done, NCH * h + (last_of[i] + 3))
                        nc.vector.tensor_reduce(row_sum[:], ch_sum[:, i % 4, 0:n], AX.X, ALU.add).then_inc(fin_link, 1)
                        dve.wait_ge(fin_link, 3 * NQ * h + (3 * i + 1))
                        nc.vector.reciprocal(inv_sum[:], row_sum[:]).then_inc(fin_link, 1)
                        dve.wait_ge(fin_link, 3 * NQ * h + (3 * i + 2))
                        nc.vector.tensor_scalar(part[:], o_ps[:, i % 2, 0:HEAD_DIM], inv_sum[:], None, ALU.mult).then_inc(fin_link, 1)
                        dve.wait_ge(fin_link, 3 * NQ * h + (3 * i + 3))
                        nc.vector.scalar_tensor_tensor(out=o_nat[:, i % 4, 0:HEAD_DIM], in0=o_ps[:, i % 2, HEAD_DIM:P], scalar=inv_sum[:], in1=part[:],
                                                       op0=ALU.mult, op1=ALU.add).then_inc(fin_done, 1)
                    for i in range(2):
                        maxima(i)
                    for m, (i, c, w) in enumerate(CH):
                        for n in ahead(m, 2):
                            maxima(n)
                        dve.wait_ge(hi_done, NCH * h + (m + 1))
                        nc.vector.tensor_tensor(p_lo[:, m % 2, 0:w * P], t_ps[:, m % 2, 0:w * P], p_hi[:, m % 2, 0:w * P].bitcast(F32), ALU.subtract).then_inc(lo_done, 1)
                        if i >= 1 and m == first[i]:
                            finish(i - 1)
                    finish(NQ - 1)

            @block.tensor
            def _(pe):
                pe.wait_ge(made, 2)
                pe.wait_ge(filled, 2)
                pe.wait_ge(k_in, 80)
                pe.sem_inc(s_done, 1)
                pe.sem_inc(t_done, 1)
                pe.sem_inc(pv_done, 2)
                with pe.Fori(0, FOX_HEADS) as h:
                    def score(m):
                        i, c, w = CH[m]
                        if c == 0:
                            pe.wait_ge(q_in[i % QS], 128 * h + 32 * (i // QS + 1))
                        pe.wait_ge(max_done, NCH * h + (m + 1))
                        out, cols = s_ps[:, m % 3, 0:w * P], slice(c * BLK, c * BLK + w * P)
                        diagonal = m == last_of[i]
                        nc.tensor.matmul(out, q_a[:, i % QS], k_a[:, bass.ds(h, 1), cols].rearrange("p o n -> p (o n)"), start=True, stop=False)
                        last = nc.tensor.matmul(out, q_b[:, i % QS], k_b[:, bass.ds(h, 1), cols].rearrange("p o n -> p (o n)"), start=False, stop=not diagonal)
                        if diagonal:
                            last = nc.tensor.matmul(s_ps[:, m % 3, (w - 1) * P:w * P], ident_r[:], causal_r[:], start=False, stop=True)
                        last.then_inc(s_done, 1)

                    def times_v(m):
                        i, c, w = CH[m]
                        if c == 0:
                            pe.wait_ge(fin_done, NQ * h + (i + 3))
                        pe.wait_ge(lo_done, NCH * h + (m + 3))
                        for t in range(w):
                            kt = 4 * c + t
                            nc.tensor.matmul(o_ps[:, i % 2, 0:P], p_hi[:, m % 2, t * P:(t + 1) * P], v_nat[:, bass.ds(h, 1), kt].rearrange("p o n -> p (o n)"),
                                             start=(kt == 0), stop=False)
                            last = nc.tensor.matmul(o_ps[:, i % 2, 0:HEAD_DIM], p_lo[:, m % 2, t * P:(t + 1) * P],
                                                    v_nat[:, bass.ds(h, 1), kt, 0:HEAD_DIM].rearrange("p o n -> p (o n)"), start=False, stop=(kt == i))
                        last.then_inc(pv_done, 1)

                    def transpose_out(i):
                        pe.wait_ge(fin_done, NQ * h + (i + 5))
                        if i % 4 == 0:
                            pe.wait_ge(ot_copied, 4 * h + (i // 4 + 1))
                        last = nc.tensor.transpose(ot_ps[:, (i % 4) * P:(i % 4 + 1) * P], o_nat[:, i % 4], ident[:])
                        if i % 4 == 3:
                            last.then_inc(ot_done, 1)
                    for i in range(2):
                        score(i)
                    for m, (i, c, w) in enumerate(CH):
                        for n in ahead(m, 2):
                            score(n)
                        pe.wait_ge(exp_done, NCH * h + (m + 2))
                        pe.wait_ge(lo_done, NCH * h + (m + 1))
                        for t in range(w):
                            o = (4 * c + t) * P
                            last = nc.tensor.transpose(t_ps[:, m % 2, t * P:(t + 1) * P], probs[:, i % 2, o:o + P], ident[:])
                        last.then_inc(t_done, 1)
                        if m >= 1:
                            times_v(m - 1)
                        if i >= 2 and m == first[i]:
                            transpose_out(i - 2)
                    times_v(NCH - 1)
                    transpose_out(NQ - 2)
                    transpose_out(NQ - 1)


def gated_linear_attention(nc, vec, consts, w_alpha, proj, mix):
    NCHUNK = SEQ // GLA_CHUNK
    GRP = 4
    NG = NBLK
    CPG = BLK // GLA_CHUNK
    with ExitStack() as ctx:
        sb = lambda n, s, d=F32: ctx.enter_context(nc.sbuf_tensor(n, s, d))
        ps = lambda n, s, d=F32: ctx.enter_context(nc.psum_tensor(n, s, d))
        sem = lambda n: ctx.enter_context(nc.semaphore(n))
        gq, gk, gv, gg = (sb("ga_" + n, [P, SEQ]) for n in ("gq", "gk", "gv", "gg"))
        glow, w_a, b_a = sb("ga_glow", [GLA_RANK, SEQ]), sb("ga_w_a", [GLA_RANK, P]), sb("ga_b_a", [P, 1])
        ident, head_ones, mask = sb("ga_ident", [P, P]), sb("ga_head_ones", [P, P]), sb("ga_mask", [P, P])
        restart = sb("ga_restart", [P, SEQ])
        z, e_neg, one_e = sb("ga_z", [P, SEQ]), sb("ga_e_neg", [P, SEQ]), sb("ga_one_e", [P, SEQ])
        b_cum = sb("ga_b_cum", [P, SEQ])
        grow = sb("ga_grow", [P, SEQ])
        k_end, q_dec, k_dec = sb("ga_k_end", [P, SEQ]), sb("ga_q_dec", [P, SEQ]), sb("ga_k_dec", [P, SEQ])
        decay = sb("ga_decay", [P, NCHUNK])
        v_n, k_n = sb("ga_v_n", [P, GRP, P]), sb("ga_k_n", [P, GRP, P])
        att = sb("ga_att", [P, 2, GRP, P])
        state = sb("ga_state", [P, NCHUNK + 1, P])
        squares, rstd, o_norm = sb("ga_squares", [P, BLK]), sb("ga_rstd", [P, BLK]), sb("ga_o_norm", [P, BLK])
        out = sb("ga_out", [P, SEQ])
        eps = sb("ga_eps", [P, 1])
        z_ps = ps("ga_z_ps", [P, 4, BLK])
        att_ps, kv_ps = z_ps[:, 0:2], z_ps[:, 2:4]
        turn_ps, o_ps, mean_ps = ps("ga_turn_ps", [P, 2, BLK]), ps("ga_o_ps", [P, BLK]), ps("ga_mean_ps", [P, BLK])
        base, loaded, made, copied, z_done, z_biased = sem("ga_base"), sem("ga_loaded"), sem("ga_made"), sem("ga_copied"), sem("ga_z_done"), sem("ga_z_biased")
        act_step, dve_step, cum_ready, turned, turn_read = sem("ga_act_step"), sem("ga_dve_step"), sem("ga_cum_ready"), sem("ga_turned"), sem("ga_turn_read")
        att_done, att_masked, kv_done, state_done, o_done = sem("ga_att_done"), sem("ga_att_masked"), sem("ga_kv_done"), sem("ga_state_done"), sem("ga_o_done")
        squared, mean_done, norm_act, o_normed, gated, stored = sem("ga_squared"), sem("ga_mean_done"), sem("ga_norm_act"), sem("ga_o_normed"), sem("ga_gated"), sem("ga_stored")
        chunks = lambda t: t.rearrange("p (c n) -> p c n", n=GLA_CHUNK)
        half = lambda h: slice(HEAD_DIM * h, HEAD_DIM * (h + 1))

        with nc.Block() as block:
            @block.sync
            def _(sp):
                sp.dma_start(glow[:], proj[T_MISC, 0:GLA_RANK]).then_inc(base, 16)
                sp.dma_start(ident[:], consts[:, C_IDENT * P:(C_IDENT + 1) * P]).then_inc(base, 16)
                sp.dma_start(head_ones[:], consts[:, C_HEAD * P:(C_HEAD + 1) * P]).then_inc(base, 16)
                sp.dma_start(mask[:], consts[:, C_CHUNK * P:(C_CHUNK + 1) * P]).then_inc(base, 16)
                with sp.Fori(0, GLA_T) as j:
                    sp.wait_ge(stored, 16 * j + 16)
                    sp.dma_start(w_a[:], w_alpha[:, bass.ds(j * P, P)]).then_inc(loaded, 16)
                    for t0, tile in ((T_GK, gk), (T_GQ, gq), (T_GV, gv), (T_GG, gg)):
                        sp.dma_start(tile[:], proj[bass.ds(j + t0, 1)].rearrange("o p n -> (o p) n")).then_inc(loaded, 16)
                    sp.wait_ge(gated, NG * j + NG)
                    sp.dma_start(mix[bass.ds(j + (LRU_T + FOX_T), 1)].rearrange("o p n -> (o p) n"), out[:]).then_inc(stored, 16)
                sp.wait_ge(stored, 16 * GLA_T + 16)

            @block.gpsimd
            def _(pool):
                nc.gpsimd.memset(restart[:], 1.0).then_inc(made, 1)
                pool.wait_ge(made, 1)
                nc.gpsimd.memset(chunks(restart[:])[:, :, 0:1], 0.0).then_inc(made, 1)
                pool.wait_ge(made, 2)
                nc.gpsimd.memset(att[:], 0.0).then_inc(made, 1)
                pool.wait_ge(made, 3)
                nc.gpsimd.memset(state[:], 0.0).then_inc(made, 1)
                pool.wait_ge(made, 4)
                nc.gpsimd.memset(eps[:], EPS).then_inc(made, 1)

            @block.scalar
            def _(act):
                act.wait_ge(made, 5)
                with act.Fori(0, GLA_T) as j:
                    act.wait_ge(loaded, 80 * j + 80)
                    act.wait_ge(stored, 16 * j + 16)
                    nc.scalar.activation(gg[:], gg[:], ACT.Silu).then_inc(act_step, 1)
                    act.wait_ge(z_biased, j + 1)
                    nc.scalar.activation(e_neg[:], z[:], ACT.Abs).then_inc(act_step, 1)
                    act.wait_ge(act_step, 8 * j + 2)
                    nc.scalar.activation(e_neg[:], e_neg[:], ACT.Exp, scale=-1.0).then_inc(act_step, 1)
                    act.wait_ge(dve_step, 8 * j + 1)
                    nc.scalar.activation(grow[:], one_e[:], ACT.Ln).then_inc(act_step, 1)
                    act.wait_ge(dve_step, 8 * j + 5)
                    nc.scalar.activation(z[:], one_e[:], ACT.Exp, scale=1.0 / GLA_TAU).then_inc(act_step, 1)
                    nc.scalar.activation(grow[:], b_cum[:], ACT.Exp, scale=-1.0 / GLA_TAU).then_inc(act_step, 1)
                    nc.scalar.activation(e_neg[:], b_cum[:], ACT.Exp, scale=1.0 / GLA_TAU).then_inc(act_step, 1)
                    nc.scalar.activation(decay[:], chunks(b_cum[:])[:, :, GLA_CHUNK - 1], ACT.Exp, scale=1.0 / GLA_TAU).then_inc(act_step, 1)
                    for g in range(NG):
                        act.wait_ge(turned, NG * j + (g + 1))
                        act.wait_ge(o_done, NG * j + (g + 1))
                        nc.scalar.activation(k_n[:], turn_ps[:, 1].rearrange("p (t n) -> p t n", t=GRP), ACT.Copy)
                        nc.scalar.activation(v_n[:], turn_ps[:, 0].rearrange("p (t n) -> p t n", t=GRP), ACT.Copy).then_inc(turn_read, 1)
                        act.wait_ge(o_done, NG * j + (g + 2))
                        nc.scalar.activation(squares[:], o_ps[:], ACT.Square).then_inc(squared, 1)
                        act.wait_ge(mean_done, NG * j + (g + 1))
                        act.wait_ge(o_normed, NG * j + (g + 1))
                        nc.scalar.activation(rstd[:], mean_ps[:], ACT.Ln, bias=eps[:]).then_inc(norm_act, 1)
                        act.wait_ge(norm_act, 2 * NG * j + (2 * g + 1))
                        nc.scalar.activation(rstd[:], rstd[:], ACT.Exp, scale=-0.5).then_inc(norm_act, 1)

            @block.vector
            def _(dve):
                dve.sem_inc(stored, 16)
                dve.sem_inc(o_normed, 1)
                dve.wait_ge(made, 5)
                dve.wait_ge(base, 64)
                for j in range(GLA_T):
                    dve.wait_ge(stored, 16 * j + 16)
                    nc.vector.tensor_copy(b_a[:], vec[:, bass.ds(j + VEC["b_alpha"], 1)]).then_inc(copied, 1)
                    dve.wait_ge(copied, j + 1)
                    dve.wait_ge(z_done, j + 1)
                    nc.vector.tensor_scalar(z[:], z_ps[:].rearrange("p b n -> p (b n)"), b_a[:], None, ALU.add).then_inc(z_biased, 1)
                    dve.wait_ge(act_step, 8 * j + 3)
                    nc.vector.tensor_scalar(one_e[:], e_neg[:], 1.0, None, ALU.add).then_inc(dve_step, 1)
                    dve.wait_ge(act_step, 8 * j + 4)
                    nc.vector.scalar_tensor_tensor(out=one_e[:], in0=one_e[:], scalar=-1.0, in1=e_neg[:], op0=ALU.add, op1=ALU.subtract).then_inc(dve_step, 1)
                    dve.wait_ge(dve_step, 8 * j + 2)
                    nc.vector.tensor_tensor(one_e[:], grow[:], one_e[:], ALU.subtract).then_inc(dve_step, 1)
                    dve.wait_ge(dve_step, 8 * j + 3)
                    nc.vector.scalar_tensor_tensor(out=e_neg[:], in0=z[:], scalar=0.0, in1=one_e[:], op0=ALU.min, op1=ALU.subtract).then_inc(dve_step, 1)
                    dve.wait_ge(dve_step, 8 * j + 4)
                    nc.vector.tensor_tensor_scan(b_cum[:], restart[:], e_neg[:], 0.0, ALU.mult, ALU.add).then_inc(cum_ready, 1)
                    dve.wait_ge(cum_ready, j + 1)
                    nc.vector.tensor_tensor(chunks(one_e[:]), chunks(b_cum[:])[:, :, GLA_CHUNK - 1:GLA_CHUNK].to_broadcast([P, NCHUNK, GLA_CHUNK]),
                                            chunks(b_cum[:]), ALU.subtract).then_inc(dve_step, 1)
                    dve.wait_ge(act_step, 8 * j + 5)
                    dve.wait_ge(loaded, 80 * j + 80)
                    nc.vector.tensor_tensor(k_end[:], gk[:], z[:], ALU.mult).then_inc(dve_step, 1)
                    dve.wait_ge(act_step, 8 * j + 6)
                    nc.vector.tensor_tensor(k_dec[:], gk[:], grow[:], ALU.mult).then_inc(dve_step, 1)
                    dve.wait_ge(act_step, 8 * j + 8)
                    nc.vector.scalar_tensor_tensor(out=q_dec[:], in0=gq[:], scalar=HEAD_DIM ** -0.5, in1=e_neg[:], op0=ALU.mult, op1=ALU.mult).then_inc(dve_step, 1)
                    for g in range(NG):
                        for h in range(2):
                            dve.wait_ge(att_done, 2 * NG * j + (2 * g + h + 1))
                            if h == 0:
                                dve.wait_ge(o_done, NG * j + (g + 1))
                            nc.vector.copy_predicated(att[:, h], mask[:, None, :].to_broadcast([P, GRP, P]).bitcast(U32),
                                                      att_ps[:, h].rearrange("p (t n) -> p t n", t=GRP)).then_inc(att_masked, 1)
                        dve.wait_ge(kv_done, NG * j + (g + 1))
                        for c in range(CPG):
                            n = CPG * g + c
                            for h in range(2):
                                if n >= 1:
                                    dve.wait_ge(state_done, 2 * NCHUNK * j + (2 * n + h - 1))
                                nc.vector.scalar_tensor_tensor(out=state[half(h), n + 1, half(h)], in0=state[half(h), n, half(h)], scalar=decay[half(h), n:n + 1],
                                                               in1=kv_ps[half(h), c % 2, (c // 2) * P + HEAD_DIM * h:(c // 2) * P + HEAD_DIM * (h + 1)],
                                                               op0=ALU.mult, op1=ALU.add).then_inc(state_done, 1)
                        dve.wait_ge(norm_act, 2 * NG * j + (2 * g + 2))
                        nc.vector.scalar_tensor_tensor(out=o_norm[:], in0=o_ps[:], scalar=vec[:, VEC["out_gain"]:VEC["out_gain"] + 1], in1=rstd[:],
                                                       op0=ALU.mult, op1=ALU.mult).then_inc(o_normed, 1)
                        dve.wait_ge(o_normed, NG * j + (g + 2))
                        cols = slice(g * BLK, (g + 1) * BLK)
                        nc.vector.tensor_tensor(out[:, cols], o_norm[:], gg[:, cols], ALU.mult).then_inc(gated, 1)

            @block.tensor
            def _(pe):
                pe.wait_ge(base, 64)
                pe.wait_ge(made, 5)
                pe.sem_inc(o_done, 1)
                with pe.Fori(0, GLA_T) as j:
                    pe.wait_ge(loaded, 80 * j + 80)
                    for b in range(NBLK):
                        last = nc.tensor.matmul(z_ps[:, b], w_a[:], glow[:, b * BLK:(b + 1) * BLK], start=True, stop=True)
                    last.then_inc(z_done, 1)
                    pe.wait_ge(dve_step, 8 * j + 8)
                    for g in range(NG):
                        if g >= 1:
                            pe.wait_ge(turn_read, NG * j + g)
                        for w, src in ((0, gv), (1, k_end)):
                            for t in range(GRP):
                                o = (GRP * g + t) * P
                                last = nc.tensor.transpose(turn_ps[:, w, t * P:(t + 1) * P], src[:, o:o + P], ident[:])
                        last.then_inc(turned, 1)
                        if g >= 1:
                            pe.wait_ge(att_masked, 2 * NG * j + 2 * g)
                        for h in range(2):
                            for t in range(GRP):
                                o = (GRP * g + t) * P
                                last = nc.tensor.matmul(att_ps[:, h, t * P:(t + 1) * P], k_dec[half(h), o:o + P], q_dec[half(h), o:o + P], start=True, stop=True)
                            last.then_inc(att_done, 1)
                        pe.wait_ge(turn_read, NG * j + (g + 1))
                        if g >= 1:
                            pe.wait_ge(state_done, 2 * NCHUNK * j + 2 * CPG * g)
                        for c in range(CPG):
                            rows = slice(GLA_CHUNK * (c % 2), GLA_CHUNK * (c % 2 + 1))
                            last = nc.tensor.matmul(kv_ps[:, c % 2, (c // 2) * P:(c // 2 + 1) * P], k_n[rows, c // 2], v_n[rows, c // 2], start=True, stop=True)
                        last.then_inc(kv_done, 1)
                        pe.wait_ge(att_masked, 2 * NG * j + (2 * g + 2))
                        pe.wait_ge(state_done, 2 * NCHUNK * j + 2 * CPG * (g + 1))
                        if g >= 1:
                            pe.wait_ge(o_normed, NG * j + (g + 1))
                        for t in range(GRP):
                            for c in range(2):
                                n = CPG * g + 2 * t + c
                                nc.tensor.matmul(o_ps[:, (2 * t + c) * GLA_CHUNK:(2 * t + c + 1) * GLA_CHUNK], state[:, n], q_dec[:, n * GLA_CHUNK:(n + 1) * GLA_CHUNK],
                                                 start=(t == 0 and c == 0), stop=False, skip_group_check=True)
                            for h in range(2):
                                last = nc.tensor.matmul(o_ps[half(h), t * P:(t + 1) * P], v_n[:, t, half(h)], att[:, h, t], start=False, stop=True, skip_group_check=True)
                        last.then_inc(o_done, 1)
                        pe.wait_ge(squared, NG * j + (g + 1))
                        nc.tensor.matmul(mean_ps[:], head_ones[:], squares[:], start=True, stop=True).then_inc(mean_done, 1)


def project_out(nc, vec, mod, mean_rstd, xT, w_out, consts, mix, x2):
    with ExitStack() as ctx:
        sb = lambda n, s, d=F32: ctx.enter_context(nc.sbuf_tensor(n, s, d))
        ps = lambda n, s, d=F32: ctx.enter_context(nc.psum_tensor(n, s, d))
        sem = lambda n: ctx.enter_context(nc.semaphore(n))
        two = lambda n: [sem(n + "_even"), sem(n + "_odd")]
        m_hi, m_lo = sb("po_m_hi", [P, KD, SEQ], F32R), sb("po_m_lo", [P, KD, SEQ], F32R)
        slot = sb("po_slot", [P, 2, SEQ])
        w_raw = sb("po_w_raw", [P, 2, KD * P])
        w_hi, w_lo = sb("po_w_hi", [P, 2, KD, P], F32R), sb("po_w_lo", [P, 2, KD, P], F32R)
        squares = sb("po_squares", [P, SEQ])
        sq_sum = mean_rstd
        mean_ones, eps = sb("po_mean_ones", [P, P]), sb("po_eps", [P, 1])
        banks = ps("po_banks", [P, 8, BLK])
        flat = lambda t: t.rearrange("p k n -> p (k n)")
        in_consts, made, mix_in, mix_hi, mix_lo = sem("po_in_consts"), sem("po_made"), two("po_mix_in"), sem("po_mix_hi"), sem("po_mix_lo")
        w_in, hi_ready, lo_ready, x_in = two("po_w_in"), sem("po_hi_ready"), sem("po_lo_ready"), two("po_x_in")
        tile_done, x2_ready, stored, squared, added = sem("po_tile_done"), sem("po_x2_ready"), two("po_stored"), sem("po_squared"), sem("po_added")
        mean_done, rms_ready, rstd_ready = sem("po_mean_done"), sem("po_rms_ready"), sem("po_rstd_ready")

        with nc.Block() as block:
            @block.sync
            def _(sp):
                sp.dma_start(mean_ones[:], consts[:, C_MEAN * P:(C_MEAN + 1) * P]).then_inc(in_consts, 16)
                for k in range(KD):
                    if k >= 2:
                        sp.wait_ge(mix_lo, k - 1)
                    sp.dma_start(slot[:, k % 2], mix[k]).then_inc(mix_in[k % 2], 16)
                    if k < 2:
                        sp.dma_start(w_raw[:, k], w_out[k]).then_inc(w_in[k], 16)
                sp.wait_ge(mix_lo, KD)
                for m in range(2):
                    sp.dma_start(slot[:, m], xT[:, m]).then_inc(x_in[m], 16)
                with sp.Fori(1, KD // 2) as i:
                    for s in range(2):
                        sp.wait_ge(lo_ready, 2 * i + (s - 1))
                        sp.dma_start(w_raw[:, s], w_out[bass.ds(2 * i + s, 1)].rearrange("o p n -> (o p) n")).then_inc(w_in[s], 16)
                    for s in range(2):
                        sp.wait_ge(stored[s], 16 * i)
                        sp.wait_ge(squared, 2 * i + (s - 1))
                        sp.dma_start(slot[:, s], xT[:, bass.ds(2 * i + s, 1)].rearrange("p o n -> p (o n)")).then_inc(x_in[s], 16)

            @block.gpsimd
            def _(pool):
                nc.gpsimd.memset(eps[:], EPS).then_inc(made, 1)
                pool.wait_ge(made, 1)
                nc.gpsimd.memset(sq_sum[:], 0.0).then_inc(made, 1)
                pool.wait_ge(made, 2)
                for m in range(2):
                    pool.wait_ge(hi_ready, m + 1)
                    nc.gpsimd.tensor_tensor(flat(w_lo[:, m]), w_raw[:, m], flat(w_hi[:, m]).bitcast(F32), ALU.subtract).then_inc(lo_ready, 1)
                with pool.Fori(1, KD // 2) as i:
                    for s in range(2):
                        pool.wait_ge(hi_ready, 2 * i + (s + 1))
                        nc.gpsimd.tensor_tensor(flat(w_lo[:, s]), w_raw[:, s], flat(w_hi[:, s]).bitcast(F32), ALU.subtract).then_inc(lo_ready, 1)
                        pool.wait_ge(squared, 2 * i + (s - 1))
                        nc.gpsimd.tensor_tensor(sq_sum[:], sq_sum[:], squares[:], ALU.add).then_inc(added, 1)
                        pool.wait_ge(added, 2 * i + s)
                for m in (KD - 2, KD - 1):
                    pool.wait_ge(squared, m + 1)
                    nc.gpsimd.tensor_tensor(sq_sum[:], sq_sum[:], squares[:], ALU.add).then_inc(added, 1)
                    pool.wait_ge(added, m + 2)

            @block.scalar
            def _(act):
                act.sem_inc(added, 1)
                for k in range(KD):
                    act.wait_ge(mix_in[k % 2], 16 * (k // 2 + 1))
                    nc.scalar.activation(m_hi[:, k], slot[:, k % 2], ACT.Copy).then_inc(mix_hi, 1)
                    if k < 2:
                        act.wait_ge(w_in[k], 16)
                        nc.scalar.activation(flat(w_hi[:, k]), w_raw[:, k], ACT.Copy).then_inc(hi_ready, 1)
                with act.Fori(1, KD // 2) as i:
                    for s in range(2):
                        act.wait_ge(w_in[s], 16 * i + 16)
                        act.wait_ge(tile_done, 2 * i + (s - 1))
                        nc.scalar.activation(flat(w_hi[:, s]), w_raw[:, s], ACT.Copy).then_inc(hi_ready, 1)
                        act.wait_ge(x2_ready, 2 * i + (s + 1))
                        act.dma_start(x2[bass.ds(2 * i + (s - 2), 1)].rearrange("o p n -> (o p) n"), slot[:, s]).then_inc(stored[s], 16)
                        act.wait_ge(added, 2 * i + (s - 1))
                        nc.scalar.activation(squares[:], slot[:, s], ACT.Square).then_inc(squared, 1)
                for m in (KD - 2, KD - 1):
                    act.wait_ge(x2_ready, m + 3)
                    act.dma_start(x2[m], slot[:, m % 2]).then_inc(stored[m % 2], 16)
                    act.wait_ge(added, m + 1)
                    nc.scalar.activation(squares[:], slot[:, m % 2], ACT.Square).then_inc(squared, 1)
                for b in range(NBLK):
                    act.wait_ge(mean_done, b + 1)
                    nc.scalar.activation(mean_rstd[:, b * BLK:(b + 1) * BLK], banks[:, b], ACT.Sqrt, bias=eps[:]).then_inc(rms_ready, 1)
                for s in range(2):
                    act.wait_ge(stored[s], 16 * (KD // 2))

            @block.vector
            def _(dve):
                for k in range(KD):
                    dve.wait_ge(mix_hi, k + 1)
                    nc.vector.tensor_tensor(m_lo[:, k], slot[:, k % 2], m_hi[:, k].bitcast(F32), ALU.subtract).then_inc(mix_lo, 1)
                with dve.Fori(0, KD // 2) as i:
                    for s in range(2):
                        dve.wait_ge(tile_done, 2 * i + (s + 1))
                        dve.wait_ge(x_in[s], 16 * i + 16)
                        nc.vector.scalar_tensor_tensor(out=slot[:, s], in0=banks[:, 4 * s:4 * s + 4].rearrange("p b n -> p (b n)"),
                                                       scalar=mod[:, bass.ds(2 * i + (s + GATE1), 1)], in1=slot[:, s],
                                                       op0=ALU.mult, op1=ALU.add).then_inc(x2_ready, 1)
                for b in range(NBLK):
                    dve.wait_ge(rms_ready, b + 1)
                    cols = slice(b * BLK, (b + 1) * BLK)
                    nc.vector.reciprocal(mean_rstd[:, cols], mean_rstd[:, cols]).then_inc(rstd_ready, 1)

            @block.tensor
            def _(pe):
                pe.sem_inc(x2_ready, 2)
                pe.wait_ge(in_consts, 16)
                pe.wait_ge(made, 2)
                with pe.Fori(0, KD // 2) as i:
                    for s in range(2):
                        pe.wait_ge(lo_ready, 2 * i + (s + 1))
                        pe.wait_ge(x2_ready, 2 * i + (s + 1))
                        for k in range(KD):
                            pe.wait_ge(mix_lo, k + 1)
                            for b in range(NBLK):
                                cols = slice(b * BLK, (b + 1) * BLK)
                                last = split_products(nc, banks[:, 4 * s + b], w_hi[:, s, k], w_lo[:, s, k], m_hi[:, k, cols], m_lo[:, k, cols],
                                                      k == 0, k == KD - 1)
                        last.then_inc(tile_done, 1)
                pe.wait_ge(added, KD + 1)
                pe.wait_ge(x2_ready, KD + 2)
                for b in range(NBLK):
                    nc.tensor.matmul(banks[:, b], mean_ones[:], sq_sum[:, b * BLK:(b + 1) * BLK], start=True, stop=True).then_inc(mean_done, 1)


def feed_forward(nc, vec, mod, mean_rstd, w_gate_up, w_down, x2, yT):
    UP, DOWN = KF, 2 * KD
    UNITS = UP + DOWN
    HALF = KF // 2
    with ExitStack() as ctx:
        sb = lambda n, s, d=F32: ctx.enter_context(nc.sbuf_tensor(n, s, d))
        ps = lambda n, s, d=F32: ctx.enter_context(nc.psum_tensor(n, s, d))
        sem = lambda n: ctx.enter_context(nc.semaphore(n))
        two = lambda n: [sem(n + "_even"), sem(n + "_odd")]
        h_hi, h_lo = sb("ff_h_hi", [P, KD, BLK], F32R), sb("ff_h_lo", [P, KD, BLK], F32R)
        a_hi, a_lo = sb("ff_a_hi", [P, KF, BLK], F32R), sb("ff_a_lo", [P, KF, BLK], F32R)
        x_blk = sb("ff_x_blk", [P, KD, BLK])
        w_raw = sb("ff_w_raw", [P, 2, 2 * KD * P])
        w_hi, w_lo = sb("ff_w_hi", [P, 2, 2 * KD * P], F32R), sb("ff_w_lo", [P, 2, 2 * KD * P], F32R)
        silu, gated = sb("ff_silu", [P, 2, BLK]), sb("ff_gated", [P, 2, BLK])
        x_res = sb("ff_x_res", [P, 2, BLK])
        y_out = gated
        scale_a = sb("ff_scale_a", [P, KD])
        g_ps, u_ps, d_ps = ps("ff_g_ps", [P, 2, BLK]), ps("ff_u_ps", [P, 2, BLK]), ps("ff_d_ps", [P, 2, BLK])
        up_w = lambda w, s: w[:, s].rearrange("p (g k n) -> p g k n", g=2, k=KD)
        down_w = lambda w, s: w[:, s, 0:HALF * P].rearrange("p (k n) -> p k n", k=HALF)
        size = lambda up: slice(0, 2 * KD * P) if up else slice(0, HALF * P)

        x_in, scaled, xn_ready, h_hi_ready, h_full, h_ready = sem("ff_x_in"), sem("ff_scaled"), sem("ff_xn_ready"), sem("ff_h_hi_ready"), sem("ff_h_full"), sem("ff_h_ready")
        w_in, hi_ready, lo_ready, unit_done = two("ff_w_in"), sem("ff_hi_ready"), sem("ff_lo_ready"), sem("ff_unit_done")
        silu_ready, gated_ready, a_hi_ready, a_ready = sem("ff_silu_ready"), sem("ff_gated_ready"), sem("ff_a_hi_ready"), sem("ff_a_ready")
        res_in, y_ready, stored = two("ff_res_in"), sem("ff_y_ready"), two("ff_stored")

        with nc.Block() as block:
            @block.sync
            def _(sp):
                with sp.Fori(0, NBLK) as t:
                    with sp.Fori(0, UP // 2) as i:
                        for s in range(2):
                            sp.wait_ge(lo_ready, UNITS * t + 2 * i + (s + 1))
                            sp.dma_start(w_raw[:, s], w_gate_up[bass.ds(2 * i + s, 1)].rearrange("o p n -> (o p) n")).then_inc(w_in[s], 16)
                    with sp.Fori(0, DOWN // 2) as i:
                        for s in range(2):
                            sp.wait_ge(lo_ready, UNITS * t + 2 * i + (UP + s + 1))
                            sp.dma_start(w_raw[:, s, size(False)], w_down[bass.ds(2 * i + s, 1)].rearrange("o p n -> (o p) n")).then_inc(w_in[s], 16)

            @block.gpsimd
            def _(pool):
                pool.sem_inc(lo_ready, 2)
                def low(up, s):
                    nc.gpsimd.tensor_tensor(w_lo[:, s, size(up)], w_raw[:, s, size(up)], w_hi[:, s, size(up)].bitcast(F32), ALU.subtract).then_inc(lo_ready, 1)
                with pool.Fori(0, NBLK) as t:
                    with pool.Fori(0, UP // 2) as i:
                        for s in range(2):
                            pool.wait_ge(hi_ready, UNITS * t + 2 * i + (s + 1))
                            low(True, s)
                    with pool.Fori(0, DOWN // 2) as i:
                        for s in range(2):
                            pool.wait_ge(hi_ready, UNITS * t + 2 * i + (UP + s + 1))
                            low(False, s)

            @block.scalar
            def _(act):
                def norm(t):
                    act.wait_ge(xn_ready, t + 1)
                    for k in range(KD):
                        last = nc.scalar.activation(h_hi[:, k], x_blk[:, k], ACT.Identity, bias=mod[:, SHIFT2 + k:SHIFT2 + k + 1], scale=scale_a[:, k:k + 1])
                    last.then_inc(h_hi_ready, 1)

                def load_block(t):
                    act.dma_start(x_blk[:], x2[:, :, t * BLK:(t + 1) * BLK].rearrange("k p n -> p k n")).then_inc(x_in, 16)

                def high(t, up, i, s, n):
                    act.wait_ge(w_in[s], 16 * (UNITS // 2) * t + 16 * i + (16 if up else 16 * (UP // 2) + 16))
                    act.wait_ge(unit_done, UNITS * t + n + 1)
                    nc.scalar.activation(w_hi[:, s, size(up)], w_raw[:, s, size(up)], ACT.Copy).then_inc(hi_ready, 1)

                def gate(t, s, n):
                    act.wait_ge(unit_done, UNITS * t + n + 3)
                    act.wait_ge(gated_ready, UP * t + n + 1)
                    nc.scalar.activation(silu[:, s], g_ps[:, s], ACT.Silu).then_inc(silu_ready, 1)

                def act_high(t, s, n, at):
                    act.wait_ge(gated_ready, UP * t + n + 3)
                    nc.scalar.activation(a_hi[:, at].rearrange("p o n -> p (o n)"), gated[:, s], ACT.Copy).then_inc(a_hi_ready, 1)

                def load_res(t, m, s):
                    act.dma_start(x_res[:, s], x2[m, :, t * BLK:(t + 1) * BLK].rearrange("o p n -> (o p) n")).then_inc(res_in[s], 16)

                def store(t, m, at, s):
                    act.wait_ge(y_ready, KD * t + m + 3)
                    act.dma_start(yT[at, :, t * BLK:(t + 1) * BLK].rearrange("o p n -> (o p) n"), y_out[:, s]).then_inc(stored[s], 16)

                for s in range(2):
                    act.sem_inc(stored[s], 16)
                load_block(0)
                for s in range(2):
                    load_res(0, slice(s, s + 1), s)
                norm(0)
                for t in range(NBLK):
                    for s in range(2):
                        high(t, True, 0, s, s)
                    if t >= 1:
                        store(t - 1, KD - 1, slice(KD - 1, KD), 1)
                        load_res(t, slice(1, 2), 1)
                    with act.Fori(1, UP // 2) as i:
                        for s in range(2):
                            gate(t, s, 2 * i + (s - 2))
                            high(t, True, i, s, 2 * i + s)
                            act_high(t, s, 2 * i + (s - 2), bass.ds(2 * i + (s - 2), 1))
                    for s in range(2):
                        gate(t, s, UP - 2 + s)
                        high(t, False, 0, s, UP + s)
                        act_high(t, s, UP - 2 + s, slice(UP - 2 + s, UP - 1 + s))
                    if t + 1 < NBLK:
                        act.wait_ge(h_ready, t + 1)
                        load_block(t + 1)
                        norm(t + 1)
                    with act.Fori(0, KD // 2 - 1) as i:
                        for o in range(2):
                            for s in range(2):
                                high(t, False, 2 * i + (1 + o), s, 4 * i + (UP + 2 + 2 * o + s))
                            store(t, 2 * i + o, bass.ds(2 * i + o, 1), o)
                            load_res(t, bass.ds(2 * i + (o + 2), 1), o)
                    for s in range(2):
                        high(t, False, KD - 1, s, UP + DOWN - 2 + s)
                    store(t, KD - 2, slice(KD - 2, KD - 1), 0)
                    if t + 1 < NBLK:
                        load_res(t + 1, slice(0, 1), 0)
                store(NBLK - 1, KD - 1, slice(KD - 1, KD), 1)
                for s in range(2):
                    act.wait_ge(stored[s], 16 + 16 * NBLK * (KD // 2))

            @block.vector
            def _(dve):
                dve.sem_inc(gated_ready, 2)
                nc.vector.scalar_tensor_tensor(out=scale_a[:], in0=mod[:, SCALE2:SCALE2 + KD], scalar=1.0, in1=vec[:, VEC["g2"]:VEC["g2"] + KD],
                                               op0=ALU.add, op1=ALU.mult).then_inc(scaled, 1)
                dve.wait_ge(scaled, 1)

                def norm(t):
                    dve.wait_ge(x_in, 16 * (t + 1))
                    nc.vector.tensor_tensor(x_blk[:], x_blk[:], mean_rstd[:, None, t * BLK:(t + 1) * BLK].to_broadcast([P, KD, BLK]), ALU.mult).then_inc(xn_ready, 1)
                    dve.wait_ge(h_hi_ready, t + 1)
                    for k in range(KD):
                        last = nc.vector.tensor_scalar(x_blk[:, k], x_blk[:, k], scale_a[:, k:k + 1], mod[:, SHIFT2 + k:SHIFT2 + k + 1], ALU.mult, ALU.add)
                    last.then_inc(h_full, 1)
                    dve.wait_ge(h_full, t + 1)
                    nc.vector.tensor_tensor(h_lo[:], x_blk[:], h_hi[:].bitcast(F32), ALU.subtract).then_inc(h_ready, 1)

                norm(0)
                for t in range(NBLK):
                    for s in range(2):
                        dve.wait_ge(stored[s], 16 * (KD // 2) * t + 16)
                    with dve.Fori(0, UP // 2) as i:
                        for s in range(2):
                            n = 2 * i + s
                            dve.wait_ge(silu_ready, UP * t + n + 1)
                            dve.wait_ge(a_ready, UP * t + n + 1)
                            nc.vector.tensor_tensor(gated[:, s], silu[:, s], u_ps[:, s], ALU.mult).then_inc(gated_ready, 1)
                            dve.wait_ge(a_hi_ready, UP * t + n + 1)
                            nc.vector.tensor_tensor(a_lo[:, bass.ds(n, 1)].rearrange("p o n -> p (o n)"), gated[:, s],
                                                    a_hi[:, bass.ds(n, 1)].rearrange("p o n -> p (o n)").bitcast(F32), ALU.subtract).then_inc(a_ready, 1)
                    if t + 1 < NBLK:
                        norm(t + 1)
                    with dve.Fori(0, KD // 2) as i:
                        for s in range(2):
                            dve.wait_ge(unit_done, UNITS * t + 4 * i + (UP + 2 * s + 4))
                            dve.wait_ge(res_in[s], 16 * (KD // 2) * t + 16 * i + 16)
                            dve.wait_ge(stored[s], 16 * (KD // 2) * t + 16 * i + 16)
                            nc.vector.scalar_tensor_tensor(out=y_out[:, s], in0=d_ps[:, s], scalar=mod[:, bass.ds(2 * i + (s + GATE2), 1)], in1=x_res[:, s],
                                                           op0=ALU.mult, op1=ALU.add).then_inc(y_ready, 1)

            @block.tensor
            def _(pe):
                pe.sem_inc(unit_done, 2)
                pe.sem_inc(a_ready, 2)
                pe.sem_inc(y_ready, 2)
                for t in range(NBLK):
                    pe.wait_ge(h_ready, t + 1)
                    with pe.Fori(0, UP // 2) as i:
                        for s in range(2):
                            n = 2 * i + s
                            pe.wait_ge(lo_ready, UNITS * t + n + 3)
                            pe.wait_ge(a_ready, UP * t + n + 1)
                            for g, out in ((0, g_ps[:, s]), (1, u_ps[:, s])):
                                for k in range(KD):
                                    last = split_products(nc, out, up_w(w_hi, s)[:, g, k], up_w(w_lo, s)[:, g, k], h_hi[:, k], h_lo[:, k], k == 0, k == KD - 1)
                            last.then_inc(unit_done, 1)
                    with pe.Fori(0, KD // 2) as i:
                        for m in range(2):
                            pe.wait_ge(y_ready, KD * t + 2 * i + (m + 1))
                            for s in range(2):
                                pe.wait_ge(lo_ready, UNITS * t + 4 * i + (UP + 2 * m + s + 3))
                                if s == 1:
                                    pe.wait_ge(a_ready, UP * (t + 1) + 2)
                                for k in range(HALF):
                                    f = HALF * s + k
                                    last = split_products(nc, d_ps[:, m], down_w(w_hi, s)[:, k], down_w(w_lo, s)[:, k], a_hi[:, f], a_lo[:, f], f == 0, f == KF - 1)
                                last.then_inc(unit_done, 1)


def lay_out(inputs):
    a = {k: np.asarray(v) for k, v in inputs.items()}
    f32 = np.float32
    cols = lambda v, n: v.reshape(n, P).T
    w_in = a["w_in"][0]
    cut = np.cumsum([LRU_WIDTH, LRU_WIDTH, FOX_T * P, FOX_T * P, FOX_T * P, FOX_HEADS, GLA_T * P, GLA_T * P, GLA_T * P, GLA_RANK, GLA_T * P])
    xa, ya, fq, fk, fv, ff, gq, gk, gv, glow, gg = np.split(w_in, cut[:-1], axis=1)
    misc = np.zeros((D_MODEL, P), f32)
    misc[:, 0:GLA_RANK] = glow
    misc[:, FF_ROW:FF_ROW + FOX_HEADS] = ff
    w_in = np.concatenate([xa, ya, fq, fk, fv, gq, gk, gv, gg, misc], axis=1)
    tiles = lambda w, kt, mt: np.ascontiguousarray(w.reshape(kt, P, mt, -1).transpose(2, 1, 0, 3))
    blocks = np.zeros((2, LRU_T, P, P), f32)
    for g, name in enumerate(("lru_w_r", "lru_w_i")):
        for n in range(LRU_WIDTH // HEAD_DIM):
            o = HEAD_DIM * (n % 2)
            blocks[g, n // 2, o:o + HEAD_DIM, o:o + HEAD_DIM] = a[name][0, n]
    b_f = np.zeros((P, 1), f32)
    b_f[FF_ROW:FF_ROW + FOX_HEADS, 0] = a["fox_b_f"][0]
    twice = lambda v: np.concatenate([v, v]).reshape(P, 1)
    parts = {
        "c": cols(a["c"][0], KD), "g1": cols(a["norm1_gain"][0], KD), "g2": cols(a["norm2_gain"][0], KD),
        "b_mod": cols(a["b_mod"][0], 6 * KD), "conv_w": np.concatenate([cols(w, LRU_T) for w in a["conv_w"][0]], axis=1),
        "conv_b": cols(a["conv_b"][0], LRU_T), "b_r": cols(a["lru_b_r"][0], LRU_T), "b_i": cols(a["lru_b_i"][0], LRU_T),
        "lam": cols(a["lru_lambda"][0], LRU_T), "q_gain": twice(a["fox_q_gain"][0]), "k_gain": twice(a["fox_k_gain"][0]),
        "b_alpha": cols(a["gla_b_alpha"][0], GLA_T), "out_gain": twice(a["gla_out_gain"][0]), "b_f": b_f,
    }
    gate_up = a["ffn_w_gate_up"][0].reshape(KD, P, 2, KF, P).transpose(3, 1, 2, 0, 4)
    down = a["ffn_w_down"][0].reshape(2, KF // 2, P, KD, P).transpose(3, 0, 2, 1, 4)
    p, q = np.arange(P)[:, None], np.arange(P)[None, :]
    same_head = p // HEAD_DIM == q // HEAD_DIM
    consts = np.concatenate([
        np.full((P, P), 1.0 / D_MODEL), same_head / HEAD_DIM, p == q,
        np.where(q <= p, 0.0, MASKED),
        same_head & (p <= q),
    ], axis=1).astype(f32)
    tiles6 = 2 * FOX_T
    head_of = 2 * np.arange(tiles6)[None, :] + np.arange(P)[:, None] // HEAD_DIM
    one_hot = head_of[:, :, None] == np.arange(2 * FOX_HEADS)
    fox_rows = np.zeros((P, tiles6 * 2 * FOX_HEADS + tiles6 * P), f32)
    fox_rows[:, :tiles6 * 2 * FOX_HEADS] = (one_hot / HEAD_DIM).reshape(P, -1)
    fox_rows[:2 * FOX_HEADS, tiles6 * 2 * FOX_HEADS:] = one_hot.transpose(2, 1, 0).reshape(2 * FOX_HEADS, -1)
    return {
        "xT": np.ascontiguousarray(a["x"][0].T).reshape(KD, P, SEQ),
        "vec": np.ascontiguousarray(np.concatenate([parts[k] for k in VEC], axis=1)),
        "w_mod": tiles(a["w_mod"][0], KD, MOD_CHUNKS),
        "w_in": tiles(w_in, KD, N_PROJ).reshape(N_PROJ, P, KD * P),
        "w_gates": blocks,
        "w_alpha": np.ascontiguousarray(a["gla_w_alpha"][0]),
        "w_out": tiles(a["w_out"][0], KD, KD).reshape(KD, P, KD * P),
        "w_gate_up": np.ascontiguousarray(gate_up).reshape(KF, P, 2 * KD * P),
        "w_down": np.ascontiguousarray(down).reshape(2 * KD, P, (KF // 2) * P),
        "consts": consts,
        "fox_rows": fox_rows,
    }


def build(nc, xT, vec_in, w_mod, w_in, w_gates, w_alpha, w_out, w_gate_up, w_down, consts, fox_rows, yT):
    proj = nc.dram_tensor("proj_dram", [N_PROJ, P, SEQ], F32).ap()
    xT = xT.rearrange("k p n -> p k n")
    with ExitStack() as ctx:
        vec = ctx.enter_context(nc.sbuf_tensor("vec", [P, N_VEC], F32))
        mod = ctx.enter_context(nc.sbuf_tensor("mod", [P, 6 * KD], F32))
        project_in(nc, vec, mod, xT, w_mod, w_in, consts, vec_in, proj)
        mix = nc.dram_tensor("mix_dram", [MIX_T, P, SEQ], F32).ap()
        x2 = nc.dram_tensor("x2_dram", [KD, P, SEQ], F32).ap()
        q_split = nc.dram_tensor("q_split_dram", [FOX_HEADS, 2, HEAD_DIM, SEQ], F32).ap()
        k_split = nc.dram_tensor("k_split_dram", [FOX_HEADS, 2, HEAD_DIM, SEQ], F32).ap()
        bias_split = nc.dram_tensor("bias_split_dram", [FOX_HEADS, 2, SEQ], F32).ap()
        recurrent_branch(nc, vec, w_gates, proj, mix)
        with nc.sbuf_tensor("v_nat", [P, FOX_HEADS, SEQ // P, P], F32R) as v_nat:
            fox_operands(nc, vec, consts, fox_rows, proj, q_split, k_split, bias_split, v_nat)
            forgetting_attention(nc, consts, q_split, k_split, bias_split, v_nat, mix)
        gated_linear_attention(nc, vec, consts, w_alpha, proj, mix)
        mean_rstd = ctx.enter_context(nc.sbuf_tensor("mean_rstd", [P, SEQ], F32))
        project_out(nc, vec, mod, mean_rstd, xT, w_out, consts, mix, x2)
        feed_forward(nc, vec, mod, mean_rstd, w_gate_up, w_down, x2, yT)


def kernel(**inputs):
    import concourse.bacc as _bacc
    from concourse.bass_utils import run_bass_kernel_spmd as _run

    arrays = lay_out(inputs)
    nc = _bacc.Bacc("TRN2", target_bir_lowering=False, num_devices=1)
    args = [nc.dram_tensor(f"in_{name}", a.shape, mybir.dt.from_np(a.dtype), kind="ExternalInput").ap() for name, a in arrays.items()]
    args.append(nc.dram_tensor("out_yT", (KD, P, SEQ), F32, kind="ExternalOutput").ap())
    build(nc, *args)
    r = _run(nc, [{f"in_{name}": a for name, a in arrays.items()}], core_ids=[0])
    y = np.asarray(r.results[0]["out_yT"])
    return np.ascontiguousarray(y.reshape(D_MODEL, SEQ).T).reshape(1, SEQ, D_MODEL)
```

```python
from contextlib import ExitStack

import numpy as np

import concourse.bass as bass
from concourse import mybir

F32 = mybir.dt.float32
F32R = mybir.dt.float32r
U32 = mybir.dt.uint32
ALU = mybir.AluOpType
ACT = mybir.ActivationFunctionType
AX = mybir.AxisListType

P = 128
D_MODEL = 1024
SEQ = 2048
EPS = 1e-6
HEAD_DIM = 64
LRU_WIDTH = 384
CONV_WIDTH = 4
LRU_C = 8.0
FOX_HEADS = 6
GLA_HEADS = 4
GLA_RANK = 16
GLA_TAU = 16.0
GLA_CHUNK = 64
D_FF = 2816

KD = D_MODEL // P
KF = D_FF // P
BLK = 512
NBLK = SEQ // BLK
LRU_T = LRU_WIDTH // P
FOX_T = FOX_HEADS * HEAD_DIM // P
GLA_T = GLA_HEADS * HEAD_DIM // P
T_XA, T_YA = 0, LRU_T
T_FQ = T_YA + LRU_T
T_FK, T_FV = T_FQ + FOX_T, T_FQ + 2 * FOX_T
T_GQ = T_FV + FOX_T
T_GK, T_GV, T_GG = T_GQ + GLA_T, T_GQ + 2 * GLA_T, T_GQ + 3 * GLA_T
T_MISC = T_GG + GLA_T
N_PROJ = T_MISC + 1
FF_ROW = 32
MIX_T = LRU_T + FOX_T + GLA_T
MASKED = -1.0e30

C_MEAN, C_HEAD, C_IDENT, C_CAUSAL, C_CAUSAL_T, C_CHUNK = range(6)

VEC = {}
_at = 0
for _name, _n in (("c", KD), ("g1", KD), ("g2", KD), ("b_mod", 6 * KD), ("conv_w", CONV_WIDTH * LRU_T),
                  ("conv_b", LRU_T), ("b_r", LRU_T), ("b_i", LRU_T), ("lam", LRU_T), ("q_gain", 1),
                  ("k_gain", 1), ("b_alpha", GLA_T), ("out_gain", 1), ("b_f", 1)):
    VEC[_name] = _at
    _at += _n
N_VEC = _at

MOD_COLS = 256
MOD_CHUNKS = 6 * D_MODEL // MOD_COLS
SHIFT1, SCALE1, GATE1, SHIFT2, SCALE2, GATE2 = (i * KD for i in range(6))


def split_products(nc, out, hi, lo, act_hi, act_lo, first, last):
    nc.tensor.matmul(out, hi, act_hi, start=first, stop=False)
    nc.tensor.matmul(out, hi, act_lo, start=False, stop=False)
    return nc.tensor.matmul(out, lo, act_hi, start=False, stop=last)


def project_in_and_recur(nc, vec, mod, xT, w_mod, w_in, w_gates, consts, vec_in, proj, mix):
    PAD = CONV_WIDTH - 1
    FIRST_CHUNKS = 2 * D_MODEL // MOD_COLS
    PAIRS = N_PROJ // 2
    LRU_PAIR = 5
    CHUNKS_A_PAIR = (MOD_CHUNKS - FIRST_CHUNKS) // (LRU_PAIR - 1)
    assert CHUNKS_A_PAIR == 4 and T_XA == 0 and 2 * LRU_PAIR > T_YA + LRU_T and LRU_PAIR + 2 * LRU_T < PAIRS
    SOFTPLUS, LINKS = 5, PAD - 1 + 6
    with ExitStack() as ctx:
        sb = lambda n, s, d=F32: ctx.enter_context(nc.sbuf_tensor(n, s, d))
        ps = lambda n, s, d=F32: ctx.enter_context(nc.psum_tensor(n, s, d))
        sem = lambda n: ctx.enter_context(nc.semaphore(n))
        two = lambda n: [sem(n + "_even"), sem(n + "_odd")]

        h_hi, h_lo = sb("h_hi", [P, KD, SEQ], F32R), sb("h_lo", [P, KD, SEQ], F32R)
        x_blk = sb("x_blk", [P, 2 * KD * BLK])
        shared = sb("shared", [P, 2 * KD * MOD_COLS])
        w_raw = sb("w_raw", [P, KD * P])
        w_hi, w_lo = sb("w_hi", [P, 2, KD, P], F32R), sb("w_lo", [P, 2, KD, P], F32R)
        mod_acc = sb("mod_acc", [P, 2, MOD_COLS])
        mean_ones, ones_col, eps = sb("mean_ones", [P, P]), sb("ones_col", [P, 1]), sb("eps", [P, 1])
        c_act, scale_a = sb("c_act", [P, KD]), sb("scale_a", [P, KD])
        rstd = sb("rstd", [P, BLK])
        xa = sb("lru_xa", [P, PAD + BLK])
        carry = sb("lru_carry", [P, 1])
        sp_abs, sp_exp, sp_one, sp_ln, sp_rec, sp_err = (sb("lru_sp%d" % i, [P, LRU_T]) for i in range(6))
        rate, neg_rate = sb("lru_rate", [P, LRU_T]), sb("lru_neg_rate", [P, LRU_T])
        banks = ps("banks", [P, 8, BLK])

        mod_w = shared[:, :].rearrange("p (s k n) -> p s k n", s=2, k=KD)
        squares = shared[:, :].rearrange("p (k n) -> p k n", k=KD)
        x_kt = x_blk[:, :].rearrange("p (s k n) -> p s k n", s=2, k=KD)
        slots = x_blk[:, :].rearrange("p (i n) -> p i n", n=BLK)
        stage = slots[:, 0:NBLK]
        ya, conv, r_gate, i_gate, tanh_y, decay, gelu_y, inv, u_in, state, out = (slots[:, NBLK + i] for i in range(11))
        gates = slots[:, NBLK + 11, 0:2 * P].rearrange("p (g n) -> p g n", g=2)
        ssum = mod_acc[:, :].rearrange("p s n -> p (s n)")
        mod_ps = banks[:, 4, 0:6 * KD]
        gate_ps = banks[:, 5:7]
        norm_ps = banks[:, 7, :]
        flat = lambda t: t.rearrange("p k n -> p (k n)")
        lam = vec[:, VEC["lam"]:VEC["lam"] + LRU_T]
        wcol = lambda name, i: vec[:, VEC[name] + i:VEC[name] + i + 1]

        params_in, c_ready, ones_ready = sem("params_in"), sem("c_ready"), sem("ones_ready")
        modw_in, modacc_ready, partial, mod_done, mod_ready = two("modw_in"), sem("modacc_ready"), sem("partial"), sem("mod_done"), sem("mod_ready")
        x_in, sq_ready, ssum_ready, norm_sum, rms_ready, rstd_ready = two("x_in"), sem("sq_ready"), sem("ssum_ready"), sem("norm_sum"), sem("rms_ready"), sem("rstd_ready")
        xn_ready, h_hi_ready, h_full, h_ready = sem("xn_ready"), sem("h_hi_ready"), sem("h_full"), sem("h_ready")
        w_in_sem, hi_ready, lo_ready = sem("w_in_sem"), sem("hi_ready"), sem("lo_ready")
        block_done, staged, stored = sem("block_done"), sem("staged"), [sem("stored_block%d" % b) for b in range(NBLK)]
        lru_in, gates_in, link, sp_act, rate_ready, halo = sem("lru_in"), sem("gates_in"), sem("lru_link"), sem("lru_sp_act"), sem("rate_ready"), sem("lru_halo")
        conv_ready, gates_done, act_done, ix_done, sqrt_done = sem("lru_conv_ready"), sem("lru_gates_done"), sem("lru_act_done"), sem("lru_ix_done"), sem("lru_sqrt_done")
        out_ready, out_stored, carried, tile_start = sem("lru_out_ready"), sem("lru_out_stored"), sem("lru_carried"), sem("lru_tile_start")

        def pairs(engine, step, before_tile=None):
            for s in range(2):
                step(0, None, s)
            with engine.Fori(1, LRU_PAIR) as i:
                for s in range(2):
                    step(i, -1, s)
            for t in range(LRU_T):
                if before_tile:
                    before_tile(t)
                with engine.Fori(LRU_PAIR + 2 * t, LRU_PAIR + 2 * t + 2) as i:
                    for s in range(2):
                        step(i, t, s)
            for s in range(2):
                step(PAIRS - 1, None, s)

        unit = lambda i, s, each=1, more=0: (2 * each) * i + (each * (s - 2 * LRU_PAIR) + more)
        with nc.Block() as block:
            @block.sync
            def _(sp):
                sp.dma_start(vec[:], vec_in).then_inc(params_in, 16)
                sp.dma_start(mean_ones[:], consts[:, C_MEAN * P:(C_MEAN + 1) * P]).then_inc(params_in, 16)
                for n in range(2):
                    sp.dma_start(mod_w[:, n], w_mod[n]).then_inc(modw_in[n], 16)
                with sp.Fori(1, FIRST_CHUNKS // 2) as i:
                    for s in range(2):
                        sp.wait_ge(modacc_ready, 2 * i + (s - 1))
                        sp.dma_start(mod_w[:, s], w_mod[bass.ds(2 * i + s, 1)].rearrange("o p k n -> (o p) k n")).then_inc(modw_in[s], 16)
                sp.dma_start(w_raw[:], w_in[0]).then_inc(w_in_sem, 16)
                sp.wait_ge(lo_ready, 1)
                sp.dma_start(w_raw[:], w_in[1]).then_inc(w_in_sem, 16)

                def chunk(i, s, c):
                    n = FIRST_CHUNKS - 4 + 2 * s + c
                    sp.wait_ge(modacc_ready, 4 * i + (n - 1))
                    sp.dma_start(mod_w[:, c], w_mod[bass.ds(4 * i + n, 1)].rearrange("o p k n -> (o p) k n")).then_inc(modw_in[c], 16)

                def step(i, t, s):
                    static = isinstance(i, int)
                    if t is not None and t >= 0:
                        sp.wait_ge(out_ready, unit(i, s, 1, 1))
                        sp.wait_ge(halo, unit(i, s, 1, 1))
                        token = (2 * BLK) * i + BLK * (s - 2 * (LRU_PAIR + 2 * t))
                        sp.dma_start(xa[:, PAD:], proj[T_XA + t, :, bass.ds(token, BLK)]).then_inc(lru_in, 16)
                        sp.dma_start(ya, proj[T_YA + t, :, bass.ds(token, BLK)]).then_inc(lru_in, 16)
                    if t == -1:
                        for c in range(2):
                            chunk(i, s, c)
                    if not (static and i):
                        sp.wait_ge(lo_ready, 2 * i + (s + 2))
                        sp.dma_start(w_raw[:], (w_in[2 + s] if static else w_in[bass.ds(2 * i + (s + 2), 1)].rearrange("o p n -> (o p) n"))).then_inc(w_in_sem, 16)
                    for b in range(NBLK):
                        sp.wait_ge(staged, 8 * i + (4 * s + b + 5))
                        dst = proj[s + 2 * i, :, b * BLK:(b + 1) * BLK] if static else proj[bass.ds(2 * i + s, 1), :, b * BLK:(b + 1) * BLK].rearrange("o p n -> (o p) n")
                        sp.dma_start(dst, stage[:, b]).then_inc(stored[b], 16)
                sp.wait_ge(ssum_ready, NBLK)
                pairs(sp, step)
                for b in range(NBLK):
                    sp.wait_ge(stored[b], 16 + 16 * N_PROJ)

            @block.gpsimd
            def _(pool):
                nc.gpsimd.memset(eps[:], EPS).then_inc(ones_ready, 1)
                nc.gpsimd.memset(ones_col[:], 1.0).then_inc(ones_ready, 1)
                for n in range(2):
                    pool.dma_start(x_kt[:, n], xT[:, :, n * BLK:(n + 1) * BLK]).then_inc(x_in[n], 16)

                def lows(n, s):
                    pool.wait_ge(hi_ready, n)
                    nc.gpsimd.tensor_tensor(flat(w_lo[:, s]), w_raw[:], flat(w_hi[:, s]).bitcast(F32), ALU.subtract).then_inc(lo_ready, 1)
                lows(1, 0)
                lows(2, 1)
                for n in range(NBLK):
                    pool.wait_ge(h_full, n + 1)
                    nc.gpsimd.tensor_tensor(h_lo[:, :, n * BLK:(n + 1) * BLK], x_kt[:, n % 2], h_hi[:, :, n * BLK:(n + 1) * BLK].bitcast(F32), ALU.subtract).then_inc(h_ready, 1)
                    if n + 2 < NBLK:
                        pool.wait_ge(h_ready, n + 1)
                        pool.dma_start(x_kt[:, n % 2], xT[:, :, (n + 2) * BLK:(n + 3) * BLK]).then_inc(x_in[n % 2], 16)
                pool.wait_ge(h_ready, NBLK)

                def step(i, t, s):
                    if t is not None and t >= 0:
                        pool.wait_ge(act_done, unit(i, s, 5, 2))
                        nc.gpsimd.tensor_tensor(u_in, i_gate, conv, ALU.mult).then_inc(ix_done, 1)
                    if not (isinstance(i, int) and i):
                        lows(2 * i + (s + 3), s)

                def start_tile(t):
                    pool.wait_ge(out_ready, NBLK * t + 1)
                    pool.wait_ge(halo, NBLK * t + 1)
                    if t >= 1:
                        pool.wait_ge(carried, NBLK * t)
                    pool.dma_start(gates, w_gates[:, t].rearrange("g p n -> p g n")).then_inc(gates_in, 16)
                    nc.gpsimd.memset(xa[:, 0:PAD], 0.0).then_inc(tile_start, 1)
                    pool.wait_ge(tile_start, 2 * t + 1)
                    nc.gpsimd.memset(carry[:], 0.0).then_inc(tile_start, 1)
                pairs(pool, step, start_tile)

            @block.scalar
            def _(act):
                act.sem_inc(out_stored, 16)
                for b in range(NBLK):
                    act.sem_inc(stored[b], 16)
                act.wait_ge(params_in, 32)
                act.wait_ge(ones_ready, 2)
                nc.scalar.activation(c_act[:], vec[:, VEC["c"]:VEC["c"] + KD], ACT.Silu).then_inc(c_ready, 1)
                nc.scalar.activation(sp_abs[:], lam, ACT.Abs).then_inc(sp_act, 1)
                act.wait_ge(sp_act, 1)
                nc.scalar.activation(sp_exp[:], sp_abs[:], ACT.Exp, scale=-1.0).then_inc(sp_act, 1)
                act.wait_ge(link, 1)
                nc.scalar.activation(sp_ln[:], sp_one[:], ACT.Ln).then_inc(sp_act, 1)

                def highs(s):
                    nc.scalar.activation(flat(w_hi[:, s]), w_raw[:], ACT.Copy).then_inc(hi_ready, 1)
                for s in range(2):
                    act.wait_ge(w_in_sem, 16 * (s + 1))
                    highs(s)
                act.wait_ge(mod_ready, 1)

                def square(n):
                    act.wait_ge(x_in[n % 2], 16 * (n // 2 + 1))
                    if n >= 1:
                        act.wait_ge(ssum_ready, n)
                    nc.scalar.activation(squares, x_kt[:, n % 2], ACT.Square).then_inc(sq_ready, 1)

                def root(n):
                    act.wait_ge(norm_sum, n + 1)
                    if n >= 1:
                        act.wait_ge(xn_ready, n)
                    nc.scalar.activation(rstd[:], norm_ps, ACT.Sqrt, bias=eps[:]).then_inc(rms_ready, 1)
                square(0)
                root(0)
                for n in range(NBLK):
                    if n + 1 < NBLK:
                        square(n + 1)
                    act.wait_ge(xn_ready, n + 1)
                    for k in range(KD):
                        last = nc.scalar.activation(h_hi[:, k, n * BLK:(n + 1) * BLK], x_kt[:, n % 2, k], ACT.Identity,
                                                    bias=mod[:, SHIFT1 + k:SHIFT1 + k + 1], scale=scale_a[:, k:k + 1])
                    last.then_inc(h_hi_ready, 1)
                    if n + 1 < NBLK:
                        root(n + 1)
                act.wait_ge(h_ready, NBLK)

                def step(i, t, s):
                    if t is not None and t >= 0:
                        act.wait_ge(gates_done, unit(i, s, 1, 2))
                        act.wait_ge(out_ready, unit(i, s, 1, 1))
                        nc.scalar.activation(r_gate, gate_ps[:, 0], ACT.Sigmoid, bias=wcol("b_r", t)).then_inc(act_done, 1)
                        nc.scalar.activation(i_gate, gate_ps[:, 1], ACT.Sigmoid, bias=wcol("b_i", t)).then_inc(act_done, 1)
                        act.wait_ge(act_done, unit(i, s, 5, 2))
                        act.wait_ge(rate_ready, 2)
                        nc.scalar.activation(tanh_y, r_gate, ACT.Tanh, scale=rate[:, t:t + 1]).then_inc(act_done, 1)
                        nc.scalar.activation(decay, r_gate, ACT.Exp, scale=neg_rate[:, t:t + 1]).then_inc(act_done, 1)
                        act.wait_ge(lru_in, unit(i, s, 32, 32))
                        nc.scalar.activation(gelu_y, ya, ACT.Gelu_apprx_tanh).then_inc(act_done, 1)
                        act.wait_ge(link, unit(i, s, LINKS, SOFTPLUS + PAD + 3))
                        nc.scalar.activation(inv, inv, ACT.Sqrt).then_inc(sqrt_done, 1)
                        act.wait_ge(out_ready, unit(i, s, 1, 2))
                        token = (2 * BLK) * i + BLK * (s - 2 * (LRU_PAIR + 2 * t))
                        act.dma_start(mix[t, :, bass.ds(token, BLK)], out).then_inc(out_stored, 16)
                    if not (isinstance(i, int) and i):
                        act.wait_ge(w_in_sem, 32 * i + (16 * s + 48))
                        act.wait_ge(block_done, 8 * i + (4 * s + 4))
                        act.wait_ge(lo_ready, 2 * i + (s + 2))
                        highs(s)
                pairs(act, step)
                act.wait_ge(out_stored, 16 + 16 * NBLK * LRU_T)

            @block.vector
            def _(dve):
                dve.sem_inc(out_ready, 1)
                dve.sem_inc(halo, 1)
                dve.wait_ge(sp_act, 2)
                nc.vector.tensor_scalar(sp_one[:], sp_exp[:], 1.0, None, ALU.add).then_inc(link, 1)
                dve.wait_ge(link, 1)
                nc.vector.reciprocal(sp_rec[:], sp_one[:])
                nc.vector.scalar_tensor_tensor(out=sp_err[:], in0=sp_one[:], scalar=-1.0, in1=sp_exp[:], op0=ALU.add, op1=ALU.subtract).then_inc(link, 1)
                dve.wait_ge(link, 2)
                nc.vector.tensor_tensor(sp_err[:], sp_err[:], sp_rec[:], ALU.mult).then_inc(link, 1)
                dve.wait_ge(link, 3)
                dve.wait_ge(sp_act, 3)
                nc.vector.tensor_tensor(sp_ln[:], sp_ln[:], sp_err[:], ALU.subtract).then_inc(link, 1)
                nc.vector.tensor_scalar(sp_abs[:], lam, 0.0, None, ALU.min)
                dve.wait_ge(link, 4)
                nc.vector.tensor_scalar(sp_ln[:], sp_ln[:], LRU_C, None, ALU.mult).then_inc(link, 1)
                dve.wait_ge(link, 5)
                nc.vector.scalar_tensor_tensor(out=rate[:], in0=sp_abs[:], scalar=-LRU_C, in1=sp_ln[:], op0=ALU.mult, op1=ALU.add).then_inc(rate_ready, 1)
                dve.wait_ge(rate_ready, 1)
                nc.vector.tensor_scalar(neg_rate[:], rate[:], -1.0, None, ALU.mult).then_inc(rate_ready, 1)
                dve.wait_ge(c_ready, 1)

                def modulate(s, loaded, done, sums):
                    dve.wait_ge(modw_in[s], loaded)
                    dve.wait_ge(mod_done, done)
                    nc.vector.tensor_scalar(mod_acc[:, s], mod_w[:, s, 0], c_act[:, 0:1], None, ALU.mult).then_inc(partial, 1)
                    for k in range(1, KD):
                        dve.wait_ge(partial, sums + k)
                        nc.vector.scalar_tensor_tensor(out=mod_acc[:, s], in0=mod_w[:, s, k], scalar=c_act[:, k:k + 1], in1=mod_acc[:, s],
                                                       op0=ALU.mult, op1=ALU.add).then_inc(partial if k < KD - 1 else modacc_ready, 1)
                with dve.Fori(0, FIRST_CHUNKS // 2) as i:
                    for s in range(2):
                        modulate(s, 16 * i + 16, 2 * i + (s + 1), 2 * (KD - 1) * i + (KD - 1) * s)
                dve.wait_ge(mod_done, FIRST_CHUNKS + 2)
                FIRST_COLS = SCALE1 + KD
                SUMS = (KD - 1) * FIRST_CHUNKS + 1
                nc.vector.tensor_tensor(mod[:, 0:FIRST_COLS], mod_ps[:, 0:FIRST_COLS], vec[:, VEC["b_mod"]:VEC["b_mod"] + FIRST_COLS], ALU.add).then_inc(partial, 1)
                dve.wait_ge(partial, SUMS)
                nc.vector.scalar_tensor_tensor(out=scale_a[:], in0=mod[:, SCALE1:SCALE1 + KD], scalar=1.0, in1=vec[:, VEC["g1"]:VEC["g1"] + KD],
                                               op0=ALU.add, op1=ALU.mult).then_inc(mod_ready, 1)
                dve.wait_ge(mod_ready, 1)

                def sum_squares(n):
                    dve.wait_ge(sq_ready, n + 1)
                    if n >= 1:
                        dve.wait_ge(norm_sum, n)
                    nc.vector.tensor_reduce(ssum, squares.rearrange("p k n -> p n k"), AX.X, ALU.add).then_inc(ssum_ready, 1)
                sum_squares(0)
                for n in range(NBLK):
                    xb = x_kt[:, n % 2]
                    dve.wait_ge(rms_ready, n + 1)
                    nc.vector.reciprocal(rstd[:], rstd[:]).then_inc(rstd_ready, 1)
                    dve.wait_ge(rstd_ready, n + 1)
                    nc.vector.tensor_tensor(xb, xb, rstd[:, None, :].to_broadcast([P, KD, BLK]), ALU.mult).then_inc(xn_ready, 1)
                    if n + 1 < NBLK:
                        sum_squares(n + 1)
                    dve.wait_ge(h_hi_ready, n + 1)
                    for k in range(KD):
                        last = nc.vector.tensor_scalar(xb[:, k], xb[:, k], scale_a[:, k:k + 1], mod[:, SHIFT1 + k:SHIFT1 + k + 1], ALU.mult, ALU.add)
                    last.then_inc(h_full, 1)
                dve.wait_ge(h_ready, NBLK)

                def copy_block(i, s, b):
                    dve.wait_ge(block_done, 8 * i + (4 * s + b + 1))
                    dve.wait_ge(stored[b], 32 * i + (16 * s + 16))
                    nc.vector.tensor_copy(stage[:, b], banks[:, b]).then_inc(staged, 1)

                def convolve(i, t, s):
                    tap = lambda j: xa[:, j:j + BLK]
                    at = lambda x: unit(i, s, LINKS, SOFTPLUS + x)
                    dve.wait_ge(lru_in, unit(i, s, 32, 32))
                    dve.wait_ge(tile_start, 2 * t + 2)
                    dve.wait_ge(gates_done, unit(i, s, 1, 1))
                    nc.vector.tensor_scalar(conv, tap(PAD), wcol("conv_w", PAD * LRU_T + t), wcol("conv_b", t), ALU.mult, ALU.add).then_inc(link, 1)
                    for j in range(PAD):
                        dve.wait_ge(link, at(j + 1))
                        nc.vector.scalar_tensor_tensor(out=conv, in0=tap(j), scalar=wcol("conv_w", j * LRU_T + t), in1=conv,
                                                       op0=ALU.mult, op1=ALU.add).then_inc(link if j < PAD - 1 else conv_ready, 1)
                    dve.wait_ge(conv_ready, unit(i, s, 1, 1))
                    nc.vector.tensor_copy(xa[:, 0:PAD], xa[:, BLK:BLK + PAD]).then_inc(halo, 1)
                    dve.wait_ge(halo, unit(i, s, 1, 2))

                def recur(i, s):
                    at = lambda x: unit(i, s, LINKS, SOFTPLUS + PAD + x)
                    dve.wait_ge(act_done, unit(i, s, 5, 3))
                    nc.vector.tensor_scalar(inv, tanh_y, 1.0, None, ALU.add).then_inc(link, 1)
                    dve.wait_ge(link, at(1))
                    nc.vector.reciprocal(inv, inv).then_inc(link, 1)
                    dve.wait_ge(link, at(2))
                    nc.vector.scalar_tensor_tensor(out=inv, in0=tanh_y, scalar=2.0, in1=inv, op0=ALU.mult, op1=ALU.mult).then_inc(link, 1)
                    dve.wait_ge(ix_done, unit(i, s, 1, 1))
                    dve.wait_ge(sqrt_done, unit(i, s, 1, 1))
                    nc.vector.tensor_tensor(u_in, u_in, inv, ALU.mult).then_inc(link, 1)
                    dve.wait_ge(link, at(4))
                    dve.wait_ge(act_done, unit(i, s, 5, 5))
                    nc.vector.tensor_tensor_scan(state, decay, u_in, carry[:, 0:1], ALU.mult, ALU.add).then_inc(link, 1)
                    dve.wait_ge(link, at(5))
                    nc.vector.tensor_copy(carry[:], state[:, BLK - 1:BLK]).then_inc(carried, 1)
                    dve.wait_ge(carried, unit(i, s, 1, 1))
                    dve.wait_ge(out_stored, unit(i, s, 16, 16))
                    nc.vector.tensor_tensor(out, state, gelu_y, ALU.mult).then_inc(out_ready, 1)

                def step(i, t, s):
                    if t is not None and t >= 0:
                        convolve(i, t, s)
                    for b in range(NBLK):
                        if t == -1 and b % 2 == 0:
                            c = 2 * s + b // 2
                            modulate(b // 2, 32 * i + (8 * FIRST_CHUNKS + 16 * s - 16), 4 * i + (FIRST_CHUNKS - 4 + c + 1),
                                     4 * (KD - 1) * i + (SUMS + (KD - 1) * (c - 4)))
                        copy_block(i, s, b)
                        if t is not None and t >= 0 and b == 1:
                            recur(i, s)
                pairs(dve, step)
                dve.wait_ge(mod_done, MOD_CHUNKS + 2)
                nc.vector.tensor_tensor(mod[:, FIRST_COLS:], mod_ps[:, FIRST_COLS:], vec[:, VEC["b_mod"] + FIRST_COLS:VEC["b_mod"] + 6 * KD], ALU.add)

            @block.tensor
            def _(pe):
                pe.sem_inc(mod_done, 2)
                pe.sem_inc(gates_done, 1)
                pe.wait_ge(ones_ready, 2)
                pe.wait_ge(params_in, 32)

                def reduce_chunk(s, ready, column):
                    pe.wait_ge(modacc_ready, ready)
                    for j in range(MOD_COLS // P):
                        last = nc.tensor.matmul(mod_ps[:, bass.ds(column + j, 1)], mod_acc[:, s, j * P:(j + 1) * P], ones_col[:], start=True, stop=True)
                    last.then_inc(mod_done, 1)
                with pe.Fori(0, FIRST_CHUNKS // 2) as i:
                    for s in range(2):
                        reduce_chunk(s, 2 * i + (s + 1), 4 * i + 2 * s)
                for n in range(NBLK):
                    pe.wait_ge(ssum_ready, n + 1)
                    if n >= 1:
                        pe.wait_ge(rms_ready, n)
                    nc.tensor.matmul(norm_ps, mean_ones[:], ssum, start=True, stop=True).then_inc(norm_sum, 1)
                pe.sem_inc(staged, NBLK)

                def step(i, t, s):
                    pe.wait_ge(lo_ready, 2 * i + (s + 1))
                    for b in range(NBLK):
                        if isinstance(i, int) and i == 0 and s == 0:
                            pe.wait_ge(h_ready, b + 1)
                            pe.wait_ge(h_hi_ready, b + 1)
                        pe.wait_ge(staged, 8 * i + (4 * s + b + 1))
                        cols = slice(b * BLK, (b + 1) * BLK)
                        for k in range(KD):
                            last = split_products(nc, banks[:, b], w_hi[:, s, k], w_lo[:, s, k], h_hi[:, k, cols], h_lo[:, k, cols], k == 0, k == KD - 1)
                        last.then_inc(block_done, 1)
                        if t == -1 and b % 2 == 1:
                            c = 2 * s + b // 2
                            reduce_chunk(b // 2, 4 * i + (FIRST_CHUNKS - 4 + c + 1), 8 * i + (2 * (FIRST_CHUNKS - 4 + c)))
                        if t is not None and t >= 0 and b == 1:
                            pe.wait_ge(conv_ready, unit(i, s, 1, 1))
                            pe.wait_ge(gates_in, 16 * t + 16)
                            pe.wait_ge(out_ready, unit(i, s, 1, 1))
                            for g in range(2):
                                last = nc.tensor.matmul(gate_ps[:, g], gates[:, g], conv, start=True, stop=True)
                            last.then_inc(gates_done, 1)
                pairs(pe, step)


def fox_operands(nc, vec, consts, fox_rows, proj, q_split, k_split, bias_split, v_split):
    HEADS2 = 2 * FOX_HEADS
    TILES = 2 * FOX_T
    with ExitStack() as ctx:
        sb = lambda n, s, d=F32: ctx.enter_context(nc.sbuf_tensor(n, s, d))
        ps = lambda n, s, d=F32: ctx.enter_context(nc.psum_tensor(n, s, d))
        sem = lambda n: ctx.enter_context(nc.semaphore(n))
        qk = sb("fp_qk", [P, TILES, SEQ])
        v_raw = sb("fp_v", [P, 2, SEQ])
        v_nat = sb("fp_v_nat", [P, FOX_HEADS, SEQ // P, 3 * HEAD_DIM], F32R)
        squares = sb("fp_squares", [P, SEQ])
        hi = sb("fp_hi", [P, SEQ], F32R)
        lo = sb("fp_lo", [P, SEQ], F32R)
        ident = sb("fp_ident", [P, P])
        rows_sel = sb("fp_rows_sel", [P, TILES, HEADS2])
        back_sel = sb("fp_back_sel", [HEADS2, TILES, P])
        rows = [sb("fp_rows%d" % i, [FF_ROW + FOX_HEADS, SEQ]) for i in range(4)]
        mean, rstd, newton = (r[0:HEADS2] for r in rows[:3])
        logit, e_neg, log1p, err = (r[FF_ROW:FF_ROW + FOX_HEADS] for r in rows)
        bias_hi, bias_lo = (t[FF_ROW:FF_ROW + FOX_HEADS] for t in (hi, lo))
        ones_col = sb("fp_ones_col", [FF_ROW + FOX_HEADS, 1])
        ones_row = ones_col[FF_ROW:FF_ROW + FOX_HEADS].to_broadcast([FOX_HEADS, SEQ])
        gains = sb("fp_gains", [P, 2])
        banks = ps("fp_banks", [P, 8, BLK])
        loaded, v_loaded, squared, summed, mean_out = sem("fp_loaded"), sem("fp_v_loaded"), sem("fp_squared"), sem("fp_summed"), sem("fp_mean_out")
        ln_done, rstd_done, spread, normed, hi_done, lo_done = sem("fp_ln_done"), sem("fp_rstd_done"), sem("fp_spread"), sem("fp_normed"), sem("fp_hi_done"), sem("fp_lo_done")
        hi_out, lo_out, v_t, v_hi_done, v_lo_done = sem("fp_hi_out"), sem("fp_lo_out"), sem("fp_v_t"), sem("fp_v_hi_done"), sem("fp_v_lo_done")
        f_act, f_link, f_hi, f_out, chain, consts_in = sem("fp_f_act"), sem("fp_f_link"), sem("fp_f_hi"), sem("fp_f_out"), sem("fp_chain"), sem("fp_consts_in")
        v_out = sem("fp_v_out")
        v_hi, v_lo = v_nat[:, :, :, 0:HEAD_DIM], v_nat[:, :, :, 2 * HEAD_DIM:3 * HEAD_DIM]
        with nc.Block() as block:
            @block.sync
            def _(sp):
                sp.dma_start(ident[:], consts[:, C_IDENT * P:(C_IDENT + 1) * P]).then_inc(consts_in, 16)
                sp.dma_start(rows_sel[:], fox_rows[:, 0:TILES * HEADS2].rearrange("p (t h) -> p t h", t=TILES)).then_inc(consts_in, 16)
                sp.dma_start(back_sel[:], fox_rows[0:HEADS2, TILES * HEADS2:].rearrange("h (t p) -> h t p", t=TILES)).then_inc(consts_in, 16)
                sp.dma_start(qk[:], proj[T_FQ:T_FQ + TILES].rearrange("t p n -> p t n")).then_inc(loaded, 16)
                sp.dma_start(v_raw[:], proj[T_FV:T_FV + 2].rearrange("t p n -> p t n")).then_inc(v_loaded, 16)
                sp.wait_ge(v_t, 4)
                sp.dma_start(v_raw[:, 0], proj[T_FV + 2]).then_inc(v_loaded, 16)
                for t in range(TILES):
                    split, j = (q_split, k_split)[t // FOX_T], t % FOX_T
                    sp.wait_ge(hi_done, t + 1)
                    for h in range(2):
                        sp.dma_start(split[2 * j + h, 0], hi[HEAD_DIM * h:HEAD_DIM * (h + 1)].bitcast(F32)).then_inc(hi_out, 16)
                    sp.wait_ge(lo_done, t + 1)
                    for h in range(2):
                        sp.dma_start(split[2 * j + h, 1], lo[HEAD_DIM * h:HEAD_DIM * (h + 1)].bitcast(F32)).then_inc(lo_out, 16)
                for j in range(FOX_T):
                    sp.wait_ge(v_lo_done, 4 * j + 4)
                    sp.dma_start(v_split[2 * j:2 * j + 2].rearrange("h p n -> p h n"), v_nat[:, 2 * j:2 * j + 2].rearrange("p h t n -> p h (t n)").bitcast(F32)).then_inc(v_out, 16)
                sp.wait_ge(v_out, 16 * FOX_T)
                sp.wait_ge(hi_out, 32 * TILES)
                sp.wait_ge(lo_out, 32 * TILES)

            @block.gpsimd
            def _(pool):
                pool.dma_start(logit, proj[T_MISC, FF_ROW:FF_ROW + FOX_HEADS]).then_inc(f_out, 16)
                nc.gpsimd.memset(ones_col[:], 1.0).then_inc(f_act, 1)
                pool.wait_ge(f_act, 1)
                nc.gpsimd.memset(v_nat[:, :, :, HEAD_DIM:2 * HEAD_DIM].rearrange("p h t d -> p (h t) d").bitcast(F32), 1.0).then_inc(f_act, 1)
                pool.wait_ge(f_hi, 2)
                pool.dma_start(bias_split[:, 0], bias_hi.bitcast(F32)).then_inc(f_out, 16)
                pool.dma_start(bias_split[:, 1], bias_lo.bitcast(F32)).then_inc(f_out, 16)
                pool.wait_ge(f_out, 48)
                for t in range(TILES):
                    pool.wait_ge(hi_done, t + 1)
                    if t >= 1:
                        pool.wait_ge(lo_out, 32 * t)
                    nc.gpsimd.tensor_tensor(lo[:], qk[:, t], hi[:].bitcast(F32), ALU.subtract).then_inc(lo_done, 1)

            @block.scalar
            def _(act):
                act.wait_ge(loaded, 16)
                for t in range(TILES):
                    if t >= 1:
                        act.wait_ge(summed, t)
                    nc.scalar.activation(squares[:], qk[:, t], ACT.Square).then_inc(squared, 1)
                act.wait_ge(mean_out, 1)
                nc.scalar.activation(rstd, mean, ACT.Ln).then_inc(ln_done, 1)
                act.wait_ge(ln_done, 1)
                nc.scalar.activation(rstd, rstd, ACT.Exp, scale=-0.5).then_inc(ln_done, 1)
                act.wait_ge(f_link, 1)
                nc.scalar.activation(e_neg, logit, ACT.Abs).then_inc(ln_done, 1)
                act.wait_ge(ln_done, 3)
                nc.scalar.activation(e_neg, e_neg, ACT.Exp, scale=-1.0).then_inc(ln_done, 1)
                act.wait_ge(f_link, 2)
                nc.scalar.activation(log1p, err, ACT.Ln).then_inc(ln_done, 1)
                act.wait_ge(f_out, 48)
                for t in range(TILES):
                    act.wait_ge(normed, t + 1)
                    if t >= 1:
                        act.wait_ge(lo_done, t)
                        act.wait_ge(hi_out, 32 * t)
                    nc.scalar.activation(hi[:], qk[:, t], ACT.Copy).then_inc(hi_done, 1)
                for n in range(4 * FOX_T):
                    j, g = n // 4, n % 4
                    act.wait_ge(v_t, n + 1)
                    nc.scalar.activation(v_hi[:, 2 * j:2 * j + 2, 4 * g:4 * g + 4].rearrange("p h t d -> p t h d"),
                                         banks[:, 4 + n % 4].rearrange("p (t h d) -> p t h d", t=4, h=2), ACT.Copy).then_inc(v_hi_done, 1)

            @block.vector
            def _(dve):
                nc.vector.tensor_scalar(gains[:, 0:1], vec[:, VEC["q_gain"]:VEC["q_gain"] + 1], HEAD_DIM ** -0.5, None, ALU.mult)
                nc.vector.tensor_copy(gains[:, 1:2], vec[:, VEC["k_gain"]:VEC["k_gain"] + 1])
                dve.wait_ge(f_out, 16)
                nc.vector.tensor_scalar(logit, logit, vec[FF_ROW:FF_ROW + FOX_HEADS, VEC["b_f"]:VEC["b_f"] + 1], None, ALU.add).then_inc(f_link, 1)
                dve.wait_ge(summed, TILES)
                nc.vector.tensor_scalar(mean, banks[0:HEADS2, 0:4].rearrange("p b n -> p (b n)"), EPS, None, ALU.add).then_inc(mean_out, 1)
                dve.wait_ge(ln_done, 2)
                nc.vector.tensor_tensor(newton, rstd, rstd, ALU.mult).then_inc(chain, 1)
                dve.wait_ge(chain, 1)
                nc.vector.tensor_tensor(newton, newton, mean, ALU.mult).then_inc(chain, 1)
                dve.wait_ge(chain, 2)
                nc.vector.tensor_scalar(newton, newton, -0.5, 1.5, ALU.mult, ALU.add).then_inc(chain, 1)
                dve.wait_ge(chain, 3)
                nc.vector.tensor_tensor(rstd, rstd, newton, ALU.mult).then_inc(rstd_done, 1)
                dve.wait_ge(ln_done, 4)
                nc.vector.tensor_scalar(err, e_neg, 1.0, None, ALU.add).then_inc(f_link, 1)
                dve.wait_ge(ln_done, 5)
                nc.vector.scalar_tensor_tensor(out=err, in0=err, scalar=-1.0, in1=e_neg, op0=ALU.add, op1=ALU.subtract).then_inc(f_link, 1)
                dve.wait_ge(f_link, 3)
                nc.vector.tensor_scalar(e_neg, logit, 0.0, None, ALU.min).then_inc(f_link, 1)
                nc.vector.tensor_tensor(log1p, log1p, err, ALU.subtract).then_inc(f_link, 1)
                dve.wait_ge(f_link, 5)
                nc.vector.tensor_tensor(err, log1p, e_neg, ALU.subtract).then_inc(f_link, 1)
                dve.wait_ge(f_link, 6)
                dve.wait_ge(f_act, 1)
                nc.vector.tensor_tensor_scan(log1p, ones_row, err, 0.0, ALU.mult, ALU.add).then_inc(f_link, 1)
                dve.wait_ge(f_link, 7)
                nc.vector.tensor_copy(bias_hi, log1p).then_inc(f_hi, 1)
                dve.wait_ge(f_hi, 1)
                nc.vector.tensor_tensor(bias_lo, log1p, bias_hi.bitcast(F32), ALU.subtract).then_inc(f_hi, 1)
                for t in range(TILES):
                    dve.wait_ge(spread, t + 1)
                    nc.vector.scalar_tensor_tensor(out=qk[:, t], in0=qk[:, t], scalar=gains[:, t // FOX_T:t // FOX_T + 1],
                                                   in1=banks[:, 0:4].rearrange("p b n -> p (b n)"), op0=ALU.mult, op1=ALU.mult).then_inc(normed, 1)
                for n in range(4 * FOX_T):
                    j, g = n // 4, n % 4
                    dve.wait_ge(v_hi_done, n + 1)
                    for h in range(2):
                        last = nc.vector.tensor_tensor(v_lo[:, 2 * j + h, 4 * g:4 * g + 4],
                                                       banks[:, 4 + n % 4].rearrange("p (t h d) -> p t h d", t=4, h=2)[:, :, h],
                                                       v_hi[:, 2 * j + h, 4 * g:4 * g + 4].bitcast(F32), ALU.subtract)
                    last.then_inc(v_lo_done, 1)

            @block.tensor
            def _(pe):
                pe.wait_ge(consts_in, 48)
                for t in range(TILES):
                    pe.wait_ge(squared, t + 1)
                    for b in range(NBLK):
                        last = nc.tensor.matmul(banks[0:HEADS2, b], rows_sel[:, t], squares[:, b * BLK:(b + 1) * BLK], start=(t == 0), stop=(t == TILES - 1))
                    last.then_inc(summed, 1)
                pe.wait_ge(v_loaded, 16)

                def transpose_v(n):
                    if n == 8:
                        pe.wait_ge(v_loaded, 32)
                    for t in range(4):
                        o = (4 * (n % 4) + t) * P
                        last = nc.tensor.transpose(banks[:, 4 + n % 4, t * P:(t + 1) * P], v_raw[:, n // 4 % 2, o:o + P], ident[:])
                    last.then_inc(v_t, 1)

                for n in range(4):
                    transpose_v(n)
                pe.wait_ge(rstd_done, 1)
                for t in range(TILES):
                    if t >= 1:
                        pe.wait_ge(normed, t)
                    for b in range(NBLK):
                        last = nc.tensor.matmul(banks[:, b], back_sel[:, t], rstd[:, b * BLK:(b + 1) * BLK], start=True, stop=True)
                    last.then_inc(spread, 1)
                for n in range(4, 4 * FOX_T):
                    pe.wait_ge(v_lo_done, n - 3)
                    transpose_v(n)


def forgetting_attention(nc, consts, q_split, k_split, bias_split, v_split, mix):
    HPB = 2
    LOOPS = FOX_HEADS // HPB
    NU = HPB * NBLK
    UNITS = [(u // NBLK % HPB, u % NBLK) for u in range(2 * NU)]
    TPB = BLK // P
    VW = 2 * HEAD_DIM
    ITEMS = [(u, kt, max(0, kt - TPB * b)) for u, (hh, b) in enumerate(UNITS[:NU]) for kt in range(TPB * (b + 1))]
    CHUNKS = [(u, i, c, min(BLK, (TPB * b + i + 1) * P - c * BLK)) for u, (hh, b) in enumerate(UNITS) for i in range(TPB) for c in range(b + 1)]
    NC = NI = len(ITEMS)
    chunks_of = lambda u: [n for n, x in enumerate(CHUNKS) if x[0] == u]
    items_of = lambda u: [m for m, x in enumerate(ITEMS) if x[0] == u]
    LEAD, AHEAD = 22, 3
    turns = {m: [u for u in range(2 * NU) if chunks_of(u)[-1] - LEAD + 2 == m] for m in range(NI)}
    EARLY = [u for u in range(2 * NU) if chunks_of(u)[-1] - LEAD + 2 < 0]
    SB, TB, PB = 2, 3, 4
    on_pool = lambda m: ITEMS[m][1] % 3 == 1
    pool_count = lambda m: sum(on_pool(x) for x in range(m + 1))
    dve_count = lambda m: m + 1 - pool_count(m)
    POOL_ALL, DVE_ALL = pool_count(NI - 1), dve_count(NI - 1)

    with ExitStack() as ctx:
        sb = lambda n, s, d=F32: ctx.enter_context(nc.sbuf_tensor(n, s, d))
        ps = lambda n, s, d=F32: ctx.enter_context(nc.psum_tensor(n, s, d))
        sem = lambda n: ctx.enter_context(nc.semaphore(n))
        two = lambda n: [sem(n + "_even"), sem(n + "_odd")]
        k_a, q_a = sb("fa_k_a", [P, HPB, SEQ], F32R), sb("fa_q_a", [P, HPB, SEQ], F32R)
        v = sb("fa_v", [P, HPB, SEQ // P, 3 * HEAD_DIM], F32R)
        k_b, q_b = sb("fa_k_b", [HEAD_DIM + 4, HPB, SEQ], F32R), sb("fa_q_b", [HEAD_DIM + 4, HPB, SEQ], F32R)
        MAXROW = HEAD_DIM + 2
        ROWS_B = HEAD_DIM + 4
        ident, ident_r = sb("fa_ident", [P, P]), sb("fa_ident_r", [P, P], F32R)
        masks, masks_r = sb("fa_masks", [P, 2, P]), sb("fa_masks_r", [P, 2, P], F32R)
        ch_max = sb("fa_ch_max", [P, 2, TPB, NBLK])
        neg_max = sb("fa_neg_max", [P, 2, TPB])
        m_cols = sb("fa_m_cols", [P, 2, TPB, ROWS_B], F32R)
        probs = sb("fa_probs", [P, PB, BLK])
        p_hi, p_lo = sb("fa_p_hi", [P, PB, BLK], F32R), sb("fa_p_lo", [P, PB, BLK], F32R)
        inv_sum, newton = sb("fa_inv_sum", [HEAD_DIM, 2, BLK]), sb("fa_newton", [HEAD_DIM, 2, BLK])
        o_t = sb("fa_o_t", [P, NBLK, BLK])
        s_ps, st_ps = ps("fa_s_ps", [P, SB, BLK]), ps("fa_st_ps", [P, TB, BLK])
        o_ps, m_ps = ps("fa_o_ps", [P, 2, BLK]), ps("fa_m_ps", [P, BLK])

        const_in, made, filled = sem("fa_const_in"), sem("fa_made"), sem("fa_filled")
        qk_in, v_in = two("fa_qk_in"), two("fa_v_in")
        m_turned, m_copied = sem("fa_m_turned"), sem("fa_m_copied")
        s_done, max_done, neg_done, m_ready = sem("fa_s_done"), sem("fa_max_done"), sem("fa_neg_done"), sem("fa_m_ready")
        st_done, hi_done, lo_dve, lo_pool, pv_done = sem("fa_st_done"), sem("fa_hi_done"), sem("fa_lo_dve"), sem("fa_lo_pool"), sem("fa_pv_done")
        ln_sum, inv_done, newton_a, newton_b, fin_done, stored = sem("fa_ln_sum"), sem("fa_inv_done"), sem("fa_newton_a"), sem("fa_newton_b"), sem("fa_fin_done"), [sem("fa_stored_block%d" % b) for b in range(NBLK)]

        with nc.Block() as block:
            @block.sync
            def _(sp):
                sp.dma_start(ident[:], consts[:, C_IDENT * P:(C_IDENT + 1) * P]).then_inc(const_in, 16)
                sp.dma_start(masks[:], consts[:, C_CAUSAL * P:(C_CAUSAL + 2) * P].rearrange("p (w n) -> p w n", w=2)).then_inc(const_in, 16)
                sp.wait_ge(filled, 2)
                with sp.Fori(0, LOOPS) as j:
                    for hh in range(HPB):
                        h = bass.ds(HPB * j + hh, 1)
                        sp.wait_ge(st_done, NI * j + (items_of(NBLK * hh + NBLK - 1)[-1] + 1))
                        one = lambda t: t.rearrange("o d n -> (o d) n")
                        sp.dma_start(q_a[:, hh].bitcast(F32), q_split[h].rearrange("o w d n -> (o w d) n")).then_inc(qk_in[hh], 16)
                        sp.dma_start(k_a[0:HEAD_DIM, hh].bitcast(F32), one(k_split[h, 0])).then_inc(qk_in[hh], 16)
                        sp.dma_start(k_a[HEAD_DIM:P, hh].bitcast(F32), one(k_split[h, 0])).then_inc(qk_in[hh], 16)
                        sp.dma_start(q_b[0:HEAD_DIM, hh].bitcast(F32), one(q_split[h, 0])).then_inc(qk_in[hh], 16)
                        sp.dma_start(k_b[0:HEAD_DIM, hh].bitcast(F32), one(k_split[h, 1])).then_inc(qk_in[hh], 16)
                        sp.dma_start(k_b[HEAD_DIM:MAXROW, hh].bitcast(F32), one(bias_split[h])).then_inc(qk_in[hh], 16)
                        sp.wait_ge(pv_done, NI * j + (items_of(NBLK * hh + NBLK - 1)[-1] + 1))
                        sp.dma_start(v[:, hh].rearrange("p t n -> p (t n)").bitcast(F32), v_split[h].rearrange("o p n -> (o p) n")).then_inc(v_in[hh], 16)
                sp.sem_inc(qk_in[0], 96)

            @block.gpsimd
            def _(pool):
                nc.gpsimd.memset(q_b[HEAD_DIM:].bitcast(F32), 1.0).then_inc(filled, 1)
                pool.wait_ge(filled, 1)
                nc.gpsimd.memset(k_b[HEAD_DIM:].bitcast(F32), 1.0).then_inc(filled, 1)
                pool.wait_ge(filled, 2)
                nc.gpsimd.memset(m_cols[:].bitcast(F32), 1.0).then_inc(filled, 1)
                with pool.Fori(0, LOOPS) as j:
                    for m, (u, kt, r) in enumerate(ITEMS):
                        if on_pool(m):
                            pool.wait_ge(hi_done, NI * j + (m + 1))
                            nc.gpsimd.tensor_tensor(p_lo[:, m % PB, r * P:BLK], probs[:, m % PB, r * P:BLK], p_hi[:, m % PB, r * P:BLK].bitcast(F32),
                                                    ALU.subtract).then_inc(lo_pool, 1)

            @block.scalar
            def _(act):
                act.sem_inc(m_copied, 1)
                act.wait_ge(filled, 1)
                for b in range(NBLK):
                    act.sem_inc(stored[b], 16)

                def copy_m(u, loops):
                    hh, b = UNITS[u]
                    act.wait_ge(m_turned, loops + (u + 3))
                    nc.scalar.activation(q_b[HEAD_DIM:ROWS_B, hh, b * BLK:(b + 1) * BLK], m_ps[HEAD_DIM:ROWS_B], ACT.Copy).then_inc(m_copied, 1)
                for u in EARLY:
                    copy_m(u, 0)
                with act.Fori(0, LOOPS) as j:
                    def store(b):
                        act.wait_ge(fin_done, NU * j + (NBLK + b + 3))
                        act.dma_start(mix[bass.ds(j + LRU_T, 1), :, b * BLK:(b + 1) * BLK].rearrange("o p n -> (o p) n"), o_t[:, b]).then_inc(stored[b], 16)

                    def invert(u):
                        act.wait_ge(pv_done, NI * j + (NI + items_of(u)[-1] + 1))
                        act.wait_ge(fin_done, NU * j + (u + 1))
                        nc.scalar.activation(newton[:, u % 2], o_ps[HEAD_DIM:P, u % 2], ACT.Ln).then_inc(ln_sum, 1)
                        act.wait_ge(ln_sum, NU * j + (u + 1))
                        nc.scalar.activation(inv_sum[:, u % 2], newton[:, u % 2], ACT.Exp, scale=-1.0).then_inc(inv_done, 1)
                    for m, (u, kt, r) in enumerate(ITEMS):
                        cols = slice(r * P, BLK)
                        act.wait_ge(st_done, NI * j + (NI + m + 1))
                        act.wait_ge(pv_done, NI * j + (NI + m + 1 - PB))
                        nc.scalar.activation(probs[:, m % PB, cols], st_ps[:, m % TB, cols], ACT.Exp)
                        nc.scalar.activation(p_hi[:, m % PB, cols], st_ps[:, m % TB, cols], ACT.Exp).then_inc(hi_done, 1)
                        for x in turns.get(m - 1, ()):
                            copy_m(x, NU * j)
                        if u > 0 and kt == 3:
                            invert(u - 1)
                        if u > NBLK and kt == 7:
                            store(u - NBLK - 1)
                    invert(NU - 1)
                    store(NBLK - 1)
                for b in range(NBLK):
                    act.wait_ge(stored[b], 16 + 16 * LOOPS)

            @block.vector
            def _(dve):
                dve.wait_ge(const_in, 32)
                nc.vector.tensor_copy(ident_r[:], ident[:]).then_inc(made, 1)
                nc.vector.tensor_copy(masks_r[:], masks[:]).then_inc(made, 1)
                dve.sem_inc(max_done, SB)
                dve.sem_inc(fin_done, 2)
                dve.sem_inc(pv_done, NI)
                dve.sem_inc(m_turned, 2)
                dve.wait_ge(filled, 3)

                def maxima(n, chunks, units):
                    u, i, c, w = CHUNKS[n]
                    b = UNITS[u][1]
                    dve.wait_ge(s_done, chunks + (n + 1))
                    nc.vector.tensor_reduce(ch_max[:, u % 2, i, c:c + 1], s_ps[:, n % SB, 0:w], AX.X, ALU.max).then_inc(max_done, 1)
                    if n == chunks_of(u)[-1]:
                        dve.wait_ge(max_done, chunks + (n + 1 + SB))
                        nc.vector.tensor_reduce(neg_max[:, u % 2], ch_max[:, u % 2, :, 0:b + 1], AX.X, ALU.max, negate=True).then_inc(neg_done, 1)
                        dve.wait_ge(neg_done, 2 * units + (2 * u + 1))
                        dve.wait_ge(m_turned, units + (u + 1))
                        nc.vector.tensor_copy(m_cols[:, u % 2, :, MAXROW], neg_max[:, u % 2]).then_inc(neg_done, 1)
                        dve.wait_ge(neg_done, 2 * units + (2 * u + 2))
                        nc.vector.tensor_tensor(m_cols[:, u % 2, :, MAXROW + 1], neg_max[:, u % 2], m_cols[:, u % 2, :, MAXROW].bitcast(F32), ALU.subtract).then_inc(m_ready, 1)
                for n in range(LEAD):
                    maxima(n, 0, 0)
                with dve.Fori(0, LOOPS) as j:
                    def correct(u):
                        dve.wait_ge(inv_done, NU * j + (u + 1))
                        nc.vector.tensor_tensor(newton[:, u % 2], o_ps[HEAD_DIM:P, u % 2], inv_sum[:, u % 2], ALU.mult).then_inc(newton_a, 1)

                    def finish(u):
                        hh, b = UNITS[u]
                        dve.wait_ge(newton_a, NU * j + (u + 1))
                        nc.vector.scalar_tensor_tensor(out=inv_sum[:, u % 2], in0=newton[:, u % 2], scalar=-2.0, in1=inv_sum[:, u % 2], op0=ALU.add, op1=ALU.mult).then_inc(newton_b, 1)
                        dve.wait_ge(newton_b, NU * j + (u + 1))
                        if hh == 0:
                            dve.wait_ge(stored[b], 16 * j + 16)
                        nc.vector.scalar_tensor_tensor(out=o_t[HEAD_DIM * hh:HEAD_DIM * (hh + 1), b], in0=o_ps[0:HEAD_DIM, u % 2], scalar=-1.0, in1=inv_sum[:, u % 2], op0=ALU.mult, op1=ALU.mult).then_inc(fin_done, 1)
                    for m, (u, kt, r) in enumerate(ITEMS):
                        if not on_pool(m):
                            dve.wait_ge(hi_done, NI * j + (m + 1))
                            nc.vector.tensor_tensor(p_lo[:, m % PB, r * P:BLK], probs[:, m % PB, r * P:BLK], p_hi[:, m % PB, r * P:BLK].bitcast(F32),
                                                    ALU.subtract).then_inc(lo_dve, 1)
                        maxima(m + LEAD, NC * j, NU * j)
                        if u > 0 and kt == 2:
                            correct(u - 1)
                        if u > 0 and kt == 3:
                            finish(u - 1)
                    correct(NU - 1)
                    finish(NU - 1)

            @block.tensor
            def _(pe):
                pe.wait_ge(made, 2)
                pe.wait_ge(filled, 2)
                pe.sem_inc(st_done, NI)

                def score(n, loop):
                    u, i, c, w = CHUNKS[n]
                    hh, b = UNITS[u]
                    if n == chunks_of(u)[0] and b == 0:
                        pe.wait_ge(qk_in[hh], 96 * loop + (96 * (u // NU) + 96))
                    pe.wait_ge(max_done, NC * loop + (n + 1))
                    out, keys = s_ps[:, n % SB, 0:w], slice(c * BLK, c * BLK + w)
                    qt = slice((TPB * b + i) * P, (TPB * b + i + 1) * P)
                    diagonal = c == b
                    nc.tensor.matmul(out, q_a[:, hh, qt], k_a[:, hh, keys], start=True, stop=False)
                    last = nc.tensor.matmul(out, q_b[0:MAXROW, hh, qt], k_b[0:MAXROW, hh, keys], start=False, stop=not diagonal)
                    if diagonal:
                        last = nc.tensor.matmul(s_ps[:, n % SB, w - P:w], ident_r[:], masks_r[:, 0], start=False, stop=True)
                    last.then_inc(s_done, 1)

                def turn_m(u, loop):
                    pe.wait_ge(m_ready, NU * loop + (u + 1))
                    pe.wait_ge(m_copied, NU * loop + (u + 1))
                    for i in range(TPB):
                        last = nc.tensor.matmul(m_ps[0:ROWS_B, i * P:(i + 1) * P], m_cols[:, u % 2, i], ident_r[:], start=True, stop=True)
                    last.then_inc(m_turned, 1)

                for n in range(LEAD):
                    score(n, 0)
                for u in EARLY:
                    turn_m(u, 0)
                with pe.Fori(0, LOOPS) as j:
                    def score_t(m):
                        u, kt, r = ITEMS[m]
                        hh, b = UNITS[u]
                        if m == items_of(u)[0]:
                            pe.wait_ge(m_copied, NU * j + (u + 2))
                        if m >= TB:
                            pe.wait_ge(hi_done, NI * j + (m + 1 - TB))
                        out, kts = st_ps[:, m % TB, r * P:BLK], slice(kt * P, (kt + 1) * P)
                        qs = slice(b * BLK + r * P, (b + 1) * BLK)
                        diagonal = kt >= TPB * b
                        nc.tensor.matmul(out, k_a[:, hh, kts], q_a[:, hh, qs], start=True, stop=False)
                        last = nc.tensor.matmul(out, k_b[:, hh, kts], q_b[:, hh, qs], start=False, stop=not diagonal)
                        if diagonal:
                            last = nc.tensor.matmul(st_ps[:, m % TB, r * P:(r + 1) * P], ident_r[:], masks_r[:, 1], start=False, stop=True)
                        last.then_inc(st_done, 1)

                    def times_v(m):
                        u, kt, r = ITEMS[m]
                        hh, b = UNITS[u]
                        if kt == 0:
                            pe.wait_ge(fin_done, NU * j + (u + 1))
                        if kt == 0 and b == 0:
                            pe.wait_ge(v_in[hh], 16 * j + 16)
                        if on_pool(m):
                            pe.wait_ge(lo_pool, POOL_ALL * j + pool_count(m))
                        else:
                            pe.wait_ge(lo_dve, DVE_ALL * j + dve_count(m))
                        qs, first, end = slice(r * P, BLK), kt == 0, kt == TPB * b + TPB - 1
                        nc.tensor.matmul(o_ps[:, u % 2, qs], v[:, hh, kt, 0:VW], p_hi[:, m % PB, qs], start=first, stop=False, skip_group_check=True)
                        nc.tensor.matmul(o_ps[0:HEAD_DIM, u % 2, qs], v[:, hh, kt, VW:VW + HEAD_DIM], p_hi[:, m % PB, qs], start=False, stop=False, skip_group_check=True)
                        nc.tensor.matmul(o_ps[:, u % 2, qs], v[:, hh, kt, 0:VW], p_lo[:, m % PB, qs], start=False, stop=end, skip_group_check=True).then_inc(pv_done, 1)

                    for m in range(AHEAD):
                        score_t(m)
                    for m in range(NI):
                        score(m + LEAD, j)
                        if m + AHEAD < NI:
                            score_t(m + AHEAD)
                        for u in turns[m]:
                            turn_m(u, j)
                        times_v(m)


def gated_linear_attention(nc, vec, consts, w_alpha, proj, mix):
    NCHUNK = SEQ // GLA_CHUNK
    GRP = 4
    NG = NBLK
    ALL = GLA_T * NG
    CPG = BLK // GLA_CHUNK
    with ExitStack() as ctx:
        sb = lambda n, s, d=F32: ctx.enter_context(nc.sbuf_tensor(n, s, d))
        ps = lambda n, s, d=F32: ctx.enter_context(nc.psum_tensor(n, s, d))
        sem = lambda n: ctx.enter_context(nc.semaphore(n))
        two = lambda n: [sem(n + "_even"), sem(n + "_odd")]
        gq, gk, gv, gg = (sb("ga_" + n, [P, GLA_T, SEQ]) for n in ("gq", "gk", "gv", "gg"))
        glow, w_a = sb("ga_glow", [GLA_RANK, SEQ]), sb("ga_w_a", [GLA_RANK, GLA_T * P])
        ident, head_ones, mask = sb("ga_ident", [P, P]), sb("ga_head_ones", [P, P]), sb("ga_mask", [P, P])
        restart = sb("ga_restart", [P, SEQ])
        z, e_neg, one_e = sb("ga_z", [P, GLA_T, SEQ]), sb("ga_e_neg", [P, SEQ]), sb("ga_one_e", [P, SEQ])
        b_cum = sb("ga_b_cum", [P, SEQ])
        grow = sb("ga_grow", [P, SEQ])
        k_end, q_dec, k_dec = sb("ga_k_end", [P, SEQ]), sb("ga_q_dec", [P, GLA_T, SEQ]), sb("ga_k_dec", [P, SEQ])
        decay = sb("ga_decay", [P, GLA_T, NCHUNK])
        v_n, k_n = sb("ga_v_n", [P, 2, GRP, P]), sb("ga_k_n", [P, 2, GRP, P])
        att = sb("ga_att", [P, 2, 2, GRP, P])
        state = sb("ga_state", [P, NCHUNK + 1, P])
        squares, rstd, o_norm = sb("ga_squares", [P, BLK]), sb("ga_rstd", [P, BLK]), sb("ga_o_norm", [P, BLK])
        eps = sb("ga_eps", [P, 1])
        z_ps = ps("ga_z_ps", [P, 4, BLK])
        att_ps, kv_ps = z_ps[:, 0:2], z_ps[:, 2:4]
        turn_ps, o_ps, mean_ps = ps("ga_turn_ps", [P, 2, BLK]), ps("ga_o_ps", [P, BLK]), ps("ga_mean_ps", [P, BLK])
        base, loaded, made, z_done, z_biased = sem("ga_base"), two("ga_loaded"), sem("ga_made"), sem("ga_z_done"), sem("ga_z_biased")
        silu_done, act_step, dve_step, cum_ready, turned, turn_read = sem("ga_silu_done"), sem("ga_act_step"), sem("ga_dve_step"), sem("ga_cum_ready"), sem("ga_turned"), sem("ga_turn_read")
        att_done, att_masked, kv_done, state_done, o_done = sem("ga_att_done"), sem("ga_att_masked"), sem("ga_kv_done"), sem("ga_state_done"), sem("ga_o_done")
        squared, mean_done, norm_act, o_normed, gated, stored = sem("ga_squared"), sem("ga_mean_done"), sem("ga_norm_act"), sem("ga_o_normed"), sem("ga_gated"), sem("ga_stored")
        chunks = lambda t: t.rearrange("p (c n) -> p c n", n=GLA_CHUNK)
        half = lambda h: slice(HEAD_DIM * h, HEAD_DIM * (h + 1))

        with nc.Block() as block:
            @block.sync
            def _(sp):
                sp.dma_start(glow[:], proj[T_MISC, 0:GLA_RANK]).then_inc(base, 16)
                sp.dma_start(w_a[:], w_alpha).then_inc(base, 16)
                sp.dma_start(ident[:], consts[:, C_IDENT * P:(C_IDENT + 1) * P]).then_inc(base, 16)
                sp.dma_start(head_ones[:], consts[:, C_HEAD * P:(C_HEAD + 1) * P]).then_inc(base, 16)
                sp.dma_start(mask[:], consts[:, C_CHUNK * P:(C_CHUNK + 1) * P]).then_inc(base, 16)
                for j in range(GLA_T):
                    for t0, tile in ((T_GK, gk), (T_GQ, gq), (T_GV, gv), (T_GG, gg)):
                        sp.dma_start(tile[:, j], proj[t0 + j]).then_inc(loaded[j], 16)
                for j in range(GLA_T):
                    sp.wait_ge(gated, NG * (j + 1))
                    sp.dma_start(mix[LRU_T + FOX_T + j], gg[:, j]).then_inc(stored, 16)
                sp.wait_ge(stored, 16 * GLA_T)

            @block.gpsimd
            def _(pool):
                nc.gpsimd.memset(restart[:], 1.0).then_inc(made, 1)
                pool.wait_ge(made, 1)
                nc.gpsimd.memset(chunks(restart[:])[:, :, 0:1], 0.0).then_inc(made, 1)
                pool.wait_ge(made, 2)
                nc.gpsimd.memset(att[:], 0.0).then_inc(made, 1)
                pool.wait_ge(made, 3)
                nc.gpsimd.memset(state[:], 0.0).then_inc(made, 1)
                pool.wait_ge(made, 4)
                nc.gpsimd.memset(eps[:], EPS).then_inc(made, 1)

            @block.scalar
            def _(act):
                act.wait_ge(made, 5)

                def gate(j):
                    act.wait_ge(loaded[j], 64)
                    nc.scalar.activation(gg[:, j], gg[:, j], ACT.Silu).then_inc(silu_done, 1)

                def exp_z(j):
                    act.wait_ge(z_biased, j + 1)
                    if j >= 1:
                        act.wait_ge(dve_step, 8 * j)
                    nc.scalar.activation(e_neg[:], z[:, j], ACT.Abs).then_inc(act_step, 1)
                    act.wait_ge(act_step, 7 * j + 1)
                    nc.scalar.activation(e_neg[:], e_neg[:], ACT.Exp, scale=-1.0).then_inc(act_step, 1)

                def ln_z(j):
                    act.wait_ge(dve_step, 8 * j + 1)
                    nc.scalar.activation(grow[:], one_e[:], ACT.Ln).then_inc(act_step, 1)

                def decays(j):
                    act.wait_ge(dve_step, 8 * j + 5)
                    nc.scalar.activation(z[:, j], one_e[:], ACT.Exp, scale=1.0 / GLA_TAU).then_inc(act_step, 1)
                    nc.scalar.activation(grow[:], b_cum[:], ACT.Exp, scale=-1.0 / GLA_TAU).then_inc(act_step, 1)
                    nc.scalar.activation(e_neg[:], b_cum[:], ACT.Exp, scale=1.0 / GLA_TAU).then_inc(act_step, 1)
                    nc.scalar.activation(decay[:, j], chunks(b_cum[:])[:, :, GLA_CHUNK - 1], ACT.Exp, scale=1.0 / GLA_TAU).then_inc(act_step, 1)

                def copy_turned(n):
                    act.wait_ge(turned, n + 1)
                    if n >= 2:
                        act.wait_ge(o_done, n - 1)
                    nc.scalar.activation(k_n[:, n % 2], turn_ps[:, 1].rearrange("p (t n) -> p t n", t=GRP), ACT.Copy)
                    nc.scalar.activation(v_n[:, n % 2], turn_ps[:, 0].rearrange("p (t n) -> p t n", t=GRP), ACT.Copy).then_inc(turn_read, 1)

                exp_z(0)
                ln_z(0)
                decays(0)
                copy_turned(0)
                gate(0)
                exp_z(1)
                gate(1)
                for n in range(ALL):
                    if n + 1 < ALL:
                        copy_turned(n + 1)
                    act.wait_ge(o_done, n + 1)
                    if n >= 1:
                        act.wait_ge(mean_done, n)
                    nc.scalar.activation(squares[:], o_ps[:], ACT.Square).then_inc(squared, 1)
                    act.wait_ge(mean_done, n + 1)
                    if n >= 1:
                        act.wait_ge(o_normed, n)
                    nc.scalar.activation(rstd[:], mean_ps[:], ACT.Ln, bias=eps[:]).then_inc(norm_act, 1)
                    act.wait_ge(norm_act, 2 * n + 1)
                    nc.scalar.activation(rstd[:], rstd[:], ACT.Exp, scale=-0.5).then_inc(norm_act, 1)
                    if n == 0:
                        ln_z(1)
                    if n == 1:
                        decays(1)

            @block.vector
            def _(dve):
                dve.wait_ge(made, 5)
                dve.wait_ge(base, 80)

                def bias(j):
                    dve.wait_ge(z_done, j + 1)
                    nc.vector.tensor_scalar(z[:, j], z_ps[:].rearrange("p b n -> p (b n)"), vec[:, VEC["b_alpha"] + j:VEC["b_alpha"] + j + 1], None, ALU.add).then_inc(z_biased, 1)

                def one_plus_e(j):
                    dve.wait_ge(act_step, 7 * j + 2)
                    nc.vector.tensor_scalar(one_e[:], e_neg[:], 1.0, None, ALU.add).then_inc(dve_step, 1)

                def cumulate(j):
                    dve.wait_ge(act_step, 7 * j + 3)
                    nc.vector.scalar_tensor_tensor(out=one_e[:], in0=one_e[:], scalar=-1.0, in1=e_neg[:], op0=ALU.add, op1=ALU.subtract).then_inc(dve_step, 1)
                    dve.wait_ge(dve_step, 8 * j + 2)
                    nc.vector.tensor_tensor(one_e[:], grow[:], one_e[:], ALU.subtract).then_inc(dve_step, 1)
                    dve.wait_ge(dve_step, 8 * j + 3)
                    nc.vector.scalar_tensor_tensor(out=e_neg[:], in0=z[:, j], scalar=0.0, in1=one_e[:], op0=ALU.min, op1=ALU.subtract).then_inc(dve_step, 1)
                    dve.wait_ge(dve_step, 8 * j + 4)
                    nc.vector.tensor_tensor_scan(b_cum[:], restart[:], e_neg[:], 0.0, ALU.mult, ALU.add).then_inc(cum_ready, 1)
                    dve.wait_ge(cum_ready, j + 1)
                    nc.vector.tensor_tensor(chunks(one_e[:]), chunks(b_cum[:])[:, :, GLA_CHUNK - 1:GLA_CHUNK].to_broadcast([P, NCHUNK, GLA_CHUNK]),
                                            chunks(b_cum[:]), ALU.subtract).then_inc(dve_step, 1)

                def decayed(j):
                    dve.wait_ge(act_step, 7 * j + 4)
                    dve.wait_ge(loaded[j], 64)
                    if j >= 1:
                        dve.wait_ge(turned, NG * j)
                        dve.wait_ge(att_done, 2 * NG * j)
                    nc.vector.tensor_tensor(k_end[:], gk[:, j], z[:, j], ALU.mult).then_inc(dve_step, 1)
                    dve.wait_ge(act_step, 7 * j + 5)
                    nc.vector.tensor_tensor(k_dec[:], gk[:, j], grow[:], ALU.mult).then_inc(dve_step, 1)
                    dve.wait_ge(act_step, 7 * j + 7)
                    nc.vector.scalar_tensor_tensor(out=q_dec[:, j], in0=gq[:, j], scalar=HEAD_DIM ** -0.5, in1=e_neg[:], op0=ALU.mult, op1=ALU.mult).then_inc(dve_step, 1)

                def mask_att(n):
                    for h in range(2):
                        dve.wait_ge(att_done, 2 * n + h + 1)
                        if h == 0 and n >= 2:
                            dve.wait_ge(o_done, n - 1)
                        nc.vector.copy_predicated(att[:, n % 2, h], mask[:, None, :].to_broadcast([P, GRP, P]).bitcast(U32),
                                                  att_ps[:, h].rearrange("p (t n) -> p t n", t=GRP)).then_inc(att_masked, 1)

                def states(n):
                    j, g = n // NG, n % NG
                    dve.wait_ge(kv_done, n + 1)
                    for c in range(CPG):
                        m = CPG * g + c
                        for h in range(2):
                            if m >= 1:
                                dve.wait_ge(state_done, 2 * NCHUNK * j + (2 * m + h - 1))
                            nc.vector.scalar_tensor_tensor(out=state[half(h), m + 1, half(h)], in0=state[half(h), m, half(h)], scalar=decay[half(h), j, m:m + 1],
                                                           in1=kv_ps[half(h), c % 2, (c // 2) * P + HEAD_DIM * h:(c // 2) * P + HEAD_DIM * (h + 1)],
                                                           op0=ALU.mult, op1=ALU.add).then_inc(state_done, 1)

                def finish(n):
                    j, g = n // NG, n % NG
                    dve.wait_ge(norm_act, 2 * n + 2)
                    dve.wait_ge(silu_done, j + 1)
                    if n >= 1:
                        dve.wait_ge(gated, n)
                    nc.vector.scalar_tensor_tensor(out=o_norm[:], in0=o_ps[:], scalar=vec[:, VEC["out_gain"]:VEC["out_gain"] + 1], in1=rstd[:],
                                                   op0=ALU.mult, op1=ALU.mult).then_inc(o_normed, 1)
                    dve.wait_ge(o_normed, n + 1)
                    cols = slice(g * BLK, (g + 1) * BLK)
                    nc.vector.tensor_tensor(gg[:, j, cols], o_norm[:], gg[:, j, cols], ALU.mult).then_inc(gated, 1)

                for j in range(GLA_T):
                    bias(j)
                one_plus_e(0)
                cumulate(0)
                decayed(0)
                mask_att(0)
                states(0)
                for n in range(ALL):
                    if n + 1 == NG:
                        decayed(1)
                    if n + 1 < ALL:
                        mask_att(n + 1)
                        states(n + 1)
                    finish(n)
                    if n == 0:
                        one_plus_e(1)
                    if n == 1:
                        cumulate(1)

            @block.tensor
            def _(pe):
                pe.wait_ge(base, 80)
                pe.wait_ge(made, 5)
                for j in range(GLA_T):
                    if j >= 1:
                        pe.wait_ge(z_biased, j)
                    for b in range(NBLK):
                        last = nc.tensor.matmul(z_ps[:, b], w_a[:, j * P:(j + 1) * P], glow[:, b * BLK:(b + 1) * BLK], start=True, stop=True)
                    last.then_inc(z_done, 1)

                def turn(n):
                    j, g = n // NG, n % NG
                    if g == 0:
                        pe.wait_ge(loaded[j], 64)
                        pe.wait_ge(dve_step, 8 * j + 8)
                    if n >= 1:
                        pe.wait_ge(turn_read, n)
                    for w, src in ((0, gv[:, j]), (1, k_end[:])):
                        for t in range(GRP):
                            o = (GRP * g + t) * P
                            last = nc.tensor.transpose(turn_ps[:, w, t * P:(t + 1) * P], src[:, o:o + P], ident[:])
                    last.then_inc(turned, 1)

                def attend(n):
                    j, g = n // NG, n % NG
                    if n >= 1:
                        pe.wait_ge(att_masked, 2 * n)
                    for h in range(2):
                        for t in range(GRP):
                            o = (GRP * g + t) * P
                            last = nc.tensor.matmul(att_ps[:, h, t * P:(t + 1) * P], k_dec[half(h), o:o + P], q_dec[half(h), j, o:o + P], start=True, stop=True)
                        last.then_inc(att_done, 1)

                def products_kv(n):
                    pe.wait_ge(turn_read, n + 1)
                    if n >= 1:
                        pe.wait_ge(state_done, 2 * CPG * n)
                    for c in range(CPG):
                        rows = slice(GLA_CHUNK * (c % 2), GLA_CHUNK * (c % 2 + 1))
                        last = nc.tensor.matmul(kv_ps[:, c % 2, (c // 2) * P:(c // 2 + 1) * P], k_n[rows, n % 2, c // 2], v_n[rows, n % 2, c // 2], start=True, stop=True)
                    last.then_inc(kv_done, 1)

                def outputs(n):
                    j, g = n // NG, n % NG
                    pe.wait_ge(att_masked, 2 * n + 2)
                    pe.wait_ge(state_done, 2 * CPG * (n + 1))
                    if n >= 1:
                        pe.wait_ge(o_normed, n)
                    for t in range(GRP):
                        for c in range(2):
                            m = CPG * g + 2 * t + c
                            nc.tensor.matmul(o_ps[:, (2 * t + c) * GLA_CHUNK:(2 * t + c + 1) * GLA_CHUNK], state[:, m], q_dec[:, j, m * GLA_CHUNK:(m + 1) * GLA_CHUNK],
                                             start=(t == 0 and c == 0), stop=False, skip_group_check=True)
                        for h in range(2):
                            last = nc.tensor.matmul(o_ps[half(h), t * P:(t + 1) * P], v_n[:, n % 2, t, half(h)], att[:, n % 2, h, t], start=False, stop=True, skip_group_check=True)
                    last.then_inc(o_done, 1)

                pe.wait_ge(z_biased, GLA_T)
                turn(0)
                attend(0)
                products_kv(0)
                for n in range(ALL):
                    if n + 1 < ALL:
                        turn(n + 1)
                        attend(n + 1)
                        products_kv(n + 1)
                    outputs(n)
                    pe.wait_ge(squared, n + 1)
                    nc.tensor.matmul(mean_ps[:], head_ones[:], squares[:], start=True, stop=True).then_inc(mean_done, 1)


def project_out(nc, vec, mod, mean_rstd, xT, w_out, consts, mix, x2):
    with ExitStack() as ctx:
        sb = lambda n, s, d=F32: ctx.enter_context(nc.sbuf_tensor(n, s, d))
        ps = lambda n, s, d=F32: ctx.enter_context(nc.psum_tensor(n, s, d))
        sem = lambda n: ctx.enter_context(nc.semaphore(n))
        two = lambda n: [sem(n + "_even"), sem(n + "_odd")]
        m_hi, m_lo = sb("po_m_hi", [P, KD, SEQ], F32R), sb("po_m_lo", [P, KD, SEQ], F32R)
        slot = sb("po_slot", [P, 2, SEQ])
        w_raw = sb("po_w_raw", [P, 2, KD * P])
        w_hi, w_lo = sb("po_w_hi", [P, 2, KD, P], F32R), sb("po_w_lo", [P, 2, KD, P], F32R)
        squares = sb("po_squares", [P, SEQ])
        sq_sum = mean_rstd
        mean_ones, eps = sb("po_mean_ones", [P, P]), sb("po_eps", [P, 1])
        banks = ps("po_banks", [P, 8, BLK])
        flat = lambda t: t.rearrange("p k n -> p (k n)")
        in_consts, made, mix_in, mix_hi, mix_lo = sem("po_in_consts"), sem("po_made"), two("po_mix_in"), sem("po_mix_hi"), sem("po_mix_lo")
        w_in, hi_ready, lo_ready, x_in = two("po_w_in"), sem("po_hi_ready"), sem("po_lo_ready"), two("po_x_in")
        tile_done, x2_ready, stored, squared, added = sem("po_tile_done"), sem("po_x2_ready"), two("po_stored"), sem("po_squared"), sem("po_added")
        mean_done, rms_ready = sem("po_mean_done"), sem("po_rms_ready")

        with nc.Block() as block:
            @block.sync
            def _(sp):
                sp.dma_start(mean_ones[:], consts[:, C_MEAN * P:(C_MEAN + 1) * P]).then_inc(in_consts, 16)
                for k in range(KD):
                    if k >= 2:
                        sp.wait_ge(mix_lo, k - 1)
                    sp.dma_start(slot[:, k % 2], mix[k]).then_inc(mix_in[k % 2], 16)
                    if k < 2:
                        sp.dma_start(w_raw[:, k], w_out[k]).then_inc(w_in[k], 16)
                sp.wait_ge(mix_lo, KD)
                for m in range(2):
                    sp.dma_start(slot[:, m], xT[:, m]).then_inc(x_in[m], 16)
                with sp.Fori(1, KD // 2) as i:
                    for s in range(2):
                        sp.wait_ge(lo_ready, 2 * i + (s - 1))
                        sp.dma_start(w_raw[:, s], w_out[bass.ds(2 * i + s, 1)].rearrange("o p n -> (o p) n")).then_inc(w_in[s], 16)
                    for s in range(2):
                        sp.wait_ge(stored[s], 16 * i)
                        sp.wait_ge(squared, 2 * i + (s - 1))
                        sp.dma_start(slot[:, s], xT[:, bass.ds(2 * i + s, 1)].rearrange("p o n -> p (o n)")).then_inc(x_in[s], 16)

            @block.gpsimd
            def _(pool):
                nc.gpsimd.memset(eps[:], EPS).then_inc(made, 1)
                pool.wait_ge(made, 1)
                nc.gpsimd.memset(sq_sum[:], 0.0).then_inc(made, 1)
                pool.wait_ge(made, 2)
                for m in range(2):
                    pool.wait_ge(hi_ready, m + 1)
                    nc.gpsimd.tensor_tensor(flat(w_lo[:, m]), w_raw[:, m], flat(w_hi[:, m]).bitcast(F32), ALU.subtract).then_inc(lo_ready, 1)
                with pool.Fori(1, KD // 2) as i:
                    for s in range(2):
                        pool.wait_ge(hi_ready, 2 * i + (s + 1))
                        nc.gpsimd.tensor_tensor(flat(w_lo[:, s]), w_raw[:, s], flat(w_hi[:, s]).bitcast(F32), ALU.subtract).then_inc(lo_ready, 1)
                        pool.wait_ge(squared, 2 * i + (s - 1))
                        nc.gpsimd.tensor_tensor(sq_sum[:], sq_sum[:], squares[:], ALU.add).then_inc(added, 1)
                        pool.wait_ge(added, 2 * i + s)
                for m in (KD - 2, KD - 1):
                    pool.wait_ge(squared, m + 1)
                    nc.gpsimd.tensor_tensor(sq_sum[:], sq_sum[:], squares[:], ALU.add).then_inc(added, 1)
                    pool.wait_ge(added, m + 2)

            @block.scalar
            def _(act):
                act.sem_inc(added, 1)
                for k in range(KD):
                    act.wait_ge(mix_in[k % 2], 16 * (k // 2 + 1))
                    nc.scalar.activation(m_hi[:, k], slot[:, k % 2], ACT.Copy).then_inc(mix_hi, 1)
                    if k < 2:
                        act.wait_ge(w_in[k], 16)
                        nc.scalar.activation(flat(w_hi[:, k]), w_raw[:, k], ACT.Copy).then_inc(hi_ready, 1)
                with act.Fori(1, KD // 2) as i:
                    for s in range(2):
                        act.wait_ge(w_in[s], 16 * i + 16)
                        act.wait_ge(tile_done, 2 * i + (s - 1))
                        nc.scalar.activation(flat(w_hi[:, s]), w_raw[:, s], ACT.Copy).then_inc(hi_ready, 1)
                        act.wait_ge(x2_ready, 2 * i + (s + 1))
                        act.dma_start(x2[bass.ds(2 * i + (s - 2), 1)].rearrange("o p n -> (o p) n"), slot[:, s]).then_inc(stored[s], 16)
                        act.wait_ge(added, 2 * i + (s - 1))
                        nc.scalar.activation(squares[:], slot[:, s], ACT.Square).then_inc(squared, 1)
                for m in (KD - 2, KD - 1):
                    act.wait_ge(x2_ready, m + 3)
                    act.dma_start(x2[m], slot[:, m % 2]).then_inc(stored[m % 2], 16)
                    act.wait_ge(added, m + 1)
                    nc.scalar.activation(squares[:], slot[:, m % 2], ACT.Square).then_inc(squared, 1)
                for b in range(NBLK):
                    act.wait_ge(mean_done, b + 1)
                    nc.scalar.activation(mean_rstd[:, b * BLK:(b + 1) * BLK], banks[:, b], ACT.Sqrt, bias=eps[:]).then_inc(rms_ready, 1)
                for s in range(2):
                    act.wait_ge(stored[s], 16 * (KD // 2))

            @block.vector
            def _(dve):
                for k in range(KD):
                    dve.wait_ge(mix_hi, k + 1)
                    nc.vector.tensor_tensor(m_lo[:, k], slot[:, k % 2], m_hi[:, k].bitcast(F32), ALU.subtract).then_inc(mix_lo, 1)
                with dve.Fori(0, KD // 2) as i:
                    for s in range(2):
                        dve.wait_ge(tile_done, 2 * i + (s + 1))
                        dve.wait_ge(x_in[s], 16 * i + 16)
                        nc.vector.scalar_tensor_tensor(out=slot[:, s], in0=banks[:, 4 * s:4 * s + 4].rearrange("p b n -> p (b n)"),
                                                       scalar=mod[:, bass.ds(2 * i + (s + GATE1), 1)], in1=slot[:, s],
                                                       op0=ALU.mult, op1=ALU.add).then_inc(x2_ready, 1)
                for b in range(NBLK):
                    dve.wait_ge(rms_ready, b + 1)
                    cols = slice(b * BLK, (b + 1) * BLK)
                    nc.vector.reciprocal(mean_rstd[:, cols], mean_rstd[:, cols])

            @block.tensor
            def _(pe):
                pe.sem_inc(x2_ready, 2)
                pe.wait_ge(in_consts, 16)
                pe.wait_ge(made, 2)
                with pe.Fori(0, KD // 2) as i:
                    for s in range(2):
                        pe.wait_ge(lo_ready, 2 * i + (s + 1))
                        pe.wait_ge(x2_ready, 2 * i + (s + 1))
                        for k in range(KD):
                            pe.wait_ge(mix_lo, k + 1)
                            for b in range(NBLK):
                                cols = slice(b * BLK, (b + 1) * BLK)
                                last = split_products(nc, banks[:, 4 * s + b], w_hi[:, s, k], w_lo[:, s, k], m_hi[:, k, cols], m_lo[:, k, cols],
                                                      k == 0, k == KD - 1)
                        last.then_inc(tile_done, 1)
                pe.wait_ge(added, KD + 1)
                pe.wait_ge(x2_ready, KD + 2)
                for b in range(NBLK):
                    nc.tensor.matmul(banks[:, b], mean_ones[:], sq_sum[:, b * BLK:(b + 1) * BLK], start=True, stop=True).then_inc(mean_done, 1)


def feed_forward(nc, vec, mod, mean_rstd, w_gate_up, w_down, x2, yT):
    UP, DOWN = KF, 2 * KD
    UNITS = UP + DOWN
    HALF = KF // 2
    KHALVES = range(0, KD // 2), range(KD // 2, KD)
    with ExitStack() as ctx:
        sb = lambda n, s, d=F32: ctx.enter_context(nc.sbuf_tensor(n, s, d))
        ps = lambda n, s, d=F32: ctx.enter_context(nc.psum_tensor(n, s, d))
        sem = lambda n: ctx.enter_context(nc.semaphore(n))
        two = lambda n: [sem(n + "_even"), sem(n + "_odd")]
        h_hi, h_lo = sb("ff_h_hi", [P, KD, BLK], F32R), sb("ff_h_lo", [P, KD, BLK], F32R)
        a_hi, a_lo = sb("ff_a_hi", [P, KF, BLK], F32R), sb("ff_a_lo", [P, KF, BLK], F32R)
        x_blk = sb("ff_x_blk", [P, KD, BLK])
        w_raw = sb("ff_w_raw", [P, 2, 2 * KD * P])
        w_hi, w_lo = sb("ff_w_hi", [P, 2, 2 * KD * P], F32R), sb("ff_w_lo", [P, 2, 2 * KD * P], F32R)
        silu, gated = sb("ff_silu", [P, 2, BLK]), sb("ff_gated", [P, 2, BLK])
        x_res = sb("ff_x_res", [P, 2, BLK])
        y_out = gated
        scale_a = sb("ff_scale_a", [P, KD])
        g_ps, u_ps, d_ps = ps("ff_g_ps", [P, 2, BLK]), ps("ff_u_ps", [P, 2, BLK]), ps("ff_d_ps", [P, 2, BLK])
        up_w = lambda w, s: w[:, s].rearrange("p (g k n) -> p g k n", g=2, k=KD)
        down_w = lambda w, s: w[:, s, 0:HALF * P].rearrange("p (k n) -> p k n", k=HALF)
        size = lambda up: slice(0, 2 * KD * P) if up else slice(0, HALF * P)

        x_in, scaled, xn_ready, h_hi_ready, h_full, h_ready = sem("ff_x_in"), sem("ff_scaled"), sem("ff_xn_ready"), sem("ff_h_hi_ready"), sem("ff_h_full"), sem("ff_h_ready")
        w_in, hi_ready, lo_ready, unit_done = two("ff_w_in"), sem("ff_hi_ready"), sem("ff_lo_ready"), sem("ff_unit_done")
        silu_ready, gated_ready, a_hi_ready, a_ready = sem("ff_silu_ready"), sem("ff_gated_ready"), sem("ff_a_hi_ready"), sem("ff_a_ready")
        res_in, y_ready, stored = two("ff_res_in"), sem("ff_y_ready"), two("ff_stored")

        with nc.Block() as block:
            @block.sync
            def _(sp):
                sp.wait_ge(x_in, 16)
                with sp.Fori(0, NBLK) as t:
                    with sp.Fori(0, UP // 2) as i:
                        for s in range(2):
                            sp.wait_ge(lo_ready, UNITS * t + 2 * i + (s + 1))
                            sp.dma_start(w_raw[:, s], w_gate_up[bass.ds(2 * i + s, 1)].rearrange("o p n -> (o p) n")).then_inc(w_in[s], 16)
                    with sp.Fori(0, DOWN // 2) as i:
                        for s in range(2):
                            sp.wait_ge(lo_ready, UNITS * t + 2 * i + (UP + s + 1))
                            sp.dma_start(w_raw[:, s, size(False)], w_down[bass.ds(2 * i + s, 1)].rearrange("o p n -> (o p) n")).then_inc(w_in[s], 16)

            @block.gpsimd
            def _(pool):
                pool.sem_inc(lo_ready, 2)
                def low(up, s):
                    nc.gpsimd.tensor_tensor(w_lo[:, s, size(up)], w_raw[:, s, size(up)], w_hi[:, s, size(up)].bitcast(F32), ALU.subtract).then_inc(lo_ready, 1)
                with pool.Fori(0, NBLK) as t:
                    with pool.Fori(0, UP // 2) as i:
                        for s in range(2):
                            pool.wait_ge(hi_ready, UNITS * t + 2 * i + (s + 1))
                            low(True, s)
                    with pool.Fori(0, DOWN // 2) as i:
                        for s in range(2):
                            pool.wait_ge(hi_ready, UNITS * t + 2 * i + (UP + s + 1))
                            low(False, s)

            @block.scalar
            def _(act):
                def norm(t):
                    for w, ks in enumerate(KHALVES):
                        act.wait_ge(xn_ready, 2 * t + w + 1)
                        if t >= 1:
                            act.wait_ge(unit_done, UNITS * (t - 1) + UP + 2)
                        for k in ks:
                            last = nc.scalar.activation(h_hi[:, k], x_blk[:, k], ACT.Identity, bias=mod[:, SHIFT2 + k:SHIFT2 + k + 1], scale=scale_a[:, k:k + 1])
                        last.then_inc(h_hi_ready, 1)

                def load_block(t):
                    act.dma_start(x_blk[:], x2[:, :, t * BLK:(t + 1) * BLK].rearrange("k p n -> p k n")).then_inc(x_in, 16)

                def high(t, up, i, s, n):
                    act.wait_ge(w_in[s], 16 * (UNITS // 2) * t + 16 * i + (16 if up else 16 * (UP // 2) + 16))
                    act.wait_ge(unit_done, UNITS * t + n + 1)
                    nc.scalar.activation(w_hi[:, s, size(up)], w_raw[:, s, size(up)], ACT.Copy).then_inc(hi_ready, 1)

                def gate(t, s, n):
                    act.wait_ge(unit_done, UNITS * t + n + 3)
                    act.wait_ge(gated_ready, UP * t + n + 1)
                    nc.scalar.activation(silu[:, s], g_ps[:, s], ACT.Silu).then_inc(silu_ready, 1)

                def act_high(t, s, n, at):
                    act.wait_ge(gated_ready, UP * t + n + 3)
                    nc.scalar.activation(a_hi[:, at].rearrange("p o n -> p (o n)"), gated[:, s], ACT.Copy).then_inc(a_hi_ready, 1)

                def load_res(t, m, s):
                    act.dma_start(x_res[:, s], x2[m, :, t * BLK:(t + 1) * BLK].rearrange("o p n -> (o p) n")).then_inc(res_in[s], 16)

                def store(t, m, at, s):
                    act.wait_ge(y_ready, KD * t + m + 3)
                    act.dma_start(yT[at, :, t * BLK:(t + 1) * BLK].rearrange("o p n -> (o p) n"), y_out[:, s]).then_inc(stored[s], 16)

                for s in range(2):
                    act.sem_inc(stored[s], 16)
                load_block(0)
                norm(0)
                for s in range(2):
                    load_res(0, slice(s, s + 1), s)
                for t in range(NBLK):
                    for s in range(2):
                        high(t, True, 0, s, s)
                    if t + 1 < NBLK:
                        act.wait_ge(h_ready, 2 * t + 2)
                        load_block(t + 1)
                    if t >= 1:
                        store(t - 1, KD - 1, slice(KD - 1, KD), 1)
                        load_res(t, slice(1, 2), 1)
                    with act.Fori(1, UP // 2) as i:
                        for s in range(2):
                            gate(t, s, 2 * i + (s - 2))
                            high(t, True, i, s, 2 * i + s)
                            act_high(t, s, 2 * i + (s - 2), bass.ds(2 * i + (s - 2), 1))
                    for s in range(2):
                        gate(t, s, UP - 2 + s)
                        high(t, False, 0, s, UP + s)
                        act_high(t, s, UP - 2 + s, slice(UP - 2 + s, UP - 1 + s))
                    if t + 1 < NBLK:
                        norm(t + 1)
                    with act.Fori(0, KD // 2 - 1) as i:
                        for o in range(2):
                            for s in range(2):
                                high(t, False, 2 * i + (1 + o), s, 4 * i + (UP + 2 + 2 * o + s))
                            store(t, 2 * i + o, bass.ds(2 * i + o, 1), o)
                            load_res(t, bass.ds(2 * i + (o + 2), 1), o)
                    for s in range(2):
                        high(t, False, KD - 1, s, UP + DOWN - 2 + s)
                    store(t, KD - 2, slice(KD - 2, KD - 1), 0)
                    if t + 1 < NBLK:
                        load_res(t + 1, slice(0, 1), 0)
                store(NBLK - 1, KD - 1, slice(KD - 1, KD), 1)
                for s in range(2):
                    act.wait_ge(stored[s], 16 + 16 * NBLK * (KD // 2))

            @block.vector
            def _(dve):
                dve.sem_inc(gated_ready, 2)
                nc.vector.scalar_tensor_tensor(out=scale_a[:], in0=mod[:, SCALE2:SCALE2 + KD], scalar=1.0, in1=vec[:, VEC["g2"]:VEC["g2"] + KD],
                                               op0=ALU.add, op1=ALU.mult).then_inc(scaled, 1)
                dve.wait_ge(scaled, 1)

                def scale(t):
                    dve.wait_ge(x_in, 16 * (t + 1))
                    for ks in KHALVES:
                        at = slice(ks[0], ks[-1] + 1)
                        nc.vector.tensor_tensor(x_blk[:, at], x_blk[:, at], mean_rstd[:, None, t * BLK:(t + 1) * BLK].to_broadcast([P, len(ks), BLK]), ALU.mult).then_inc(xn_ready, 1)

                def norm(t):
                    for w, ks in enumerate(KHALVES):
                        at = slice(ks[0], ks[-1] + 1)
                        dve.wait_ge(h_hi_ready, 2 * t + w + 1)
                        for k in ks:
                            last = nc.vector.tensor_scalar(x_blk[:, k], x_blk[:, k], scale_a[:, k:k + 1], mod[:, SHIFT2 + k:SHIFT2 + k + 1], ALU.mult, ALU.add)
                        last.then_inc(h_full, 1)
                        dve.wait_ge(h_full, 2 * t + w + 1)
                        nc.vector.tensor_tensor(h_lo[:, at], x_blk[:, at], h_hi[:, at].bitcast(F32), ALU.subtract).then_inc(h_ready, 1)

                scale(0)
                norm(0)
                for t in range(NBLK):
                    for s in range(2):
                        dve.wait_ge(stored[s], 16 * (KD // 2) * t + 16)
                    if t + 1 < NBLK:
                        scale(t + 1)
                    with dve.Fori(0, UP // 2) as i:
                        for s in range(2):
                            n = 2 * i + s
                            dve.wait_ge(silu_ready, UP * t + n + 1)
                            dve.wait_ge(a_ready, UP * t + n + 1)
                            nc.vector.tensor_tensor(gated[:, s], silu[:, s], u_ps[:, s], ALU.mult).then_inc(gated_ready, 1)
                            dve.wait_ge(a_hi_ready, UP * t + n + 1)
                            nc.vector.tensor_tensor(a_lo[:, bass.ds(n, 1)].rearrange("p o n -> p (o n)"), gated[:, s],
                                                    a_hi[:, bass.ds(n, 1)].rearrange("p o n -> p (o n)").bitcast(F32), ALU.subtract).then_inc(a_ready, 1)
                    if t + 1 < NBLK:
                        norm(t + 1)
                    with dve.Fori(0, KD // 2) as i:
                        for s in range(2):
                            dve.wait_ge(unit_done, UNITS * t + 4 * i + (UP + 2 * s + 4))
                            dve.wait_ge(res_in[s], 16 * (KD // 2) * t + 16 * i + 16)
                            dve.wait_ge(stored[s], 16 * (KD // 2) * t + 16 * i + 16)
                            nc.vector.scalar_tensor_tensor(out=y_out[:, s], in0=d_ps[:, s], scalar=mod[:, bass.ds(2 * i + (s + GATE2), 1)], in1=x_res[:, s],
                                                           op0=ALU.mult, op1=ALU.add).then_inc(y_ready, 1)

            @block.tensor
            def _(pe):
                pe.sem_inc(unit_done, 2)
                pe.sem_inc(a_ready, 2)
                pe.sem_inc(y_ready, 2)
                for t in range(NBLK):
                    pe.wait_ge(h_ready, 2 * t + 2)
                    with pe.Fori(0, UP // 2) as i:
                        for s in range(2):
                            n = 2 * i + s
                            pe.wait_ge(lo_ready, UNITS * t + n + 3)
                            pe.wait_ge(a_ready, UP * t + n + 1)
                            for g, out in ((0, g_ps[:, s]), (1, u_ps[:, s])):
                                for k in range(KD):
                                    last = split_products(nc, out, up_w(w_hi, s)[:, g, k], up_w(w_lo, s)[:, g, k], h_hi[:, k], h_lo[:, k], k == 0, k == KD - 1)
                            last.then_inc(unit_done, 1)
                    with pe.Fori(0, KD // 2) as i:
                        for m in range(2):
                            pe.wait_ge(y_ready, KD * t + 2 * i + (m + 1))
                            for s in range(2):
                                pe.wait_ge(lo_ready, UNITS * t + 4 * i + (UP + 2 * m + s + 3))
                                if s == 1:
                                    pe.wait_ge(a_ready, UP * (t + 1) + 2)
                                for k in range(HALF):
                                    f = HALF * s + k
                                    last = split_products(nc, d_ps[:, m], down_w(w_hi, s)[:, k], down_w(w_lo, s)[:, k], a_hi[:, f], a_lo[:, f], f == 0, f == KF - 1)
                                last.then_inc(unit_done, 1)


def lay_out(inputs):
    a = {k: np.asarray(v) for k, v in inputs.items()}
    f32 = np.float32
    cols = lambda v, n: v.reshape(n, P).T
    w_in = a["w_in"][0]
    cut = np.cumsum([LRU_WIDTH, LRU_WIDTH, FOX_T * P, FOX_T * P, FOX_T * P, FOX_HEADS, GLA_T * P, GLA_T * P, GLA_T * P, GLA_RANK, GLA_T * P])
    xa, ya, fq, fk, fv, ff, gq, gk, gv, glow, gg = np.split(w_in, cut[:-1], axis=1)
    misc = np.zeros((D_MODEL, P), f32)
    misc[:, 0:GLA_RANK] = glow
    misc[:, FF_ROW:FF_ROW + FOX_HEADS] = ff
    w_in = np.concatenate([xa, ya, fq, fk, fv, gq, gk, gv, gg, misc], axis=1)
    tiles = lambda w, kt, mt: np.ascontiguousarray(w.reshape(kt, P, mt, -1).transpose(2, 1, 0, 3))
    blocks = np.zeros((2, LRU_T, P, P), f32)
    for g, name in enumerate(("lru_w_r", "lru_w_i")):
        for n in range(LRU_WIDTH // HEAD_DIM):
            o = HEAD_DIM * (n % 2)
            blocks[g, n // 2, o:o + HEAD_DIM, o:o + HEAD_DIM] = a[name][0, n]
    b_f = np.zeros((P, 1), f32)
    b_f[FF_ROW:FF_ROW + FOX_HEADS, 0] = a["fox_b_f"][0]
    twice = lambda v: np.concatenate([v, v]).reshape(P, 1)
    parts = {
        "c": cols(a["c"][0], KD), "g1": cols(a["norm1_gain"][0], KD), "g2": cols(a["norm2_gain"][0], KD),
        "b_mod": cols(a["b_mod"][0], 6 * KD), "conv_w": np.concatenate([cols(w, LRU_T) for w in a["conv_w"][0]], axis=1),
        "conv_b": cols(a["conv_b"][0], LRU_T), "b_r": cols(a["lru_b_r"][0], LRU_T), "b_i": cols(a["lru_b_i"][0], LRU_T),
        "lam": cols(a["lru_lambda"][0], LRU_T), "q_gain": twice(a["fox_q_gain"][0]), "k_gain": twice(a["fox_k_gain"][0]),
        "b_alpha": cols(a["gla_b_alpha"][0], GLA_T), "out_gain": twice(a["gla_out_gain"][0]), "b_f": b_f,
    }
    gate_up = a["ffn_w_gate_up"][0].reshape(KD, P, 2, KF, P).transpose(3, 1, 2, 0, 4)
    down = a["ffn_w_down"][0].reshape(2, KF // 2, P, KD, P).transpose(3, 0, 2, 1, 4)
    p, q = np.arange(P)[:, None], np.arange(P)[None, :]
    same_head = p // HEAD_DIM == q // HEAD_DIM
    consts = np.concatenate([
        np.full((P, P), 1.0 / D_MODEL), same_head / HEAD_DIM, p == q,
        np.where(q <= p, 0.0, MASKED),
        np.where(p <= q, 0.0, MASKED),
        same_head & (p <= q),
    ], axis=1).astype(f32)
    tiles6 = 2 * FOX_T
    head_of = 2 * np.arange(tiles6)[None, :] + np.arange(P)[:, None] // HEAD_DIM
    one_hot = head_of[:, :, None] == np.arange(2 * FOX_HEADS)
    fox_rows = np.zeros((P, tiles6 * 2 * FOX_HEADS + tiles6 * P), f32)
    fox_rows[:, :tiles6 * 2 * FOX_HEADS] = (one_hot / HEAD_DIM).reshape(P, -1)
    fox_rows[:2 * FOX_HEADS, tiles6 * 2 * FOX_HEADS:] = one_hot.transpose(2, 1, 0).reshape(2 * FOX_HEADS, -1)
    return {
        "xT": np.ascontiguousarray(a["x"][0].T).reshape(KD, P, SEQ),
        "vec": np.ascontiguousarray(np.concatenate([parts[k] for k in VEC], axis=1)),
        "w_mod": tiles(a["w_mod"][0], KD, MOD_CHUNKS),
        "w_in": tiles(w_in, KD, N_PROJ).reshape(N_PROJ, P, KD * P),
        "w_gates": blocks,
        "w_alpha": np.ascontiguousarray(a["gla_w_alpha"][0]),
        "w_out": tiles(a["w_out"][0], KD, KD).reshape(KD, P, KD * P),
        "w_gate_up": np.ascontiguousarray(gate_up).reshape(KF, P, 2 * KD * P),
        "w_down": np.ascontiguousarray(down).reshape(2 * KD, P, (KF // 2) * P),
        "consts": consts,
        "fox_rows": fox_rows,
    }


def build(nc, xT, vec_in, w_mod, w_in, w_gates, w_alpha, w_out, w_gate_up, w_down, consts, fox_rows, yT):
    proj = nc.dram_tensor("proj_dram", [N_PROJ, P, SEQ], F32).ap()
    xT = xT.rearrange("k p n -> p k n")
    with ExitStack() as ctx:
        vec = ctx.enter_context(nc.sbuf_tensor("vec", [P, N_VEC], F32))
        mod = ctx.enter_context(nc.sbuf_tensor("mod", [P, 6 * KD], F32))
        mix = nc.dram_tensor("mix_dram", [MIX_T, P, SEQ], F32).ap()
        project_in_and_recur(nc, vec, mod, xT, w_mod, w_in, w_gates, consts, vec_in, proj, mix)
        x2 = nc.dram_tensor("x2_dram", [KD, P, SEQ], F32).ap()
        q_split = nc.dram_tensor("q_split_dram", [FOX_HEADS, 2, HEAD_DIM, SEQ], F32).ap()
        k_split = nc.dram_tensor("k_split_dram", [FOX_HEADS, 2, HEAD_DIM, SEQ], F32).ap()
        bias_split = nc.dram_tensor("bias_split_dram", [FOX_HEADS, 2, SEQ], F32).ap()
        v_split = nc.dram_tensor("v_split_dram", [FOX_HEADS, P, SEQ // P * 3 * HEAD_DIM], F32).ap()
        fox_operands(nc, vec, consts, fox_rows, proj, q_split, k_split, bias_split, v_split)
        forgetting_attention(nc, consts, q_split, k_split, bias_split, v_split, mix)
        gated_linear_attention(nc, vec, consts, w_alpha, proj, mix)
        mean_rstd = ctx.enter_context(nc.sbuf_tensor("mean_rstd", [P, SEQ], F32))
        project_out(nc, vec, mod, mean_rstd, xT, w_out, consts, mix, x2)
        feed_forward(nc, vec, mod, mean_rstd, w_gate_up, w_down, x2, yT)


def kernel(**inputs):
    import concourse.bacc as _bacc
    from concourse.bass_utils import run_bass_kernel_spmd as _run

    arrays = lay_out(inputs)
    nc = _bacc.Bacc("TRN2", target_bir_lowering=False, num_devices=1)
    args = [nc.dram_tensor(f"in_{name}", a.shape, mybir.dt.from_np(a.dtype), kind="ExternalInput").ap() for name, a in arrays.items()]
    args.append(nc.dram_tensor("out_yT", (KD, P, SEQ), F32, kind="ExternalOutput").ap())
    build(nc, *args)
    r = _run(nc, [{f"in_{name}": a for name, a in arrays.items()}], core_ids=[0])
    y = np.asarray(r.results[0]["out_yT"])
    return np.ascontiguousarray(y.reshape(D_MODEL, SEQ).T).reshape(1, SEQ, D_MODEL)
```

```python
from contextlib import ExitStack

import numpy as np

import concourse.bass as bass
from concourse import mybir

F32 = mybir.dt.float32
F32R = mybir.dt.float32r
U32 = mybir.dt.uint32
ALU = mybir.AluOpType
ACT = mybir.ActivationFunctionType
AX = mybir.AxisListType

P = 128
D_MODEL = 1024
SEQ = 2048
EPS = 1e-6
HEAD_DIM = 64
LRU_WIDTH = 384
CONV_WIDTH = 4
LRU_C = 8.0
FOX_HEADS = 6
GLA_HEADS = 4
GLA_RANK = 16
GLA_TAU = 16.0
GLA_CHUNK = 64
D_FF = 2816

KD = D_MODEL // P
KF = D_FF // P
BLK = 512
NBLK = SEQ // BLK
LRU_T = LRU_WIDTH // P
FOX_T = FOX_HEADS * HEAD_DIM // P
GLA_T = GLA_HEADS * HEAD_DIM // P
T_XA, T_YA = 0, LRU_T
T_FQ = T_YA + LRU_T
T_FK, T_FV = T_FQ + FOX_T, T_FQ + 2 * FOX_T
T_GQ = T_FV + FOX_T
T_GK, T_GV, T_GG = T_GQ + GLA_T, T_GQ + 2 * GLA_T, T_GQ + 3 * GLA_T
T_MISC = T_GG + GLA_T
N_PROJ = T_MISC + 1
FF_ROW = 32
MIX_T = LRU_T + FOX_T + GLA_T
MASKED = -1.0e30

C_MEAN, C_HEAD, C_IDENT, C_CAUSAL, C_CAUSAL_T, C_CHUNK = range(6)

VEC = {}
_at = 0
for _name, _n in (("c", KD), ("g1", KD), ("g2", KD), ("b_mod", 6 * KD), ("conv_w", CONV_WIDTH * LRU_T),
                  ("conv_b", LRU_T), ("b_r", LRU_T), ("b_i", LRU_T), ("lam", LRU_T), ("q_gain", 1),
                  ("k_gain", 1), ("b_alpha", GLA_T), ("out_gain", 1), ("b_f", 1)):
    VEC[_name] = _at
    _at += _n
N_VEC = _at

MOD_COLS = 256
MOD_CHUNKS = 6 * D_MODEL // MOD_COLS
SHIFT1, SCALE1, GATE1, SHIFT2, SCALE2, GATE2 = (i * KD for i in range(6))


def split_products(nc, out, hi, lo, act_hi, act_lo, first, last):
    nc.tensor.matmul(out, hi, act_hi, start=first, stop=False)
    nc.tensor.matmul(out, hi, act_lo, start=False, stop=False)
    return nc.tensor.matmul(out, lo, act_hi, start=False, stop=last)


def project_in_and_recur(nc, vec, mod, xT, w_mod, w_in, w_gates, consts, vec_in, proj, mix):
    PAD = CONV_WIDTH - 1
    FIRST_CHUNKS = 2 * D_MODEL // MOD_COLS
    PAIRS = N_PROJ // 2
    LRU_PAIR = 5
    CHUNKS_A_PAIR = (MOD_CHUNKS - FIRST_CHUNKS) // (LRU_PAIR - 1)
    assert CHUNKS_A_PAIR == 4 and T_XA == 0 and 2 * LRU_PAIR > T_YA + LRU_T and LRU_PAIR + 2 * LRU_T < PAIRS
    SOFTPLUS, LINKS = 5, PAD - 1 + 6
    with ExitStack() as ctx:
        sb = lambda n, s, d=F32: ctx.enter_context(nc.sbuf_tensor(n, s, d))
        ps = lambda n, s, d=F32: ctx.enter_context(nc.psum_tensor(n, s, d))
        sem = lambda n: ctx.enter_context(nc.semaphore(n))
        two = lambda n: [sem(n + "_even"), sem(n + "_odd")]

        with nc.sbuf_tensor("x_late", [P, KD, SEQ], F32) as x_late:
            pass
        h_lo, h_hi = sb("h_lo", [P, KD, SEQ], F32R), sb("h_hi", [P, KD, SEQ], F32R)
        x_blk = sb("x_blk", [P, 2 * KD * BLK])
        shared = sb("shared", [P, 2 * KD * MOD_COLS])
        w_raw = sb("w_raw", [P, KD * P])
        w_hi, w_lo = sb("w_hi", [P, 2, KD, P], F32R), sb("w_lo", [P, 2, KD, P], F32R)
        mod_acc = sb("mod_acc", [P, 2, MOD_COLS])
        mean_ones, ones_col, eps = sb("mean_ones", [P, P]), sb("ones_col", [P, 1]), sb("eps", [P, 1])
        c_act, scale_a = sb("c_act", [P, KD]), sb("scale_a", [P, KD])
        rstd = sb("rstd", [P, BLK])
        xa = sb("lru_xa", [P, PAD + BLK])
        carry = sb("lru_carry", [P, 1])
        sp_abs, sp_exp, sp_one, sp_ln, sp_rec, sp_err = (sb("lru_sp%d" % i, [P, LRU_T]) for i in range(6))
        rate, neg_rate = sb("lru_rate", [P, LRU_T]), sb("lru_neg_rate", [P, LRU_T])
        banks = ps("banks", [P, 8, BLK])

        mod_w = shared[:, :].rearrange("p (s k n) -> p s k n", s=2, k=KD)
        squares = shared[:, :].rearrange("p (k n) -> p k n", k=KD)
        x_kt = x_blk[:, :].rearrange("p (s k n) -> p s k n", s=2, k=KD)
        slots = x_blk[:, :].rearrange("p (i n) -> p i n", n=BLK)
        x_src = lambda n: x_kt[:, n] if n < 2 else x_late[:, :, n * BLK:(n + 1) * BLK]
        stage = slots[:, 0:NBLK]
        ya, conv, r_gate, i_gate, tanh_y, decay, gelu_y, inv, u_in, state, out = (slots[:, NBLK + i] for i in range(11))
        gates = slots[:, NBLK + 11, 0:2 * P].rearrange("p (g n) -> p g n", g=2)
        ssum = mod_acc[:, :].rearrange("p s n -> p (s n)")
        mod_ps = banks[:, 4, 0:6 * KD]
        gate_ps = banks[:, 5:7]
        norm_ps = banks[:, 7, :]
        flat = lambda t: t.rearrange("p k n -> p (k n)")
        lam = vec[:, VEC["lam"]:VEC["lam"] + LRU_T]
        wcol = lambda name, i: vec[:, VEC[name] + i:VEC[name] + i + 1]

        params_in, c_ready, ones_ready = sem("params_in"), sem("c_ready"), sem("ones_ready")
        modw_in, modacc_ready, partial, mod_done, mod_ready = two("modw_in"), sem("modacc_ready"), sem("partial"), sem("mod_done"), sem("mod_ready")
        x_in, sq_ready, ssum_ready, norm_sum, rms_ready, rstd_ready = two("x_in"), sem("sq_ready"), sem("ssum_ready"), sem("norm_sum"), sem("rms_ready"), sem("rstd_ready")
        xn_ready, h_hi_ready, h_full, h_ready = sem("xn_ready"), sem("h_hi_ready"), sem("h_full"), sem("h_ready")
        w_in_sem, hi_ready, lo_ready = sem("w_in_sem"), sem("hi_ready"), sem("lo_ready")
        block_done, staged, stored = sem("block_done"), sem("staged"), [sem("stored_block%d" % b) for b in range(NBLK)]
        lru_in, gates_in, link, sp_act, rate_ready, halo = sem("lru_in"), sem("gates_in"), sem("lru_link"), sem("lru_sp_act"), sem("rate_ready"), sem("lru_halo")
        conv_ready, gates_done, act_done, ix_done, sqrt_done = sem("lru_conv_ready"), sem("lru_gates_done"), sem("lru_act_done"), sem("lru_ix_done"), sem("lru_sqrt_done")
        out_ready, out_stored, carried, tile_start = sem("lru_out_ready"), sem("lru_out_stored"), sem("lru_carried"), sem("lru_tile_start")

        def pairs(engine, step, before_tile=None):
            for s in range(2):
                step(0, None, s)
            with engine.Fori(1, LRU_PAIR) as i:
                for s in range(2):
                    step(i, -1, s)
            for t in range(LRU_T):
                if before_tile:
                    before_tile(t)
                with engine.Fori(LRU_PAIR + 2 * t, LRU_PAIR + 2 * t + 2) as i:
                    for s in range(2):
                        step(i, t, s)
            for s in range(2):
                step(PAIRS - 1, None, s)

        unit = lambda i, s, each=1, more=0: (2 * each) * i + (each * (s - 2 * LRU_PAIR) + more)
        with nc.Block() as block:
            @block.sync
            def _(sp):
                sp.dma_start(vec[:], vec_in).then_inc(params_in, 16)
                sp.dma_start(mean_ones[:], consts[:, C_MEAN * P:(C_MEAN + 1) * P]).then_inc(params_in, 16)
                for n in range(2):
                    sp.dma_start(mod_w[:, n], w_mod[n]).then_inc(modw_in[n], 16)
                with sp.Fori(1, FIRST_CHUNKS // 2) as i:
                    for s in range(2):
                        sp.wait_ge(modacc_ready, 2 * i + (s - 1))
                        sp.dma_start(mod_w[:, s], w_mod[bass.ds(2 * i + s, 1)].rearrange("o p k n -> (o p) k n")).then_inc(modw_in[s], 16)
                sp.dma_start(w_raw[:], w_in[0]).then_inc(w_in_sem, 16)
                sp.wait_ge(lo_ready, 1)
                sp.dma_start(w_raw[:], w_in[1]).then_inc(w_in_sem, 16)

                def chunk(i, s, c):
                    n = FIRST_CHUNKS - 4 + 2 * s + c
                    sp.wait_ge(modacc_ready, 4 * i + (n - 1))
                    sp.dma_start(mod_w[:, c], w_mod[bass.ds(4 * i + n, 1)].rearrange("o p k n -> (o p) k n")).then_inc(modw_in[c], 16)

                def step(i, t, s):
                    static = isinstance(i, int)
                    if t is not None and t >= 0:
                        sp.wait_ge(out_ready, unit(i, s, 1, 1))
                        sp.wait_ge(halo, unit(i, s, 1, 1))
                        token = (2 * BLK) * i + BLK * (s - 2 * (LRU_PAIR + 2 * t))
                        sp.dma_start(xa[:, PAD:], proj[T_XA + t, :, bass.ds(token, BLK)]).then_inc(lru_in, 16)
                        sp.dma_start(ya, proj[T_YA + t, :, bass.ds(token, BLK)]).then_inc(lru_in, 16)
                    if t == -1:
                        for c in range(2):
                            chunk(i, s, c)
                    if not (static and i):
                        sp.wait_ge(lo_ready, 2 * i + (s + 2))
                        sp.dma_start(w_raw[:], (w_in[2 + s] if static else w_in[bass.ds(2 * i + (s + 2), 1)].rearrange("o p n -> (o p) n"))).then_inc(w_in_sem, 16)
                    for b in range(NBLK):
                        sp.wait_ge(staged, 8 * i + (4 * s + b + 5))
                        dst = proj[s + 2 * i, :, b * BLK:(b + 1) * BLK] if static else proj[bass.ds(2 * i + s, 1), :, b * BLK:(b + 1) * BLK].rearrange("o p n -> (o p) n")
                        sp.dma_start(dst, stage[:, b]).then_inc(stored[b], 16)
                sp.wait_ge(ssum_ready, NBLK)
                pairs(sp, step)
                for b in range(NBLK):
                    sp.wait_ge(stored[b], 16 + 16 * N_PROJ)

            @block.gpsimd
            def _(pool):
                nc.gpsimd.memset(eps[:], EPS).then_inc(ones_ready, 1)
                nc.gpsimd.memset(ones_col[:], 1.0).then_inc(ones_ready, 1)
                for n in range(2):
                    pool.wait_ge(modacc_ready, 3 + 3 * n)
                    pool.dma_start(x_kt[:, n], xT[:, :, n * BLK:(n + 1) * BLK]).then_inc(x_in[n], 16)
                for n in range(2, NBLK):
                    pool.wait_ge(x_in[n % 2], 16)
                    pool.wait_ge(modacc_ready, FIRST_CHUNKS)
                    pool.dma_start(x_late[:, :, n * BLK:(n + 1) * BLK], xT[:, :, n * BLK:(n + 1) * BLK]).then_inc(x_in[n % 2], 16)

                def lows(n, s):
                    pool.wait_ge(hi_ready, n)
                    nc.gpsimd.tensor_tensor(flat(w_lo[:, s]), w_raw[:], flat(w_hi[:, s]).bitcast(F32), ALU.subtract).then_inc(lo_ready, 1)
                lows(1, 0)
                lows(2, 1)
                for n in range(NBLK - 1):
                    pool.wait_ge(h_full, n + 1)
                    nc.gpsimd.tensor_tensor(h_lo[:, :, n * BLK:(n + 1) * BLK], x_kt[:, n % 2], h_hi[:, :, n * BLK:(n + 1) * BLK].bitcast(F32), ALU.subtract).then_inc(h_ready, 1)
                pool.wait_ge(h_ready, NBLK)

                def step(i, t, s):
                    if t is not None and t >= 0:
                        pool.wait_ge(act_done, unit(i, s, 5, 2))
                        nc.gpsimd.tensor_tensor(u_in, i_gate, conv, ALU.mult).then_inc(ix_done, 1)
                    if not (isinstance(i, int) and i):
                        lows(2 * i + (s + 3), s)

                def start_tile(t):
                    pool.wait_ge(out_ready, NBLK * t + 1)
                    pool.wait_ge(halo, NBLK * t + 1)
                    if t >= 1:
                        pool.wait_ge(carried, NBLK * t)
                    pool.dma_start(gates, w_gates[:, t].rearrange("g p n -> p g n")).then_inc(gates_in, 16)
                    nc.gpsimd.memset(xa[:, 0:PAD], 0.0).then_inc(tile_start, 1)
                    pool.wait_ge(tile_start, 2 * t + 1)
                    nc.gpsimd.memset(carry[:], 0.0).then_inc(tile_start, 1)
                pairs(pool, step, start_tile)

            @block.scalar
            def _(act):
                act.sem_inc(out_stored, 16)
                for b in range(NBLK):
                    act.sem_inc(stored[b], 16)
                act.wait_ge(params_in, 32)
                act.wait_ge(ones_ready, 2)
                nc.scalar.activation(c_act[:], vec[:, VEC["c"]:VEC["c"] + KD], ACT.Silu).then_inc(c_ready, 1)
                nc.scalar.activation(sp_abs[:], lam, ACT.Abs).then_inc(sp_act, 1)
                act.wait_ge(sp_act, 1)
                nc.scalar.activation(sp_exp[:], sp_abs[:], ACT.Exp, scale=-1.0).then_inc(sp_act, 1)
                act.wait_ge(link, 1)
                nc.scalar.activation(sp_ln[:], sp_one[:], ACT.Ln).then_inc(sp_act, 1)

                def highs(s):
                    nc.scalar.activation(flat(w_hi[:, s]), w_raw[:], ACT.Copy).then_inc(hi_ready, 1)
                for s in range(2):
                    act.wait_ge(w_in_sem, 16 * (s + 1))
                    highs(s)
                act.wait_ge(mod_ready, 1)

                def square(n):
                    act.wait_ge(x_in[n % 2], 16 * (n // 2 + 1))
                    if n >= 1:
                        act.wait_ge(ssum_ready, n)
                    nc.scalar.activation(squares, x_src(n), ACT.Square).then_inc(sq_ready, 1)

                def root(n):
                    act.wait_ge(norm_sum, n + 1)
                    if n >= 1:
                        act.wait_ge(xn_ready, n)
                    nc.scalar.activation(rstd[:], norm_ps, ACT.Sqrt, bias=eps[:]).then_inc(rms_ready, 1)
                square(0)
                root(0)
                for n in range(NBLK):
                    if n + 1 < NBLK:
                        square(n + 1)
                    act.wait_ge(xn_ready, n + 1)
                    for k in range(KD):
                        last = nc.scalar.activation(h_hi[:, k, n * BLK:(n + 1) * BLK], x_kt[:, n % 2, k], ACT.Identity,
                                                    bias=mod[:, SHIFT1 + k:SHIFT1 + k + 1], scale=scale_a[:, k:k + 1])
                    last.then_inc(h_hi_ready, 1)
                    if n + 1 < NBLK:
                        root(n + 1)
                act.wait_ge(h_ready, NBLK)

                def step(i, t, s):
                    if t is not None and t >= 0:
                        act.wait_ge(gates_done, unit(i, s, 1, 2))
                        act.wait_ge(out_ready, unit(i, s, 1, 1))
                        nc.scalar.activation(r_gate, gate_ps[:, 0], ACT.Sigmoid, bias=wcol("b_r", t)).then_inc(act_done, 1)
                        nc.scalar.activation(i_gate, gate_ps[:, 1], ACT.Sigmoid, bias=wcol("b_i", t)).then_inc(act_done, 1)
                        act.wait_ge(act_done, unit(i, s, 5, 2))
                        act.wait_ge(rate_ready, 2)
                        nc.scalar.activation(tanh_y, r_gate, ACT.Tanh, scale=rate[:, t:t + 1]).then_inc(act_done, 1)
                        nc.scalar.activation(decay, r_gate, ACT.Exp, scale=neg_rate[:, t:t + 1]).then_inc(act_done, 1)
                        act.wait_ge(lru_in, unit(i, s, 32, 32))
                        nc.scalar.activation(gelu_y, ya, ACT.Gelu_apprx_tanh).then_inc(act_done, 1)
                        act.wait_ge(link, unit(i, s, LINKS, SOFTPLUS + PAD + 3))
                        nc.scalar.activation(inv, inv, ACT.Sqrt).then_inc(sqrt_done, 1)
                        act.wait_ge(out_ready, unit(i, s, 1, 2))
                        token = (2 * BLK) * i + BLK * (s - 2 * (LRU_PAIR + 2 * t))
                        act.dma_start(mix[t, :, bass.ds(token, BLK)], out).then_inc(out_stored, 16)
                    if not (isinstance(i, int) and i):
                        act.wait_ge(w_in_sem, 32 * i + (16 * s + 48))
                        act.wait_ge(block_done, 8 * i + (4 * s + 4))
                        act.wait_ge(lo_ready, 2 * i + (s + 2))
                        highs(s)
                pairs(act, step)
                act.wait_ge(out_stored, 16 + 16 * NBLK * LRU_T)

            @block.vector
            def _(dve):
                dve.sem_inc(out_ready, 1)
                dve.sem_inc(halo, 1)
                dve.wait_ge(sp_act, 2)
                nc.vector.tensor_scalar(sp_one[:], sp_exp[:], 1.0, None, ALU.add).then_inc(link, 1)
                dve.wait_ge(link, 1)
                nc.vector.reciprocal(sp_rec[:], sp_one[:])
                nc.vector.scalar_tensor_tensor(out=sp_err[:], in0=sp_one[:], scalar=-1.0, in1=sp_exp[:], op0=ALU.add, op1=ALU.subtract).then_inc(link, 1)
                dve.wait_ge(link, 2)
                nc.vector.tensor_tensor(sp_err[:], sp_err[:], sp_rec[:], ALU.mult).then_inc(link, 1)
                dve.wait_ge(link, 3)
                dve.wait_ge(sp_act, 3)
                nc.vector.tensor_tensor(sp_ln[:], sp_ln[:], sp_err[:], ALU.subtract).then_inc(link, 1)
                nc.vector.tensor_scalar(sp_abs[:], lam, 0.0, None, ALU.min)
                dve.wait_ge(link, 4)
                nc.vector.tensor_scalar(sp_ln[:], sp_ln[:], LRU_C, None, ALU.mult).then_inc(link, 1)
                dve.wait_ge(link, 5)
                nc.vector.scalar_tensor_tensor(out=rate[:], in0=sp_abs[:], scalar=-LRU_C, in1=sp_ln[:], op0=ALU.mult, op1=ALU.add).then_inc(rate_ready, 1)
                dve.wait_ge(rate_ready, 1)
                nc.vector.tensor_scalar(neg_rate[:], rate[:], -1.0, None, ALU.mult).then_inc(rate_ready, 1)
                dve.wait_ge(c_ready, 1)

                def modulate(s, loaded, done, sums):
                    dve.wait_ge(modw_in[s], loaded)
                    dve.wait_ge(mod_done, done)
                    nc.vector.tensor_scalar(mod_acc[:, s], mod_w[:, s, 0], c_act[:, 0:1], None, ALU.mult).then_inc(partial, 1)
                    for k in range(1, KD):
                        dve.wait_ge(partial, sums + k)
                        nc.vector.scalar_tensor_tensor(out=mod_acc[:, s], in0=mod_w[:, s, k], scalar=c_act[:, k:k + 1], in1=mod_acc[:, s],
                                                       op0=ALU.mult, op1=ALU.add).then_inc(partial if k < KD - 1 else modacc_ready, 1)
                with dve.Fori(0, FIRST_CHUNKS // 2) as i:
                    for s in range(2):
                        modulate(s, 16 * i + 16, 2 * i + (s + 1), 2 * (KD - 1) * i + (KD - 1) * s)
                dve.wait_ge(mod_done, FIRST_CHUNKS + 2)
                FIRST_COLS = SCALE1 + KD
                SUMS = (KD - 1) * FIRST_CHUNKS + 1
                nc.vector.tensor_tensor(mod[:, 0:FIRST_COLS], mod_ps[:, 0:FIRST_COLS], vec[:, VEC["b_mod"]:VEC["b_mod"] + FIRST_COLS], ALU.add).then_inc(partial, 1)
                dve.wait_ge(partial, SUMS)
                nc.vector.scalar_tensor_tensor(out=scale_a[:], in0=mod[:, SCALE1:SCALE1 + KD], scalar=1.0, in1=vec[:, VEC["g1"]:VEC["g1"] + KD],
                                               op0=ALU.add, op1=ALU.mult).then_inc(mod_ready, 1)
                dve.wait_ge(mod_ready, 1)

                def sum_squares(n):
                    dve.wait_ge(sq_ready, n + 1)
                    if n >= 1:
                        dve.wait_ge(norm_sum, n)
                    nc.vector.tensor_reduce(ssum, squares.rearrange("p k n -> p n k"), AX.X, ALU.add).then_inc(ssum_ready, 1)
                sum_squares(0)
                for n in range(NBLK):
                    xb = x_kt[:, n % 2]
                    dve.wait_ge(rms_ready, n + 1)
                    nc.vector.reciprocal(rstd[:], rstd[:]).then_inc(rstd_ready, 1)
                    dve.wait_ge(rstd_ready, n + 1)
                    if n >= 2:
                        dve.wait_ge(h_ready, n - 1)
                    nc.vector.tensor_tensor(xb, x_src(n), rstd[:, None, :].to_broadcast([P, KD, BLK]), ALU.mult).then_inc(xn_ready, 1)
                    if n + 1 < NBLK:
                        sum_squares(n + 1)
                    dve.wait_ge(h_hi_ready, n + 1)
                    for k in range(KD):
                        last = nc.vector.tensor_scalar(xb[:, k], xb[:, k], scale_a[:, k:k + 1], mod[:, SHIFT1 + k:SHIFT1 + k + 1], ALU.mult, ALU.add)
                    last.then_inc(h_full, 1)
                dve.wait_ge(h_full, NBLK)
                dve.wait_ge(h_ready, NBLK - 1)
                nc.vector.tensor_tensor(h_lo[:, :, SEQ - BLK:], x_kt[:, (NBLK - 1) % 2], h_hi[:, :, SEQ - BLK:].bitcast(F32), ALU.subtract).then_inc(h_ready, 1)
                dve.wait_ge(h_ready, NBLK)

                def copy_block(i, s, b):
                    dve.wait_ge(block_done, 8 * i + (4 * s + b + 1))
                    dve.wait_ge(stored[b], 32 * i + (16 * s + 16))
                    nc.vector.tensor_copy(stage[:, b], banks[:, b]).then_inc(staged, 1)

                def convolve(i, t, s):
                    tap = lambda j: xa[:, j:j + BLK]
                    at = lambda x: unit(i, s, LINKS, SOFTPLUS + x)
                    dve.wait_ge(lru_in, unit(i, s, 32, 32))
                    dve.wait_ge(tile_start, 2 * t + 2)
                    dve.wait_ge(gates_done, unit(i, s, 1, 1))
                    nc.vector.tensor_scalar(conv, tap(PAD), wcol("conv_w", PAD * LRU_T + t), wcol("conv_b", t), ALU.mult, ALU.add).then_inc(link, 1)
                    for j in range(PAD):
                        dve.wait_ge(link, at(j + 1))
                        nc.vector.scalar_tensor_tensor(out=conv, in0=tap(j), scalar=wcol("conv_w", j * LRU_T + t), in1=conv,
                                                       op0=ALU.mult, op1=ALU.add).then_inc(link if j < PAD - 1 else conv_ready, 1)
                    dve.wait_ge(conv_ready, unit(i, s, 1, 1))
                    nc.vector.tensor_copy(xa[:, 0:PAD], xa[:, BLK:BLK + PAD]).then_inc(halo, 1)
                    dve.wait_ge(halo, unit(i, s, 1, 2))

                def recur(i, s):
                    at = lambda x: unit(i, s, LINKS, SOFTPLUS + PAD + x)
                    dve.wait_ge(act_done, unit(i, s, 5, 3))
                    nc.vector.tensor_scalar(inv, tanh_y, 1.0, None, ALU.add).then_inc(link, 1)
                    dve.wait_ge(link, at(1))
                    nc.vector.reciprocal(inv, inv).then_inc(link, 1)
                    dve.wait_ge(link, at(2))
                    nc.vector.scalar_tensor_tensor(out=inv, in0=tanh_y, scalar=2.0, in1=inv, op0=ALU.mult, op1=ALU.mult).then_inc(link, 1)
                    dve.wait_ge(ix_done, unit(i, s, 1, 1))
                    dve.wait_ge(sqrt_done, unit(i, s, 1, 1))
                    nc.vector.tensor_tensor(u_in, u_in, inv, ALU.mult).then_inc(link, 1)
                    dve.wait_ge(link, at(4))
                    dve.wait_ge(act_done, unit(i, s, 5, 5))
                    nc.vector.tensor_tensor_scan(state, decay, u_in, carry[:, 0:1], ALU.mult, ALU.add).then_inc(link, 1)
                    dve.wait_ge(link, at(5))
                    nc.vector.tensor_copy(carry[:], state[:, BLK - 1:BLK]).then_inc(carried, 1)
                    dve.wait_ge(carried, unit(i, s, 1, 1))
                    dve.wait_ge(out_stored, unit(i, s, 16, 16))
                    nc.vector.tensor_tensor(out, state, gelu_y, ALU.mult).then_inc(out_ready, 1)

                def step(i, t, s):
                    if t is not None and t >= 0:
                        convolve(i, t, s)
                    for b in range(NBLK):
                        if t == -1 and b % 2 == 0:
                            c = 2 * s + b // 2
                            modulate(b // 2, 32 * i + (8 * FIRST_CHUNKS + 16 * s - 16), 4 * i + (FIRST_CHUNKS - 4 + c + 1),
                                     4 * (KD - 1) * i + (SUMS + (KD - 1) * (c - 4)))
                        copy_block(i, s, b)
                        if t is not None and t >= 0 and b == 1:
                            recur(i, s)
                pairs(dve, step)
                dve.wait_ge(mod_done, MOD_CHUNKS + 2)
                nc.vector.tensor_tensor(mod[:, FIRST_COLS:], mod_ps[:, FIRST_COLS:], vec[:, VEC["b_mod"] + FIRST_COLS:VEC["b_mod"] + 6 * KD], ALU.add)

            @block.tensor
            def _(pe):
                pe.sem_inc(mod_done, 2)
                pe.sem_inc(gates_done, 1)
                pe.wait_ge(ones_ready, 2)
                pe.wait_ge(params_in, 32)

                def reduce_chunk(s, ready, column):
                    pe.wait_ge(modacc_ready, ready)
                    for j in range(MOD_COLS // P):
                        last = nc.tensor.matmul(mod_ps[:, bass.ds(column + j, 1)], mod_acc[:, s, j * P:(j + 1) * P], ones_col[:], start=True, stop=True)
                    last.then_inc(mod_done, 1)
                with pe.Fori(0, FIRST_CHUNKS // 2) as i:
                    for s in range(2):
                        reduce_chunk(s, 2 * i + (s + 1), 4 * i + 2 * s)
                for n in range(NBLK):
                    pe.wait_ge(ssum_ready, n + 1)
                    if n >= 1:
                        pe.wait_ge(rms_ready, n)
                    nc.tensor.matmul(norm_ps, mean_ones[:], ssum, start=True, stop=True).then_inc(norm_sum, 1)
                pe.sem_inc(staged, NBLK)

                def step(i, t, s):
                    pe.wait_ge(lo_ready, 2 * i + (s + 1))
                    for b in range(NBLK):
                        if isinstance(i, int) and i == 0 and s == 0:
                            pe.wait_ge(h_ready, b + 1)
                            pe.wait_ge(h_hi_ready, b + 1)
                        pe.wait_ge(staged, 8 * i + (4 * s + b + 1))
                        cols = slice(b * BLK, (b + 1) * BLK)
                        for k in range(KD):
                            last = split_products(nc, banks[:, b], w_hi[:, s, k], w_lo[:, s, k], h_hi[:, k, cols], h_lo[:, k, cols], k == 0, k == KD - 1)
                        last.then_inc(block_done, 1)
                        if t == -1 and b % 2 == 1:
                            c = 2 * s + b // 2
                            reduce_chunk(b // 2, 4 * i + (FIRST_CHUNKS - 4 + c + 1), 8 * i + (2 * (FIRST_CHUNKS - 4 + c)))
                        if t is not None and t >= 0 and b == 1:
                            pe.wait_ge(conv_ready, unit(i, s, 1, 1))
                            pe.wait_ge(gates_in, 16 * t + 16)
                            pe.wait_ge(out_ready, unit(i, s, 1, 1))
                            for g in range(2):
                                last = nc.tensor.matmul(gate_ps[:, g], gates[:, g], conv, start=True, stop=True)
                            last.then_inc(gates_done, 1)
                pairs(pe, step)


def fox_operands(nc, vec, consts, fox_rows, proj, q_split, k_split, bias_split, v_nat):
    HEADS2 = 2 * FOX_HEADS
    TILES = 2 * FOX_T
    HALF = SEQ // 2
    HALVES = [(t, w) for t in range(TILES) for w in range(2)]
    with ExitStack() as ctx:
        sb = lambda n, s, d=F32: ctx.enter_context(nc.sbuf_tensor(n, s, d))
        ps = lambda n, s, d=F32: ctx.enter_context(nc.psum_tensor(n, s, d))
        sem = lambda n: ctx.enter_context(nc.semaphore(n))
        qk = sb("fp_qk", [P, TILES, SEQ])
        v_raw = sb("fp_v", [P, FOX_T, SEQ])
        squares = sb("fp_squares", [P, 2, HALF])
        hi, lo = sb("fp_hi", [P, 2, HALF], F32R), sb("fp_lo", [P, 2, HALF], F32R)
        ident = sb("fp_ident", [P, P])
        rows_sel = sb("fp_rows_sel", [P, TILES, HEADS2])
        back_sel = sb("fp_back_sel", [HEADS2, TILES, P])
        rows = [sb("fp_rows%d" % i, [FF_ROW + FOX_HEADS, SEQ]) for i in range(4)]
        mean, rstd, newton = (r[0:HEADS2] for r in rows[:3])
        logit, e_neg, log1p, err = (r[FF_ROW:FF_ROW + FOX_HEADS] for r in rows)
        bias_hi, bias_lo = (t[FF_ROW:FF_ROW + FOX_HEADS].rearrange("p w n -> p (w n)") for t in (hi, lo))
        ones_col = sb("fp_ones_col", [FF_ROW + FOX_HEADS, 1])
        ones_row = ones_col[FF_ROW:FF_ROW + FOX_HEADS].to_broadcast([FOX_HEADS, SEQ])
        gains = sb("fp_gains", [P, 2])
        banks = ps("fp_banks", [P, 8, BLK])
        two = lambda n: [sem(n + "_even"), sem(n + "_odd")]
        loaded, squared, summed = [sem("fp_loaded%d" % i) for i in range(FOX_T)], sem("fp_squared"), sem("fp_summed")
        ln_done, spread, normed, hi_done, lo_done = sem("fp_ln_done"), sem("fp_spread"), sem("fp_normed"), sem("fp_hi_done"), sem("fp_lo_done")
        hi_out, lo_out, v_t, v_hi_done, v_lo_done = two("fp_hi_out"), two("fp_lo_out"), sem("fp_v_t"), sem("fp_v_hi_done"), sem("fp_v_lo_done")
        f_act, f_link, f_hi, f_out, chain, consts_in = sem("fp_f_act"), sem("fp_f_link"), sem("fp_f_hi"), sem("fp_f_out"), sem("fp_chain"), sem("fp_consts_in")
        v_hi, v_lo = v_nat[:, :, :, 0:HEAD_DIM], v_nat[:, :, :, HEAD_DIM:]
        cols = lambda w: slice(w * HALF, (w + 1) * HALF)
        two_banks = lambda w: banks[:, 2 * w:2 * w + 2].rearrange("p b n -> p (b n)")
        with nc.Block() as block:
            @block.sync
            def _(sp):
                sp.dma_start(ident[:], consts[:, C_IDENT * P:(C_IDENT + 1) * P]).then_inc(consts_in, 16)
                sp.dma_start(rows_sel[:], fox_rows[:, 0:TILES * HEADS2].rearrange("p (t h) -> p t h", t=TILES)).then_inc(consts_in, 16)
                sp.dma_start(back_sel[:], fox_rows[0:HEADS2, TILES * HEADS2:].rearrange("h (t p) -> h t p", t=TILES)).then_inc(consts_in, 16)
                sp.dma_start(v_raw[:], proj[T_FV:T_FV + FOX_T].rearrange("t p n -> p t n")).then_inc(consts_in, 16)
                for i in range(FOX_T):
                    sp.dma_start(qk[:, 2 * i:2 * i + 2], proj[T_FQ + 2 * i:T_FQ + 2 * i + 2].rearrange("t p n -> p t n")).then_inc(loaded[i], 16)
                for u, (t, w) in enumerate(HALVES):
                    split, j = (q_split, k_split)[t // FOX_T], t % FOX_T
                    for part, (src, done, out) in enumerate(((hi, hi_done, hi_out), (lo, lo_done, lo_out))):
                        sp.wait_ge(done, u + 1)
                        for h in range(2):
                            sp.dma_start(split[2 * j + h, part, :, cols(w)], src[HEAD_DIM * h:HEAD_DIM * (h + 1), u % 2].bitcast(F32)).then_inc(out[u % 2], 16)
                for out in hi_out + lo_out:
                    sp.wait_ge(out, 32 * TILES)

            @block.gpsimd
            def _(pool):
                pool.dma_start(logit, proj[T_MISC, FF_ROW:FF_ROW + FOX_HEADS]).then_inc(f_out, 16)
                nc.gpsimd.memset(ones_col[:], 1.0).then_inc(f_act, 1)
                pool.wait_ge(f_hi, 2)
                pool.dma_start(bias_split[:, 0], bias_hi.bitcast(F32)).then_inc(f_out, 16)
                pool.dma_start(bias_split[:, 1], bias_lo.bitcast(F32)).then_inc(f_out, 16)
                pool.wait_ge(f_out, 48)

            @block.scalar
            def _(act):
                act.wait_ge(f_link, 1)
                nc.scalar.activation(e_neg, logit, ACT.Abs).then_inc(ln_done, 1)
                act.wait_ge(ln_done, 1)
                nc.scalar.activation(e_neg, e_neg, ACT.Exp, scale=-1.0).then_inc(ln_done, 1)
                act.wait_ge(f_link, 2)
                nc.scalar.activation(log1p, err, ACT.Ln).then_inc(ln_done, 1)
                for n in range(4 * FOX_T):
                    j, g = n // 4, n % 4
                    act.wait_ge(v_t, n + 1)
                    nc.scalar.activation(v_hi[:, 2 * j:2 * j + 2, 4 * g:4 * g + 4].rearrange("p h t d -> p t h d"),
                                         banks[:, 4 + n % 4].rearrange("p (t h d) -> p t h d", t=4, h=2), ACT.Copy).then_inc(v_hi_done, 1)
                for u, (t, w) in enumerate(HALVES):
                    act.wait_ge(loaded[t // 2], 16)
                    if u >= 2:
                        act.wait_ge(summed, u - 1)
                    nc.scalar.activation(squares[:, u % 2], qk[:, t, cols(w)], ACT.Square).then_inc(squared, 1)
                act.wait_ge(chain, 1)
                nc.scalar.activation(rstd, mean, ACT.Ln).then_inc(ln_done, 1)
                act.wait_ge(ln_done, 4)
                nc.scalar.activation(rstd, rstd, ACT.Exp, scale=-0.5).then_inc(ln_done, 1)
                act.wait_ge(f_out, 48)
                for u, (t, w) in enumerate(HALVES):
                    act.wait_ge(normed, u + 1)
                    if u >= 2:
                        act.wait_ge(lo_done, u - 1)
                        act.wait_ge(hi_out[u % 2], 32 * (u // 2))
                    nc.scalar.activation(hi[:, u % 2], qk[:, t, cols(w)], ACT.Copy).then_inc(hi_done, 1)

            @block.vector
            def _(dve):
                nc.vector.tensor_scalar(gains[:, 0:1], vec[:, VEC["q_gain"]:VEC["q_gain"] + 1], HEAD_DIM ** -0.5, None, ALU.mult)
                nc.vector.tensor_copy(gains[:, 1:2], vec[:, VEC["k_gain"]:VEC["k_gain"] + 1])
                dve.wait_ge(f_out, 16)
                nc.vector.tensor_scalar(logit, logit, vec[FF_ROW:FF_ROW + FOX_HEADS, VEC["b_f"]:VEC["b_f"] + 1], None, ALU.add).then_inc(f_link, 1)
                dve.wait_ge(ln_done, 2)
                nc.vector.tensor_scalar(err, e_neg, 1.0, None, ALU.add).then_inc(f_link, 1)
                dve.wait_ge(ln_done, 3)
                nc.vector.scalar_tensor_tensor(out=err, in0=err, scalar=-1.0, in1=e_neg, op0=ALU.add, op1=ALU.subtract).then_inc(f_link, 1)
                dve.wait_ge(f_link, 3)
                nc.vector.tensor_scalar(e_neg, logit, 0.0, None, ALU.min).then_inc(f_link, 1)
                nc.vector.tensor_tensor(log1p, log1p, err, ALU.subtract).then_inc(f_link, 1)
                dve.wait_ge(f_link, 5)
                nc.vector.tensor_tensor(err, log1p, e_neg, ALU.subtract).then_inc(f_link, 1)
                dve.wait_ge(f_link, 6)
                dve.wait_ge(f_act, 1)
                nc.vector.tensor_tensor_scan(log1p, ones_row, err, 0.0, ALU.mult, ALU.add).then_inc(f_link, 1)
                dve.wait_ge(f_link, 7)
                nc.vector.tensor_copy(bias_hi, log1p).then_inc(f_hi, 1)
                dve.wait_ge(f_hi, 1)
                nc.vector.tensor_tensor(bias_lo, log1p, bias_hi.bitcast(F32), ALU.subtract).then_inc(f_hi, 1)
                for n in range(4 * FOX_T):
                    j, g = n // 4, n % 4
                    dve.wait_ge(v_hi_done, n + 1)
                    for h in range(2):
                        last = nc.vector.tensor_tensor(v_lo[:, 2 * j + h, 4 * g:4 * g + 4],
                                                       banks[:, 4 + n % 4].rearrange("p (t h d) -> p t h d", t=4, h=2)[:, :, h],
                                                       v_hi[:, 2 * j + h, 4 * g:4 * g + 4].bitcast(F32), ALU.subtract)
                    last.then_inc(v_lo_done, 1)
                dve.wait_ge(summed, 2 * TILES)
                nc.vector.tensor_scalar(mean, banks[0:HEADS2, 0:4].rearrange("p b n -> p (b n)"), EPS, None, ALU.add).then_inc(chain, 1)
                dve.wait_ge(ln_done, 5)
                nc.vector.tensor_tensor(newton, rstd, rstd, ALU.mult).then_inc(chain, 1)
                dve.wait_ge(chain, 2)
                nc.vector.tensor_tensor(newton, newton, mean, ALU.mult).then_inc(chain, 1)
                dve.wait_ge(chain, 3)
                nc.vector.tensor_scalar(newton, newton, -0.5, 1.5, ALU.mult, ALU.add).then_inc(chain, 1)
                dve.wait_ge(chain, 4)
                nc.vector.tensor_tensor(rstd, rstd, newton, ALU.mult).then_inc(chain, 1)

                def norm(u):
                    t, w = HALVES[u]
                    dve.wait_ge(spread, u + 1)
                    nc.vector.scalar_tensor_tensor(out=qk[:, t, cols(w)], in0=qk[:, t, cols(w)], scalar=gains[:, t // FOX_T:t // FOX_T + 1],
                                                   in1=two_banks(w), op0=ALU.mult, op1=ALU.mult).then_inc(normed, 1)
                norm(0)
                dve.wait_ge(f_out, 48)
                for u, (t, w) in enumerate(HALVES):
                    if u + 1 < len(HALVES):
                        norm(u + 1)
                    dve.wait_ge(hi_done, u + 1)
                    if u >= 2:
                        dve.wait_ge(lo_out[u % 2], 32 * (u // 2))
                    nc.vector.tensor_tensor(lo[:, u % 2], qk[:, t, cols(w)], hi[:, u % 2].bitcast(F32), ALU.subtract).then_inc(lo_done, 1)

            @block.tensor
            def _(pe):
                pe.wait_ge(consts_in, 64)
                for n in range(4 * FOX_T):
                    if n >= 4:
                        pe.wait_ge(v_lo_done, n - 3)
                    for t in range(4):
                        o = (4 * (n % 4) + t) * P
                        last = nc.tensor.transpose(banks[:, 4 + n % 4, t * P:(t + 1) * P], v_raw[:, n // 4, o:o + P], ident[:])
                    last.then_inc(v_t, 1)
                for u, (t, w) in enumerate(HALVES):
                    pe.wait_ge(squared, u + 1)
                    for b in range(2):
                        last = nc.tensor.matmul(banks[0:HEADS2, 2 * w + b], rows_sel[:, t], squares[:, u % 2, b * BLK:(b + 1) * BLK], start=(t == 0), stop=(t == TILES - 1))
                    last.then_inc(summed, 1)
                pe.wait_ge(chain, 5)
                for u, (t, w) in enumerate(HALVES):
                    if u >= 2:
                        pe.wait_ge(normed, u - 1)
                    for b in range(2):
                        last = nc.tensor.matmul(banks[:, 2 * w + b], back_sel[:, t], rstd[:, (2 * w + b) * BLK:(2 * w + b + 1) * BLK], start=True, stop=True)
                    last.then_inc(spread, 1)


def forgetting_attention(nc, consts, q_split, k_split, bias_split, v_nat, mix):
    HPB = 2
    LOOPS = FOX_HEADS // HPB
    NU = HPB * NBLK
    UNITS = [(u // NBLK % HPB, u % NBLK) for u in range(2 * NU)]
    TPB = BLK // P
    VW = 2 * HEAD_DIM
    ITEMS = [(u, kt, max(0, kt - TPB * b)) for u, (hh, b) in enumerate(UNITS[:NU]) for kt in range(TPB * (b + 1))]
    CHUNKS = [(u, i, c, min(BLK, (TPB * b + i + 1) * P - c * BLK)) for u, (hh, b) in enumerate(UNITS) for i in range(TPB) for c in range(b + 1)]
    NC = NI = len(ITEMS)
    chunks_of = lambda u: [n for n, x in enumerate(CHUNKS) if x[0] == u]
    items_of = lambda u: [m for m, x in enumerate(ITEMS) if x[0] == u]
    LEAD, AHEAD = 22, 3
    turns = {m: [u for u in range(2 * NU) if chunks_of(u)[-1] - LEAD + 2 == m] for m in range(NI)}
    EARLY = [u for u in range(2 * NU) if chunks_of(u)[-1] - LEAD + 2 < 0]
    SB, TB, PB = 2, 3, 4
    on_pool = lambda m: ITEMS[m][1] % 3 == 1
    pool_count = lambda m: sum(on_pool(x) for x in range(m + 1))
    dve_count = lambda m: m + 1 - pool_count(m)
    POOL_ALL, DVE_ALL = pool_count(NI - 1), dve_count(NI - 1)

    with ExitStack() as ctx:
        sb = lambda n, s, d=F32: ctx.enter_context(nc.sbuf_tensor(n, s, d))
        ps = lambda n, s, d=F32: ctx.enter_context(nc.psum_tensor(n, s, d))
        sem = lambda n: ctx.enter_context(nc.semaphore(n))
        two = lambda n: [sem(n + "_even"), sem(n + "_odd")]
        k_a, q_a = sb("fa_k_a", [P, HPB, SEQ], F32R), sb("fa_q_a", [P, HPB, SEQ], F32R)
        v = sb("fa_v", [P, HPB, SEQ // P, 3 * HEAD_DIM], F32R)
        k_b, q_b = sb("fa_k_b", [HEAD_DIM + 4, HPB, SEQ], F32R), sb("fa_q_b", [HEAD_DIM + 4, HPB, SEQ], F32R)
        MAXROW = HEAD_DIM + 2
        ROWS_B = HEAD_DIM + 4
        ident, ident_r = sb("fa_ident", [P, P]), sb("fa_ident_r", [P, P], F32R)
        masks, masks_r = sb("fa_masks", [P, 2, P]), sb("fa_masks_r", [P, 2, P], F32R)
        ch_max = sb("fa_ch_max", [P, 2, TPB, NBLK])
        neg_max = sb("fa_neg_max", [P, 2, TPB])
        m_cols = sb("fa_m_cols", [P, 2, TPB, ROWS_B], F32R)
        probs = sb("fa_probs", [P, PB, BLK])
        p_hi, p_lo = sb("fa_p_hi", [P, PB, BLK], F32R), sb("fa_p_lo", [P, PB, BLK], F32R)
        inv_sum, newton = sb("fa_inv_sum", [HEAD_DIM, 2, BLK]), sb("fa_newton", [HEAD_DIM, 2, BLK])
        o_t = sb("fa_o_t", [P, NBLK, BLK])
        s_ps, st_ps = ps("fa_s_ps", [P, SB, BLK]), ps("fa_st_ps", [P, TB, BLK])
        o_ps, m_ps = ps("fa_o_ps", [P, 2, BLK]), ps("fa_m_ps", [P, BLK])

        const_in, made, filled = sem("fa_const_in"), sem("fa_made"), sem("fa_filled")
        qk_in, v_ready = two("fa_qk_in"), sem("fa_v_ready")
        m_turned, m_copied = sem("fa_m_turned"), sem("fa_m_copied")
        s_done, max_done, neg_done, m_ready = sem("fa_s_done"), sem("fa_max_done"), sem("fa_neg_done"), sem("fa_m_ready")
        st_done, hi_done, lo_dve, lo_pool, pv_done = sem("fa_st_done"), sem("fa_hi_done"), sem("fa_lo_dve"), sem("fa_lo_pool"), sem("fa_pv_done")
        ln_sum, inv_done, corrected, fin_done, stored = sem("fa_ln_sum"), sem("fa_inv_done"), sem("fa_corrected"), sem("fa_fin_done"), [sem("fa_stored_block%d" % b) for b in range(NBLK)]

        with nc.Block() as block:
            @block.sync
            def _(sp):
                sp.dma_start(ident[:], consts[:, C_IDENT * P:(C_IDENT + 1) * P]).then_inc(const_in, 16)
                sp.dma_start(masks[:], consts[:, C_CAUSAL * P:(C_CAUSAL + 2) * P].rearrange("p (w n) -> p w n", w=2)).then_inc(const_in, 16)
                with sp.Fori(0, LOOPS) as j:
                    for hh in range(HPB):
                        h = bass.ds(HPB * j + hh, 1)
                        sp.wait_ge(st_done, NI * j + (items_of(NBLK * hh + NBLK - 1)[-1] + 1))
                        one = lambda t: t.rearrange("o d n -> (o d) n")
                        sp.dma_start(q_a[:, hh].bitcast(F32), q_split[h].rearrange("o w d n -> (o w d) n")).then_inc(qk_in[hh], 16)
                        sp.dma_start(k_a[0:HEAD_DIM, hh].bitcast(F32), one(k_split[h, 0])).then_inc(qk_in[hh], 16)
                        sp.dma_start(k_a[HEAD_DIM:P, hh].bitcast(F32), one(k_split[h, 0])).then_inc(qk_in[hh], 16)
                        sp.dma_start(q_b[0:HEAD_DIM, hh].bitcast(F32), one(q_split[h, 0])).then_inc(qk_in[hh], 16)
                        sp.dma_start(k_b[0:HEAD_DIM, hh].bitcast(F32), one(k_split[h, 1])).then_inc(qk_in[hh], 16)
                        sp.wait_ge(filled, 2)
                        sp.dma_start(k_b[HEAD_DIM:MAXROW, hh].bitcast(F32), one(bias_split[h])).then_inc(qk_in[hh], 16)
                sp.sem_inc(qk_in[0], 96)

            @block.gpsimd
            def _(pool):
                nc.gpsimd.memset(q_b[HEAD_DIM:].bitcast(F32), 1.0).then_inc(filled, 1)
                pool.wait_ge(filled, 1)
                nc.gpsimd.memset(k_b[HEAD_DIM:].bitcast(F32), 1.0).then_inc(filled, 1)
                pool.wait_ge(filled, 2)
                nc.gpsimd.memset(m_cols[:].bitcast(F32), 1.0).then_inc(filled, 1)
                pool.wait_ge(filled, 3)
                nc.gpsimd.memset(v[:, :, :, HEAD_DIM:VW].rearrange("p h t n -> p (h t) n").bitcast(F32), 1.0).then_inc(filled, 1)
                pool.wait_ge(filled, 4)

                def place_v(hh, head, used):
                    pool.wait_ge(pv_done, used)
                    src = v_nat[:, head].rearrange("p o t n -> p (o t) n")
                    nc.gpsimd.tensor_copy(v[:, hh, :, 0:HEAD_DIM], src[:, :, 0:HEAD_DIM].bitcast(F32))
                    nc.gpsimd.tensor_copy(v[:, hh, :, VW:], src[:, :, HEAD_DIM:].bitcast(F32)).then_inc(v_ready, 1)

                def lows(base, head):
                    for m, (u, kt, r) in enumerate(ITEMS):
                        if m == 3:
                            place_v(1, head(1), base + NI)
                        if m == NI // 2 + 4 and head(2) is not None:
                            place_v(0, head(2), base + (NI + NI // 2))
                        if on_pool(m):
                            pool.wait_ge(hi_done, base + (m + 1))
                            nc.gpsimd.tensor_tensor(p_lo[:, m % PB, r * P:BLK], probs[:, m % PB, r * P:BLK], p_hi[:, m % PB, r * P:BLK].bitcast(F32),
                                                    ALU.subtract).then_inc(lo_pool, 1)
                place_v(0, slice(0, 1), NI)
                with pool.Fori(0, LOOPS - 1) as j:
                    lows(NI * j, lambda h: bass.ds(HPB * j + h, 1))
                last = FOX_HEADS - HPB
                lows(NI * (LOOPS - 1), lambda h: slice(last + h, last + h + 1) if h < HPB else None)

            @block.scalar
            def _(act):
                act.sem_inc(m_copied, 1)
                act.wait_ge(filled, 1)
                for b in range(NBLK):
                    act.sem_inc(stored[b], 16)

                def copy_m(u, loops):
                    hh, b = UNITS[u]
                    act.wait_ge(m_turned, loops + (u + 3))
                    nc.scalar.activation(q_b[HEAD_DIM:ROWS_B, hh, b * BLK:(b + 1) * BLK], m_ps[HEAD_DIM:ROWS_B], ACT.Copy).then_inc(m_copied, 1)
                for u in EARLY:
                    copy_m(u, 0)
                with act.Fori(0, LOOPS) as j:
                    def store(b):
                        act.wait_ge(fin_done, NU * j + (NBLK + b + 3))
                        act.dma_start(mix[bass.ds(j + LRU_T, 1), :, b * BLK:(b + 1) * BLK].rearrange("o p n -> (o p) n"), o_t[:, b]).then_inc(stored[b], 16)

                    def invert(u):
                        act.wait_ge(pv_done, NI * j + (NI + items_of(u)[-1] + 1))
                        act.wait_ge(fin_done, NU * j + (u + 1))
                        nc.scalar.activation(newton[:, u % 2], o_ps[HEAD_DIM:P, u % 2], ACT.Ln).then_inc(ln_sum, 1)
                        act.wait_ge(ln_sum, NU * j + (u + 1))
                        nc.scalar.activation(inv_sum[:, u % 2], newton[:, u % 2], ACT.Exp, scale=-1.0).then_inc(inv_done, 1)
                    for m, (u, kt, r) in enumerate(ITEMS):
                        cols = slice(r * P, BLK)
                        act.wait_ge(st_done, NI * j + (NI + m + 1))
                        act.wait_ge(pv_done, NI * j + (NI + m + 1 - PB))
                        nc.scalar.activation(probs[:, m % PB, cols], st_ps[:, m % TB, cols], ACT.Exp)
                        nc.scalar.activation(p_hi[:, m % PB, cols], st_ps[:, m % TB, cols], ACT.Exp).then_inc(hi_done, 1)
                        for x in turns.get(m - 1, ()):
                            copy_m(x, NU * j)
                        if u > 0 and kt == 3:
                            invert(u - 1)
                        if u > NBLK and kt == 7:
                            store(u - NBLK - 1)
                    invert(NU - 1)
                    store(NBLK - 1)
                for b in range(NBLK):
                    act.wait_ge(stored[b], 16 + 16 * LOOPS)

            @block.vector
            def _(dve):
                dve.wait_ge(const_in, 32)
                nc.vector.tensor_copy(ident_r[:], ident[:]).then_inc(made, 1)
                nc.vector.tensor_copy(masks_r[:], masks[:]).then_inc(made, 1)
                dve.sem_inc(max_done, SB)
                dve.sem_inc(fin_done, 2)
                dve.sem_inc(pv_done, NI)
                dve.sem_inc(m_turned, 2)
                dve.wait_ge(filled, 3)

                def maxima(n, chunks, units):
                    u, i, c, w = CHUNKS[n]
                    b = UNITS[u][1]
                    dve.wait_ge(s_done, chunks + (n + 1))
                    nc.vector.tensor_reduce(ch_max[:, u % 2, i, c:c + 1], s_ps[:, n % SB, 0:w], AX.X, ALU.max).then_inc(max_done, 1)
                    if n == chunks_of(u)[-1]:
                        dve.wait_ge(max_done, chunks + (n + 1 + SB))
                        nc.vector.tensor_reduce(neg_max[:, u % 2], ch_max[:, u % 2, :, 0:b + 1], AX.X, ALU.max, negate=True).then_inc(neg_done, 1)
                        dve.wait_ge(neg_done, 2 * units + (2 * u + 1))
                        dve.wait_ge(m_turned, units + (u + 1))
                        nc.vector.tensor_copy(m_cols[:, u % 2, :, MAXROW], neg_max[:, u % 2]).then_inc(neg_done, 1)
                        dve.wait_ge(neg_done, 2 * units + (2 * u + 2))
                        nc.vector.tensor_tensor(m_cols[:, u % 2, :, MAXROW + 1], neg_max[:, u % 2], m_cols[:, u % 2, :, MAXROW].bitcast(F32), ALU.subtract).then_inc(m_ready, 1)
                for n in range(LEAD):
                    maxima(n, 0, 0)
                with dve.Fori(0, LOOPS) as j:
                    def correct(u):
                        dve.wait_ge(inv_done, NU * j + (u + 1))
                        nc.vector.tensor_tensor(newton[:, u % 2], o_ps[HEAD_DIM:P, u % 2], inv_sum[:, u % 2], ALU.mult).then_inc(corrected, 1)

                    def finish(u):
                        hh, b = UNITS[u]
                        dve.wait_ge(corrected, 2 * NU * j + (2 * u + 1))
                        nc.vector.scalar_tensor_tensor(out=inv_sum[:, u % 2], in0=newton[:, u % 2], scalar=-2.0, in1=inv_sum[:, u % 2], op0=ALU.add, op1=ALU.mult).then_inc(corrected, 1)
                        dve.wait_ge(corrected, 2 * NU * j + (2 * u + 2))
                        if hh == 0:
                            dve.wait_ge(stored[b], 16 * j + 16)
                        nc.vector.scalar_tensor_tensor(out=o_t[HEAD_DIM * hh:HEAD_DIM * (hh + 1), b], in0=o_ps[0:HEAD_DIM, u % 2], scalar=-1.0, in1=inv_sum[:, u % 2], op0=ALU.mult, op1=ALU.mult).then_inc(fin_done, 1)
                    for m, (u, kt, r) in enumerate(ITEMS):
                        if not on_pool(m):
                            dve.wait_ge(hi_done, NI * j + (m + 1))
                            nc.vector.tensor_tensor(p_lo[:, m % PB, r * P:BLK], probs[:, m % PB, r * P:BLK], p_hi[:, m % PB, r * P:BLK].bitcast(F32),
                                                    ALU.subtract).then_inc(lo_dve, 1)
                        maxima(m + LEAD, NC * j, NU * j)
                        if u > 0 and kt == 2:
                            correct(u - 1)
                        if u > 0 and kt == 3:
                            finish(u - 1)
                    correct(NU - 1)
                    finish(NU - 1)

            @block.tensor
            def _(pe):
                pe.wait_ge(made, 2)
                pe.wait_ge(filled, 2)
                pe.sem_inc(st_done, NI)

                def score(n, loop):
                    u, i, c, w = CHUNKS[n]
                    hh, b = UNITS[u]
                    if n == chunks_of(u)[0] and b == 0:
                        pe.wait_ge(qk_in[hh], 96 * loop + (96 * (u // NU) + 96))
                    pe.wait_ge(max_done, NC * loop + (n + 1))
                    out, keys = s_ps[:, n % SB, 0:w], slice(c * BLK, c * BLK + w)
                    qt = slice((TPB * b + i) * P, (TPB * b + i + 1) * P)
                    diagonal = c == b
                    nc.tensor.matmul(out, q_a[:, hh, qt], k_a[:, hh, keys], start=True, stop=False)
                    last = nc.tensor.matmul(out, q_b[0:MAXROW, hh, qt], k_b[0:MAXROW, hh, keys], start=False, stop=not diagonal)
                    if diagonal:
                        last = nc.tensor.matmul(s_ps[:, n % SB, w - P:w], ident_r[:], masks_r[:, 0], start=False, stop=True)
                    last.then_inc(s_done, 1)

                def turn_m(u, loop):
                    pe.wait_ge(m_ready, NU * loop + (u + 1))
                    pe.wait_ge(m_copied, NU * loop + (u + 1))
                    for i in range(TPB):
                        last = nc.tensor.matmul(m_ps[0:ROWS_B, i * P:(i + 1) * P], m_cols[:, u % 2, i], ident_r[:], start=True, stop=True)
                    last.then_inc(m_turned, 1)

                for n in range(LEAD):
                    score(n, 0)
                for u in EARLY:
                    turn_m(u, 0)
                with pe.Fori(0, LOOPS) as j:
                    def score_t(m):
                        u, kt, r = ITEMS[m]
                        hh, b = UNITS[u]
                        if m == items_of(u)[0]:
                            pe.wait_ge(m_copied, NU * j + (u + 2))
                        if m >= TB:
                            pe.wait_ge(hi_done, NI * j + (m + 1 - TB))
                        out, kts = st_ps[:, m % TB, r * P:BLK], slice(kt * P, (kt + 1) * P)
                        qs = slice(b * BLK + r * P, (b + 1) * BLK)
                        diagonal = kt >= TPB * b
                        nc.tensor.matmul(out, k_a[:, hh, kts], q_a[:, hh, qs], start=True, stop=False)
                        last = nc.tensor.matmul(out, k_b[:, hh, kts], q_b[:, hh, qs], start=False, stop=not diagonal)
                        if diagonal:
                            last = nc.tensor.matmul(st_ps[:, m % TB, r * P:(r + 1) * P], ident_r[:], masks_r[:, 1], start=False, stop=True)
                        last.then_inc(st_done, 1)

                    def times_v(m):
                        u, kt, r = ITEMS[m]
                        hh, b = UNITS[u]
                        if kt == 0:
                            pe.wait_ge(fin_done, NU * j + (u + 1))
                        if kt == 0 and b == 0:
                            pe.wait_ge(v_ready, HPB * j + (hh + 1))
                        if on_pool(m):
                            pe.wait_ge(lo_pool, POOL_ALL * j + pool_count(m))
                        else:
                            pe.wait_ge(lo_dve, DVE_ALL * j + dve_count(m))
                        qs, first, end = slice(r * P, BLK), kt == 0, kt == TPB * b + TPB - 1
                        nc.tensor.matmul(o_ps[:, u % 2, qs], v[:, hh, kt, 0:VW], p_hi[:, m % PB, qs], start=first, stop=False, skip_group_check=True)
                        nc.tensor.matmul(o_ps[0:HEAD_DIM, u % 2, qs], v[:, hh, kt, VW:VW + HEAD_DIM], p_hi[:, m % PB, qs], start=False, stop=False, skip_group_check=True)
                        nc.tensor.matmul(o_ps[:, u % 2, qs], v[:, hh, kt, 0:VW], p_lo[:, m % PB, qs], start=False, stop=end, skip_group_check=True).then_inc(pv_done, 1)

                    for m in range(AHEAD):
                        score_t(m)
                    for m in range(NI):
                        score(m + LEAD, j)
                        if m + AHEAD < NI:
                            score_t(m + AHEAD)
                        for u in turns[m]:
                            turn_m(u, j)
                        times_v(m)


def gated_linear_attention(nc, vec, consts, w_alpha, proj, mix):
    NCHUNK = SEQ // GLA_CHUNK
    GRP = 4
    NG = NBLK
    ALL = GLA_T * NG
    GPS = NG // 2
    span = lambda x: (x // 2, slice(x % 2 * SEQ // 2, (x % 2 + 1) * SEQ // 2))
    span_chunks = lambda x: slice(x % 2 * NCHUNK // 2, (x % 2 + 1) * NCHUNK // 2)
    CPG = BLK // GLA_CHUNK
    with ExitStack() as ctx:
        sb = lambda n, s, d=F32: ctx.enter_context(nc.sbuf_tensor(n, s, d))
        ps = lambda n, s, d=F32: ctx.enter_context(nc.psum_tensor(n, s, d))
        sem = lambda n: ctx.enter_context(nc.semaphore(n))
        two = lambda n: [sem(n + "_even"), sem(n + "_odd")]
        gq, gk, gv, gg = (sb("ga_" + n, [P, GLA_T, SEQ]) for n in ("gq", "gk", "gv", "gg"))
        glow, w_a = sb("ga_glow", [GLA_RANK, SEQ]), sb("ga_w_a", [GLA_RANK, GLA_T * P])
        ident, head_ones, mask = sb("ga_ident", [P, P]), sb("ga_head_ones", [P, P]), sb("ga_mask", [P, P])
        restart = sb("ga_restart", [P, SEQ])
        z, e_neg, one_e = sb("ga_z", [P, GLA_T, SEQ]), sb("ga_e_neg", [P, SEQ]), sb("ga_one_e", [P, SEQ])
        b_cum = sb("ga_b_cum", [P, SEQ])
        grow = sb("ga_grow", [P, SEQ])
        k_end, q_dec, k_dec = sb("ga_k_end", [P, SEQ]), sb("ga_q_dec", [P, GLA_T, SEQ]), sb("ga_k_dec", [P, SEQ])
        decay = sb("ga_decay", [P, GLA_T, NCHUNK])
        v_n, k_n = sb("ga_v_n", [P, 2, GRP, P]), sb("ga_k_n", [P, 2, GRP, P])
        att = sb("ga_att", [P, 2, 2, GRP, P])
        state = sb("ga_state", [P, NCHUNK + 1, P])
        squares, rstd, o_norm = sb("ga_squares", [P, BLK]), sb("ga_rstd", [P, BLK]), sb("ga_o_norm", [P, BLK])
        eps = sb("ga_eps", [P, 1])
        z_ps = ps("ga_z_ps", [P, 4, BLK])
        att_ps, kv_ps = z_ps[:, 0:2], z_ps[:, 2:4]
        turn_ps, o_ps, mean_ps = ps("ga_turn_ps", [P, 2, BLK]), ps("ga_o_ps", [P, BLK]), ps("ga_mean_ps", [P, BLK])
        base, loaded, made, z_done, z_biased = sem("ga_base"), two("ga_loaded"), sem("ga_made"), sem("ga_z_done"), sem("ga_z_biased")
        silu_done, exp_done, ln_done, grown, turned, turn_read = sem("ga_silu_done"), sem("ga_exp_done"), sem("ga_ln_done"), sem("ga_grown"), sem("ga_turned"), sem("ga_turn_read")
        one_e_done, cumulated, decayed_done = sem("ga_one_e_done"), sem("ga_cumulated"), sem("ga_decayed_done")
        att_done, att_masked, kv_done, state_done, o_done = sem("ga_att_done"), sem("ga_att_masked"), sem("ga_kv_done"), sem("ga_state_done"), sem("ga_o_done")
        squared, mean_done, norm_act, o_normed, gated, stored = sem("ga_squared"), sem("ga_mean_done"), sem("ga_norm_act"), sem("ga_o_normed"), sem("ga_gated"), sem("ga_stored")
        chunks = lambda t: t.rearrange("p (c n) -> p c n", n=GLA_CHUNK)
        half = lambda h: slice(HEAD_DIM * h, HEAD_DIM * (h + 1))

        with nc.Block() as block:
            @block.sync
            def _(sp):
                sp.dma_start(glow[:], proj[T_MISC, 0:GLA_RANK]).then_inc(base, 16)
                sp.dma_start(w_a[:], w_alpha).then_inc(base, 16)
                sp.dma_start(ident[:], consts[:, C_IDENT * P:(C_IDENT + 1) * P]).then_inc(base, 16)
                sp.dma_start(head_ones[:], consts[:, C_HEAD * P:(C_HEAD + 1) * P]).then_inc(base, 16)
                sp.dma_start(mask[:], consts[:, C_CHUNK * P:(C_CHUNK + 1) * P]).then_inc(base, 16)
                for j in range(GLA_T):
                    for t0, tile in ((T_GK, gk), (T_GQ, gq), (T_GV, gv), (T_GG, gg)):
                        sp.dma_start(tile[:, j], proj[t0 + j]).then_inc(loaded[j], 16)
                for j in range(GLA_T):
                    sp.wait_ge(gated, NG * (j + 1))
                    sp.dma_start(mix[LRU_T + FOX_T + j], gg[:, j]).then_inc(stored, 16)
                sp.wait_ge(stored, 16 * GLA_T)

            @block.gpsimd
            def _(pool):
                nc.gpsimd.memset(restart[:], 1.0).then_inc(made, 1)
                pool.wait_ge(made, 1)
                nc.gpsimd.memset(chunks(restart[:])[:, :, 0:1], 0.0).then_inc(made, 1)
                pool.wait_ge(made, 2)
                nc.gpsimd.memset(att[:], 0.0).then_inc(made, 1)
                pool.wait_ge(made, 3)
                nc.gpsimd.memset(state[:], 0.0).then_inc(made, 1)
                pool.wait_ge(made, 4)
                nc.gpsimd.memset(eps[:], EPS).then_inc(made, 1)

            @block.scalar
            def _(act):
                act.wait_ge(made, 5)

                def gate(j):
                    act.wait_ge(loaded[j], 64)
                    nc.scalar.activation(gg[:, j], gg[:, j], ACT.Silu).then_inc(silu_done, 1)

                def exp_z(x):
                    j, at = span(x)
                    act.wait_ge(z_biased, j + 1)
                    if x >= 2:
                        act.wait_ge(decayed_done, 3 * (x - 1))
                    nc.scalar.activation(e_neg[:, at], z[:, j, at], ACT.Abs).then_inc(exp_done, 1)
                    act.wait_ge(exp_done, 2 * x + 1)
                    nc.scalar.activation(e_neg[:, at], e_neg[:, at], ACT.Exp, scale=-1.0).then_inc(exp_done, 1)

                def ln_z(x):
                    j, at = span(x)
                    act.wait_ge(one_e_done, x + 1)
                    nc.scalar.activation(grow[:, at], one_e[:, at], ACT.Ln).then_inc(ln_done, 1)

                def decays(x):
                    j, at = span(x)
                    act.wait_ge(cumulated, 5 * x + 5)
                    nc.scalar.activation(z[:, j, at], one_e[:, at], ACT.Exp, scale=1.0 / GLA_TAU).then_inc(grown, 1)
                    nc.scalar.activation(grow[:, at], b_cum[:, at], ACT.Exp, scale=-1.0 / GLA_TAU).then_inc(grown, 1)
                    nc.scalar.activation(e_neg[:, at], b_cum[:, at], ACT.Exp, scale=1.0 / GLA_TAU).then_inc(grown, 1)
                    nc.scalar.activation(decay[:, j, span_chunks(x)], chunks(b_cum[:, at])[:, :, GLA_CHUNK - 1], ACT.Exp, scale=1.0 / GLA_TAU).then_inc(grown, 1)

                def copy_turned(n):
                    act.wait_ge(turned, n + 1)
                    if n >= 2:
                        act.wait_ge(o_done, n - 1)
                    nc.scalar.activation(k_n[:, n % 2], turn_ps[:, 1].rearrange("p (t n) -> p t n", t=GRP), ACT.Copy)
                    nc.scalar.activation(v_n[:, n % 2], turn_ps[:, 0].rearrange("p (t n) -> p t n", t=GRP), ACT.Copy).then_inc(turn_read, 1)

                exp_z(0)
                exp_z(1)
                ln_z(0)
                decays(0)
                ln_z(1)
                copy_turned(0)
                decays(1)
                gate(0)
                exp_z(2)
                gate(1)
                for n in range(ALL):
                    if n + 1 < ALL:
                        copy_turned(n + 1)
                    act.wait_ge(o_done, n + 1)
                    if n >= 1:
                        act.wait_ge(mean_done, n)
                    nc.scalar.activation(squares[:], o_ps[:], ACT.Square).then_inc(squared, 1)
                    act.wait_ge(mean_done, n + 1)
                    if n >= 1:
                        act.wait_ge(o_normed, n)
                    nc.scalar.activation(rstd[:], mean_ps[:], ACT.Ln, bias=eps[:]).then_inc(norm_act, 1)
                    act.wait_ge(norm_act, 2 * n + 1)
                    nc.scalar.activation(rstd[:], rstd[:], ACT.Exp, scale=-0.5).then_inc(norm_act, 1)
                    if n == 0:
                        ln_z(2)
                        exp_z(3)
                    if n == 1:
                        decays(2)
                        ln_z(3)
                    if n == 2:
                        decays(3)

            @block.vector
            def _(dve):
                dve.wait_ge(made, 5)
                dve.wait_ge(base, 80)

                def bias(j):
                    dve.wait_ge(z_done, j + 1)
                    nc.vector.tensor_scalar(z[:, j], z_ps[:].rearrange("p b n -> p (b n)"), vec[:, VEC["b_alpha"] + j:VEC["b_alpha"] + j + 1], None, ALU.add).then_inc(z_biased, 1)

                def one_plus_e(x):
                    j, at = span(x)
                    dve.wait_ge(exp_done, 2 * x + 2)
                    nc.vector.tensor_scalar(one_e[:, at], e_neg[:, at], 1.0, None, ALU.add).then_inc(one_e_done, 1)

                def cumulate(x):
                    j, at = span(x)
                    dve.wait_ge(ln_done, x + 1)
                    nc.vector.scalar_tensor_tensor(out=one_e[:, at], in0=one_e[:, at], scalar=-1.0, in1=e_neg[:, at], op0=ALU.add, op1=ALU.subtract).then_inc(cumulated, 1)
                    dve.wait_ge(cumulated, 5 * x + 1)
                    nc.vector.tensor_tensor(one_e[:, at], grow[:, at], one_e[:, at], ALU.subtract).then_inc(cumulated, 1)
                    dve.wait_ge(cumulated, 5 * x + 2)
                    nc.vector.scalar_tensor_tensor(out=e_neg[:, at], in0=z[:, j, at], scalar=0.0, in1=one_e[:, at], op0=ALU.min, op1=ALU.subtract).then_inc(cumulated, 1)
                    dve.wait_ge(cumulated, 5 * x + 3)
                    nc.vector.tensor_tensor_scan(b_cum[:, at], restart[:, at], e_neg[:, at], 0.0, ALU.mult, ALU.add).then_inc(cumulated, 1)
                    dve.wait_ge(cumulated, 5 * x + 4)
                    nc.vector.tensor_tensor(chunks(one_e[:, at]), chunks(b_cum[:, at])[:, :, GLA_CHUNK - 1:GLA_CHUNK].to_broadcast([P, NCHUNK // 2, GLA_CHUNK]),
                                            chunks(b_cum[:, at]), ALU.subtract).then_inc(cumulated, 1)

                def decayed(x):
                    j, at = span(x)
                    dve.wait_ge(grown, 4 * x + 1)
                    dve.wait_ge(loaded[j], 64)
                    if x >= 2:
                        dve.wait_ge(turned, GPS * (x - 1))
                        dve.wait_ge(att_done, 2 * GPS * (x - 1))
                    nc.vector.tensor_tensor(k_end[:, at], gk[:, j, at], z[:, j, at], ALU.mult).then_inc(decayed_done, 1)
                    dve.wait_ge(grown, 4 * x + 2)
                    nc.vector.tensor_tensor(k_dec[:, at], gk[:, j, at], grow[:, at], ALU.mult).then_inc(decayed_done, 1)
                    dve.wait_ge(grown, 4 * x + 4)
                    nc.vector.scalar_tensor_tensor(out=q_dec[:, j, at], in0=gq[:, j, at], scalar=HEAD_DIM ** -0.5, in1=e_neg[:, at], op0=ALU.mult, op1=ALU.mult).then_inc(decayed_done, 1)

                def mask_att(n):
                    for h in range(2):
                        dve.wait_ge(att_done, 2 * n + h + 1)
                        if h == 0 and n >= 2:
                            dve.wait_ge(o_done, n - 1)
                        nc.vector.copy_predicated(att[:, n % 2, h], mask[:, None, :].to_broadcast([P, GRP, P]).bitcast(U32),
                                                  att_ps[:, h].rearrange("p (t n) -> p t n", t=GRP)).then_inc(att_masked, 1)

                def states(n):
                    j, g = n // NG, n % NG
                    dve.wait_ge(kv_done, n + 1)
                    for c in range(CPG):
                        m = CPG * g + c
                        for h in range(2):
                            if m >= 1:
                                dve.wait_ge(state_done, 2 * NCHUNK * j + (2 * m + h - 1))
                            nc.vector.scalar_tensor_tensor(out=state[half(h), m + 1, half(h)], in0=state[half(h), m, half(h)], scalar=decay[half(h), j, m:m + 1],
                                                           in1=kv_ps[half(h), c % 2, (c // 2) * P + HEAD_DIM * h:(c // 2) * P + HEAD_DIM * (h + 1)],
                                                           op0=ALU.mult, op1=ALU.add).then_inc(state_done, 1)

                def finish(n):
                    j, g = n // NG, n % NG
                    dve.wait_ge(norm_act, 2 * n + 2)
                    dve.wait_ge(silu_done, j + 1)
                    if n >= 1:
                        dve.wait_ge(gated, n)
                    nc.vector.scalar_tensor_tensor(out=o_norm[:], in0=o_ps[:], scalar=vec[:, VEC["out_gain"]:VEC["out_gain"] + 1], in1=rstd[:],
                                                   op0=ALU.mult, op1=ALU.mult).then_inc(o_normed, 1)
                    dve.wait_ge(o_normed, n + 1)
                    cols = slice(g * BLK, (g + 1) * BLK)
                    nc.vector.tensor_tensor(gg[:, j, cols], o_norm[:], gg[:, j, cols], ALU.mult).then_inc(gated, 1)

                for j in range(GLA_T):
                    bias(j)
                one_plus_e(0)
                cumulate(0)
                one_plus_e(1)
                decayed(0)
                cumulate(1)
                mask_att(0)
                states(0)
                decayed(1)
                for n in range(ALL):
                    if n + 1 < ALL:
                        mask_att(n + 1)
                        states(n + 1)
                    finish(n)
                    if n == 0:
                        one_plus_e(2)
                    if n == 1:
                        cumulate(2)
                        one_plus_e(3)
                    if n == 2:
                        decayed(2)
                        cumulate(3)
                    if n == 3:
                        decayed(3)

            @block.tensor
            def _(pe):
                pe.wait_ge(base, 80)
                pe.wait_ge(made, 5)
                for j in range(GLA_T):
                    if j >= 1:
                        pe.wait_ge(z_biased, j)
                    for b in range(NBLK):
                        last = nc.tensor.matmul(z_ps[:, b], w_a[:, j * P:(j + 1) * P], glow[:, b * BLK:(b + 1) * BLK], start=True, stop=True)
                    last.then_inc(z_done, 1)

                def turn(n):
                    j, g = n // NG, n % NG
                    if g == 0:
                        pe.wait_ge(loaded[j], 64)
                    if g % GPS == 0:
                        pe.wait_ge(decayed_done, 3 * (n // GPS + 1))
                    if n >= 1:
                        pe.wait_ge(turn_read, n)
                    for w, src in ((0, gv[:, j]), (1, k_end[:])):
                        for t in range(GRP):
                            o = (GRP * g + t) * P
                            last = nc.tensor.transpose(turn_ps[:, w, t * P:(t + 1) * P], src[:, o:o + P], ident[:])
                    last.then_inc(turned, 1)

                def attend(n):
                    j, g = n // NG, n % NG
                    if n >= 1:
                        pe.wait_ge(att_masked, 2 * n)
                    for h in range(2):
                        for t in range(GRP):
                            o = (GRP * g + t) * P
                            last = nc.tensor.matmul(att_ps[:, h, t * P:(t + 1) * P], k_dec[half(h), o:o + P], q_dec[half(h), j, o:o + P], start=True, stop=True)
                        last.then_inc(att_done, 1)

                def products_kv(n):
                    pe.wait_ge(turn_read, n + 1)
                    if n >= 1:
                        pe.wait_ge(state_done, 2 * CPG * n)
                    for c in range(CPG):
                        rows = slice(GLA_CHUNK * (c % 2), GLA_CHUNK * (c % 2 + 1))
                        last = nc.tensor.matmul(kv_ps[:, c % 2, (c // 2) * P:(c // 2 + 1) * P], k_n[rows, n % 2, c // 2], v_n[rows, n % 2, c // 2], start=True, stop=True)
                    last.then_inc(kv_done, 1)

                def outputs(n):
                    j, g = n // NG, n % NG
                    pe.wait_ge(att_masked, 2 * n + 2)
                    pe.wait_ge(state_done, 2 * CPG * (n + 1))
                    if n >= 1:
                        pe.wait_ge(o_normed, n)
                    for t in range(GRP):
                        for c in range(2):
                            m = CPG * g + 2 * t + c
                            nc.tensor.matmul(o_ps[:, (2 * t + c) * GLA_CHUNK:(2 * t + c + 1) * GLA_CHUNK], state[:, m], q_dec[:, j, m * GLA_CHUNK:(m + 1) * GLA_CHUNK],
                                             start=(t == 0 and c == 0), stop=False, skip_group_check=True)
                        for h in range(2):
                            last = nc.tensor.matmul(o_ps[half(h), t * P:(t + 1) * P], v_n[:, n % 2, t, half(h)], att[:, n % 2, h, t], start=False, stop=True, skip_group_check=True)
                    last.then_inc(o_done, 1)

                pe.wait_ge(z_biased, GLA_T)
                turn(0)
                attend(0)
                products_kv(0)
                for n in range(ALL):
                    if n + 1 < ALL:
                        turn(n + 1)
                        attend(n + 1)
                        products_kv(n + 1)
                    outputs(n)
                    pe.wait_ge(squared, n + 1)
                    nc.tensor.matmul(mean_ps[:], head_ones[:], squares[:], start=True, stop=True).then_inc(mean_done, 1)


def project_out(nc, vec, mod, rms_all, xT, w_out, consts, mix, x2):
    with ExitStack() as ctx:
        sb = lambda n, s, d=F32: ctx.enter_context(nc.sbuf_tensor(n, s, d))
        ps = lambda n, s, d=F32: ctx.enter_context(nc.psum_tensor(n, s, d))
        sem = lambda n: ctx.enter_context(nc.semaphore(n))
        two = lambda n: [sem(n + "_even"), sem(n + "_odd")]
        m_hi, m_lo = sb("po_m_hi", [P, KD, SEQ], F32R), sb("po_m_lo", [P, KD, SEQ], F32R)
        slot = sb("po_slot", [P, 2, SEQ])
        w_raw = sb("po_w_raw", [P, 2, KD * P])
        w_hi, w_lo = sb("po_w_hi", [P, 2, KD, P], F32R), sb("po_w_lo", [P, 2, KD, P], F32R)
        squares = sb("po_squares", [P, SEQ])
        sq_sum = rms_all
        mean_ones, eps = sb("po_mean_ones", [P, P]), sb("po_eps", [P, 1])
        banks = ps("po_banks", [P, 8, BLK])
        flat = lambda t: t.rearrange("p k n -> p (k n)")
        in_consts, made, mix_in, mix_hi, mix_lo = sem("po_in_consts"), sem("po_made"), two("po_mix_in"), sem("po_mix_hi"), sem("po_mix_lo")
        w_in, hi_ready, lo_ready, x_in = two("po_w_in"), sem("po_hi_ready"), sem("po_lo_ready"), two("po_x_in")
        tile_done, x2_ready, stored, squared, added = sem("po_tile_done"), sem("po_x2_ready"), two("po_stored"), sem("po_squared"), sem("po_added")
        mean_done = sem("po_mean_done")

        with nc.Block() as block:
            @block.sync
            def _(sp):
                sp.dma_start(mean_ones[:], consts[:, C_MEAN * P:(C_MEAN + 1) * P]).then_inc(in_consts, 16)
                for k in range(KD):
                    if k >= 2:
                        sp.wait_ge(mix_lo, k - 1)
                    sp.dma_start(slot[:, k % 2], mix[k]).then_inc(mix_in[k % 2], 16)
                    if k < 2:
                        sp.dma_start(w_raw[:, k], w_out[k]).then_inc(w_in[k], 16)
                sp.wait_ge(mix_lo, KD)
                for m in range(2):
                    sp.dma_start(slot[:, m], xT[:, m]).then_inc(x_in[m], 16)
                with sp.Fori(1, KD // 2) as i:
                    for s in range(2):
                        sp.wait_ge(lo_ready, 2 * i + (s - 1))
                        sp.dma_start(w_raw[:, s], w_out[bass.ds(2 * i + s, 1)].rearrange("o p n -> (o p) n")).then_inc(w_in[s], 16)
                    for s in range(2):
                        sp.wait_ge(stored[s], 16 * i)
                        sp.wait_ge(squared, 2 * i + (s - 1))
                        sp.dma_start(slot[:, s], xT[:, bass.ds(2 * i + s, 1)].rearrange("p o n -> p (o n)")).then_inc(x_in[s], 16)

            @block.gpsimd
            def _(pool):
                nc.gpsimd.memset(eps[:], EPS).then_inc(made, 1)
                pool.wait_ge(made, 1)
                nc.gpsimd.memset(sq_sum[:], 0.0).then_inc(made, 1)
                pool.wait_ge(made, 2)
                for m in range(2):
                    pool.wait_ge(hi_ready, m + 1)
                    nc.gpsimd.tensor_tensor(flat(w_lo[:, m]), w_raw[:, m], flat(w_hi[:, m]).bitcast(F32), ALU.subtract).then_inc(lo_ready, 1)
                with pool.Fori(1, KD // 2) as i:
                    for s in range(2):
                        pool.wait_ge(hi_ready, 2 * i + (s + 1))
                        nc.gpsimd.tensor_tensor(flat(w_lo[:, s]), w_raw[:, s], flat(w_hi[:, s]).bitcast(F32), ALU.subtract).then_inc(lo_ready, 1)
                        pool.wait_ge(squared, 2 * i + (s - 1))
                        nc.gpsimd.tensor_tensor(sq_sum[:], sq_sum[:], squares[:], ALU.add).then_inc(added, 1)
                        pool.wait_ge(added, 2 * i + s)
                pool.wait_ge(squared, KD - 1)
                nc.gpsimd.tensor_tensor(sq_sum[:], sq_sum[:], squares[:], ALU.add).then_inc(added, 1)

            @block.scalar
            def _(act):
                act.sem_inc(added, 1)
                for k in range(KD):
                    act.wait_ge(mix_in[k % 2], 16 * (k // 2 + 1))
                    nc.scalar.activation(m_hi[:, k], slot[:, k % 2], ACT.Copy).then_inc(mix_hi, 1)
                    if k < 2:
                        act.wait_ge(w_in[k], 16)
                        nc.scalar.activation(flat(w_hi[:, k]), w_raw[:, k], ACT.Copy).then_inc(hi_ready, 1)
                with act.Fori(1, KD // 2) as i:
                    for s in range(2):
                        act.wait_ge(w_in[s], 16 * i + 16)
                        act.wait_ge(tile_done, 2 * i + (s - 1))
                        nc.scalar.activation(flat(w_hi[:, s]), w_raw[:, s], ACT.Copy).then_inc(hi_ready, 1)
                        act.wait_ge(x2_ready, 2 * i + (s + 1))
                        act.dma_start(x2[bass.ds(2 * i + (s - 2), 1)].rearrange("o p n -> (o p) n"), slot[:, s]).then_inc(stored[s], 16)
                        act.wait_ge(added, 2 * i + (s - 1))
                        nc.scalar.activation(squares[:], slot[:, s], ACT.Square).then_inc(squared, 1)
                for m in (KD - 2, KD - 1):
                    act.wait_ge(x2_ready, m + 3)
                    act.dma_start(x2[m], slot[:, m % 2]).then_inc(stored[m % 2], 16)
                    act.wait_ge(added, m + 1)
                    nc.scalar.activation(squares[:], slot[:, m % 2], ACT.Square).then_inc(squared, 1)
                for b in range(NBLK):
                    act.wait_ge(mean_done, b + 1)
                    nc.scalar.activation(rms_all[:, b * BLK:(b + 1) * BLK], banks[:, b], ACT.Sqrt, bias=eps[:])
                for s in range(2):
                    act.wait_ge(stored[s], 16 * (KD // 2))

            @block.vector
            def _(dve):
                for k in range(KD):
                    dve.wait_ge(mix_hi, k + 1)
                    nc.vector.tensor_tensor(m_lo[:, k], slot[:, k % 2], m_hi[:, k].bitcast(F32), ALU.subtract).then_inc(mix_lo, 1)
                with dve.Fori(0, KD // 2) as i:
                    for s in range(2):
                        dve.wait_ge(tile_done, 2 * i + (s + 1))
                        dve.wait_ge(x_in[s], 16 * i + 16)
                        nc.vector.scalar_tensor_tensor(out=slot[:, s], in0=banks[:, 4 * s:4 * s + 4].rearrange("p b n -> p (b n)"),
                                                       scalar=mod[:, bass.ds(2 * i + (s + GATE1), 1)], in1=slot[:, s],
                                                       op0=ALU.mult, op1=ALU.add).then_inc(x2_ready, 1)

            @block.tensor
            def _(pe):
                pe.sem_inc(x2_ready, 2)
                pe.wait_ge(in_consts, 16)
                pe.wait_ge(made, 2)
                with pe.Fori(0, KD // 2) as i:
                    for s in range(2):
                        pe.wait_ge(lo_ready, 2 * i + (s + 1))
                        pe.wait_ge(x2_ready, 2 * i + (s + 1))
                        for k in range(KD):
                            pe.wait_ge(mix_lo, k + 1)
                            for b in range(NBLK):
                                cols = slice(b * BLK, (b + 1) * BLK)
                                last = split_products(nc, banks[:, 4 * s + b], w_hi[:, s, k], w_lo[:, s, k], m_hi[:, k, cols], m_lo[:, k, cols],
                                                      k == 0, k == KD - 1)
                        last.then_inc(tile_done, 1)
                pe.wait_ge(added, KD)
                pe.wait_ge(x2_ready, KD + 1)
                for b in range(NBLK):
                    nc.tensor.matmul(banks[:, b], mean_ones[:], sq_sum[:, b * BLK:(b + 1) * BLK], start=True, stop=False)
                pe.wait_ge(squared, KD)
                for b in range(NBLK):
                    nc.tensor.matmul(banks[:, b], mean_ones[:], squares[:, b * BLK:(b + 1) * BLK], start=False, stop=True).then_inc(mean_done, 1)


def feed_forward(nc, vec, mod, rms_all, w_gate_up, w_down, x2, yT):
    UP, DOWN = KF, 2 * KD
    UNITS = UP + DOWN
    HALF = KF // 2
    KHALVES = range(0, KD // 2), range(KD // 2, KD)
    with ExitStack() as ctx:
        sb = lambda n, s, d=F32: ctx.enter_context(nc.sbuf_tensor(n, s, d))
        ps = lambda n, s, d=F32: ctx.enter_context(nc.psum_tensor(n, s, d))
        sem = lambda n: ctx.enter_context(nc.semaphore(n))
        two = lambda n: [sem(n + "_even"), sem(n + "_odd")]
        h_hi, h_lo = sb("ff_h_hi", [P, KD, BLK], F32R), sb("ff_h_lo", [P, KD, BLK], F32R)
        a_hi, a_lo = sb("ff_a_hi", [P, KF, BLK], F32R), sb("ff_a_lo", [P, KF, BLK], F32R)
        x_blk = sb("ff_x_blk", [P, KD, BLK])
        w_raw = sb("ff_w_raw", [P, 2, 2 * KD * P])
        w_hi, w_lo = sb("ff_w_hi", [P, 2, 2 * KD * P], F32R), sb("ff_w_lo", [P, 2, 2 * KD * P], F32R)
        silu, gated = sb("ff_silu", [P, 2, BLK]), sb("ff_gated", [P, 2, BLK])
        x_res = sb("ff_x_res", [P, 2, BLK])
        y_out = gated
        scale_a = sb("ff_scale_a", [P, KD])
        g_ps, u_ps, d_ps = ps("ff_g_ps", [P, 2, BLK]), ps("ff_u_ps", [P, 2, BLK]), ps("ff_d_ps", [P, 2, BLK])
        up_w = lambda w, s: w[:, s].rearrange("p (g k n) -> p g k n", g=2, k=KD)
        down_w = lambda w, s: w[:, s, 0:HALF * P].rearrange("p (k n) -> p k n", k=HALF)
        size = lambda up: slice(0, 2 * KD * P) if up else slice(0, HALF * P)

        x_in, scaled, xn_ready, h_hi_ready, h_full, h_ready = sem("ff_x_in"), sem("ff_scaled"), sem("ff_xn_ready"), sem("ff_h_hi_ready"), sem("ff_h_full"), sem("ff_h_ready")
        w_in, hi_ready, lo_ready, unit_done = two("ff_w_in"), sem("ff_hi_ready"), sem("ff_lo_ready"), sem("ff_unit_done")
        silu_ready, gated_ready, a_hi_ready, a_ready = sem("ff_silu_ready"), sem("ff_gated_ready"), sem("ff_a_hi_ready"), sem("ff_a_ready")
        res_in, y_ready, stored = two("ff_res_in"), sem("ff_y_ready"), two("ff_stored")

        with nc.Block() as block:
            @block.sync
            def _(sp):
                sp.wait_ge(x_in, 16)
                with sp.Fori(0, NBLK) as t:
                    with sp.Fori(0, UP // 2) as i:
                        for s in range(2):
                            sp.wait_ge(lo_ready, UNITS * t + 2 * i + (s + 1))
                            sp.dma_start(w_raw[:, s], w_gate_up[bass.ds(2 * i + s, 1)].rearrange("o p n -> (o p) n")).then_inc(w_in[s], 16)
                    with sp.Fori(0, DOWN // 2) as i:
                        for s in range(2):
                            sp.wait_ge(lo_ready, UNITS * t + 2 * i + (UP + s + 1))
                            sp.dma_start(w_raw[:, s, size(False)], w_down[bass.ds(2 * i + s, 1)].rearrange("o p n -> (o p) n")).then_inc(w_in[s], 16)

            @block.gpsimd
            def _(pool):
                pool.sem_inc(lo_ready, 2)
                def low(up, s):
                    nc.gpsimd.tensor_tensor(w_lo[:, s, size(up)], w_raw[:, s, size(up)], w_hi[:, s, size(up)].bitcast(F32), ALU.subtract).then_inc(lo_ready, 1)
                with pool.Fori(0, NBLK) as t:
                    with pool.Fori(0, UP // 2) as i:
                        for s in range(2):
                            pool.wait_ge(hi_ready, UNITS * t + 2 * i + (s + 1))
                            low(True, s)
                    with pool.Fori(0, DOWN // 2) as i:
                        for s in range(2):
                            pool.wait_ge(hi_ready, UNITS * t + 2 * i + (UP + s + 1))
                            low(False, s)

            @block.scalar
            def _(act):
                def norm(t):
                    for w, ks in enumerate(KHALVES):
                        act.wait_ge(xn_ready, 2 * t + w + 1)
                        if t >= 1:
                            act.wait_ge(unit_done, UNITS * (t - 1) + UP + 2)
                        for k in ks:
                            last = nc.scalar.activation(h_hi[:, k], x_blk[:, k], ACT.Identity, bias=mod[:, SHIFT2 + k:SHIFT2 + k + 1], scale=scale_a[:, k:k + 1])
                        last.then_inc(h_hi_ready, 1)

                def load_block(t):
                    act.dma_start(x_blk[:], x2[:, :, t * BLK:(t + 1) * BLK].rearrange("k p n -> p k n")).then_inc(x_in, 16)

                def high(t, up, i, s, n):
                    act.wait_ge(w_in[s], 16 * (UNITS // 2) * t + 16 * i + (16 if up else 16 * (UP // 2) + 16))
                    act.wait_ge(unit_done, UNITS * t + n + 1)
                    nc.scalar.activation(w_hi[:, s, size(up)], w_raw[:, s, size(up)], ACT.Copy).then_inc(hi_ready, 1)

                def gate(t, s, n):
                    act.wait_ge(unit_done, UNITS * t + n + 3)
                    act.wait_ge(gated_ready, UP * t + n + 1)
                    nc.scalar.activation(silu[:, s], g_ps[:, s], ACT.Silu).then_inc(silu_ready, 1)

                def act_high(t, s, n, at):
                    act.wait_ge(gated_ready, UP * t + n + 3)
                    nc.scalar.activation(a_hi[:, at].rearrange("p o n -> p (o n)"), gated[:, s], ACT.Copy).then_inc(a_hi_ready, 1)

                def load_res(t, m, s):
                    act.dma_start(x_res[:, s], x2[m, :, t * BLK:(t + 1) * BLK].rearrange("o p n -> (o p) n")).then_inc(res_in[s], 16)

                def store(t, m, at, s):
                    act.wait_ge(y_ready, KD * t + m + 3)
                    act.dma_start(yT[at, :, t * BLK:(t + 1) * BLK].rearrange("o p n -> (o p) n"), y_out[:, s]).then_inc(stored[s], 16)

                for s in range(2):
                    act.sem_inc(stored[s], 16)
                load_block(0)
                norm(0)
                for s in range(2):
                    load_res(0, slice(s, s + 1), s)
                for t in range(NBLK):
                    for s in range(2):
                        high(t, True, 0, s, s)
                    if t + 1 < NBLK:
                        act.wait_ge(h_ready, 2 * t + 2)
                        load_block(t + 1)
                    if t >= 1:
                        store(t - 1, KD - 1, slice(KD - 1, KD), 1)
                        load_res(t, slice(1, 2), 1)
                    with act.Fori(1, UP // 2) as i:
                        for s in range(2):
                            gate(t, s, 2 * i + (s - 2))
                            high(t, True, i, s, 2 * i + s)
                            act_high(t, s, 2 * i + (s - 2), bass.ds(2 * i + (s - 2), 1))
                    for s in range(2):
                        gate(t, s, UP - 2 + s)
                        high(t, False, 0, s, UP + s)
                        act_high(t, s, UP - 2 + s, slice(UP - 2 + s, UP - 1 + s))
                    if t + 1 < NBLK:
                        norm(t + 1)
                    with act.Fori(0, KD // 2 - 1) as i:
                        for o in range(2):
                            for s in range(2):
                                high(t, False, 2 * i + (1 + o), s, 4 * i + (UP + 2 + 2 * o + s))
                            store(t, 2 * i + o, bass.ds(2 * i + o, 1), o)
                            load_res(t, bass.ds(2 * i + (o + 2), 1), o)
                    for s in range(2):
                        high(t, False, KD - 1, s, UP + DOWN - 2 + s)
                    store(t, KD - 2, slice(KD - 2, KD - 1), 0)
                    if t + 1 < NBLK:
                        load_res(t + 1, slice(0, 1), 0)
                store(NBLK - 1, KD - 1, slice(KD - 1, KD), 1)
                for s in range(2):
                    act.wait_ge(stored[s], 16 + 16 * NBLK * (KD // 2))

            @block.vector
            def _(dve):
                dve.sem_inc(gated_ready, 2)
                nc.vector.scalar_tensor_tensor(out=scale_a[:], in0=mod[:, SCALE2:SCALE2 + KD], scalar=1.0, in1=vec[:, VEC["g2"]:VEC["g2"] + KD],
                                               op0=ALU.add, op1=ALU.mult).then_inc(scaled, 1)
                dve.wait_ge(scaled, 1)

                def scale(t):
                    rstd = rms_all[:, t * BLK:(t + 1) * BLK]
                    nc.vector.reciprocal(rstd, rstd).then_inc(scaled, 1)
                    dve.wait_ge(scaled, t + 2)
                    dve.wait_ge(x_in, 16 * (t + 1))
                    for ks in KHALVES:
                        at = slice(ks[0], ks[-1] + 1)
                        nc.vector.tensor_tensor(x_blk[:, at], x_blk[:, at], rstd[:, None, :].to_broadcast([P, len(ks), BLK]), ALU.mult).then_inc(xn_ready, 1)

                def norm(t):
                    for w, ks in enumerate(KHALVES):
                        at = slice(ks[0], ks[-1] + 1)
                        dve.wait_ge(h_hi_ready, 2 * t + w + 1)
                        for k in ks:
                            last = nc.vector.tensor_scalar(x_blk[:, k], x_blk[:, k], scale_a[:, k:k + 1], mod[:, SHIFT2 + k:SHIFT2 + k + 1], ALU.mult, ALU.add)
                        last.then_inc(h_full, 1)
                        dve.wait_ge(h_full, 2 * t + w + 1)
                        nc.vector.tensor_tensor(h_lo[:, at], x_blk[:, at], h_hi[:, at].bitcast(F32), ALU.subtract).then_inc(h_ready, 1)

                scale(0)
                norm(0)
                for t in range(NBLK):
                    for s in range(2):
                        dve.wait_ge(stored[s], 16 * (KD // 2) * t + 16)
                    if t + 1 < NBLK:
                        scale(t + 1)
                    with dve.Fori(0, UP // 2) as i:
                        for s in range(2):
                            n = 2 * i + s
                            dve.wait_ge(silu_ready, UP * t + n + 1)
                            dve.wait_ge(a_ready, UP * t + n + 1)
                            nc.vector.tensor_tensor(gated[:, s], silu[:, s], u_ps[:, s], ALU.mult).then_inc(gated_ready, 1)
                            dve.wait_ge(a_hi_ready, UP * t + n + 1)
                            nc.vector.tensor_tensor(a_lo[:, bass.ds(n, 1)].rearrange("p o n -> p (o n)"), gated[:, s],
                                                    a_hi[:, bass.ds(n, 1)].rearrange("p o n -> p (o n)").bitcast(F32), ALU.subtract).then_inc(a_ready, 1)
                    if t + 1 < NBLK:
                        norm(t + 1)
                    with dve.Fori(0, KD // 2) as i:
                        for s in range(2):
                            dve.wait_ge(unit_done, UNITS * t + 4 * i + (UP + 2 * s + 4))
                            dve.wait_ge(res_in[s], 16 * (KD // 2) * t + 16 * i + 16)
                            dve.wait_ge(stored[s], 16 * (KD // 2) * t + 16 * i + 16)
                            nc.vector.scalar_tensor_tensor(out=y_out[:, s], in0=d_ps[:, s], scalar=mod[:, bass.ds(2 * i + (s + GATE2), 1)], in1=x_res[:, s],
                                                           op0=ALU.mult, op1=ALU.add).then_inc(y_ready, 1)

            @block.tensor
            def _(pe):
                pe.sem_inc(unit_done, 2)
                pe.sem_inc(a_ready, 2)
                pe.sem_inc(y_ready, 2)
                for t in range(NBLK):
                    pe.wait_ge(h_ready, 2 * t + 2)
                    with pe.Fori(0, UP // 2) as i:
                        for s in range(2):
                            n = 2 * i + s
                            pe.wait_ge(lo_ready, UNITS * t + n + 3)
                            pe.wait_ge(a_ready, UP * t + n + 1)
                            for g, out in ((0, g_ps[:, s]), (1, u_ps[:, s])):
                                for k in range(KD):
                                    last = split_products(nc, out, up_w(w_hi, s)[:, g, k], up_w(w_lo, s)[:, g, k], h_hi[:, k], h_lo[:, k], k == 0, k == KD - 1)
                            last.then_inc(unit_done, 1)
                    with pe.Fori(0, KD // 2) as i:
                        for m in range(2):
                            pe.wait_ge(y_ready, KD * t + 2 * i + (m + 1))
                            for s in range(2):
                                pe.wait_ge(lo_ready, UNITS * t + 4 * i + (UP + 2 * m + s + 3))
                                if s == 1:
                                    pe.wait_ge(a_ready, UP * (t + 1) + 2)
                                for k in range(HALF):
                                    f = HALF * s + k
                                    last = split_products(nc, d_ps[:, m], down_w(w_hi, s)[:, k], down_w(w_lo, s)[:, k], a_hi[:, f], a_lo[:, f], f == 0, f == KF - 1)
                                last.then_inc(unit_done, 1)


def lay_out(inputs):
    a = {k: np.asarray(v) for k, v in inputs.items()}
    f32 = np.float32
    cols = lambda v, n: v.reshape(n, P).T
    w_in = a["w_in"][0]
    cut = np.cumsum([LRU_WIDTH, LRU_WIDTH, FOX_T * P, FOX_T * P, FOX_T * P, FOX_HEADS, GLA_T * P, GLA_T * P, GLA_T * P, GLA_RANK, GLA_T * P])
    xa, ya, fq, fk, fv, ff, gq, gk, gv, glow, gg = np.split(w_in, cut[:-1], axis=1)
    misc = np.zeros((D_MODEL, P), f32)
    misc[:, 0:GLA_RANK] = glow
    misc[:, FF_ROW:FF_ROW + FOX_HEADS] = ff
    w_in = np.concatenate([xa, ya, fq, fk, fv, gq, gk, gv, gg, misc], axis=1)
    tiles = lambda w, kt, mt: np.ascontiguousarray(w.reshape(kt, P, mt, -1).transpose(2, 1, 0, 3))
    blocks = np.zeros((2, LRU_T, P, P), f32)
    for g, name in enumerate(("lru_w_r", "lru_w_i")):
        for n in range(LRU_WIDTH // HEAD_DIM):
            o = HEAD_DIM * (n % 2)
            blocks[g, n // 2, o:o + HEAD_DIM, o:o + HEAD_DIM] = a[name][0, n]
    b_f = np.zeros((P, 1), f32)
    b_f[FF_ROW:FF_ROW + FOX_HEADS, 0] = a["fox_b_f"][0]
    twice = lambda v: np.concatenate([v, v]).reshape(P, 1)
    parts = {
        "c": cols(a["c"][0], KD), "g1": cols(a["norm1_gain"][0], KD), "g2": cols(a["norm2_gain"][0], KD),
        "b_mod": cols(a["b_mod"][0], 6 * KD), "conv_w": np.concatenate([cols(w, LRU_T) for w in a["conv_w"][0]], axis=1),
        "conv_b": cols(a["conv_b"][0], LRU_T), "b_r": cols(a["lru_b_r"][0], LRU_T), "b_i": cols(a["lru_b_i"][0], LRU_T),
        "lam": cols(a["lru_lambda"][0], LRU_T), "q_gain": twice(a["fox_q_gain"][0]), "k_gain": twice(a["fox_k_gain"][0]),
        "b_alpha": cols(a["gla_b_alpha"][0], GLA_T), "out_gain": twice(a["gla_out_gain"][0]), "b_f": b_f,
    }
    gate_up = a["ffn_w_gate_up"][0].reshape(KD, P, 2, KF, P).transpose(3, 1, 2, 0, 4)
    down = a["ffn_w_down"][0].reshape(2, KF // 2, P, KD, P).transpose(3, 0, 2, 1, 4)
    p, q = np.arange(P)[:, None], np.arange(P)[None, :]
    same_head = p // HEAD_DIM == q // HEAD_DIM
    consts = np.concatenate([
        np.full((P, P), 1.0 / D_MODEL), same_head / HEAD_DIM, p == q,
        np.where(q <= p, 0.0, MASKED),
        np.where(p <= q, 0.0, MASKED),
        same_head & (p <= q),
    ], axis=1).astype(f32)
    tiles6 = 2 * FOX_T
    head_of = 2 * np.arange(tiles6)[None, :] + np.arange(P)[:, None] // HEAD_DIM
    one_hot = head_of[:, :, None] == np.arange(2 * FOX_HEADS)
    fox_rows = np.zeros((P, tiles6 * 2 * FOX_HEADS + tiles6 * P), f32)
    fox_rows[:, :tiles6 * 2 * FOX_HEADS] = (one_hot / HEAD_DIM).reshape(P, -1)
    fox_rows[:2 * FOX_HEADS, tiles6 * 2 * FOX_HEADS:] = one_hot.transpose(2, 1, 0).reshape(2 * FOX_HEADS, -1)
    return {
        "xT": np.ascontiguousarray(a["x"][0].T).reshape(KD, P, SEQ),
        "vec": np.ascontiguousarray(np.concatenate([parts[k] for k in VEC], axis=1)),
        "w_mod": tiles(a["w_mod"][0], KD, MOD_CHUNKS),
        "w_in": tiles(w_in, KD, N_PROJ).reshape(N_PROJ, P, KD * P),
        "w_gates": blocks,
        "w_alpha": np.ascontiguousarray(a["gla_w_alpha"][0]),
        "w_out": tiles(a["w_out"][0], KD, KD).reshape(KD, P, KD * P),
        "w_gate_up": np.ascontiguousarray(gate_up).reshape(KF, P, 2 * KD * P),
        "w_down": np.ascontiguousarray(down).reshape(2 * KD, P, (KF // 2) * P),
        "consts": consts,
        "fox_rows": fox_rows,
    }


def build(nc, xT, vec_in, w_mod, w_in, w_gates, w_alpha, w_out, w_gate_up, w_down, consts, fox_rows, yT):
    proj = nc.dram_tensor("proj_dram", [N_PROJ, P, SEQ], F32).ap()
    xT = xT.rearrange("k p n -> p k n")
    with ExitStack() as ctx:
        vec = ctx.enter_context(nc.sbuf_tensor("vec", [P, N_VEC], F32))
        mod = ctx.enter_context(nc.sbuf_tensor("mod", [P, 6 * KD], F32))
        mix = nc.dram_tensor("mix_dram", [MIX_T, P, SEQ], F32).ap()
        project_in_and_recur(nc, vec, mod, xT, w_mod, w_in, w_gates, consts, vec_in, proj, mix)
        x2 = nc.dram_tensor("x2_dram", [KD, P, SEQ], F32).ap()
        q_split = nc.dram_tensor("q_split_dram", [FOX_HEADS, 2, HEAD_DIM, SEQ], F32).ap()
        k_split = nc.dram_tensor("k_split_dram", [FOX_HEADS, 2, HEAD_DIM, SEQ], F32).ap()
        bias_split = nc.dram_tensor("bias_split_dram", [FOX_HEADS, 2, SEQ], F32).ap()
        with nc.sbuf_tensor("v_nat", [P, FOX_HEADS, SEQ // P, 2 * HEAD_DIM], F32R) as v_nat:
            fox_operands(nc, vec, consts, fox_rows, proj, q_split, k_split, bias_split, v_nat)
            forgetting_attention(nc, consts, q_split, k_split, bias_split, v_nat, mix)
        gated_linear_attention(nc, vec, consts, w_alpha, proj, mix)
        rms_all = ctx.enter_context(nc.sbuf_tensor("rms_all", [P, SEQ], F32))
        project_out(nc, vec, mod, rms_all, xT, w_out, consts, mix, x2)
        feed_forward(nc, vec, mod, rms_all, w_gate_up, w_down, x2, yT)


def kernel(**inputs):
    import concourse.bacc as _bacc
    from concourse.bass_utils import run_bass_kernel_spmd as _run

    arrays = lay_out(inputs)
    nc = _bacc.Bacc("TRN2", target_bir_lowering=False, num_devices=1)
    args = [nc.dram_tensor(f"in_{name}", a.shape, mybir.dt.from_np(a.dtype), kind="ExternalInput").ap() for name, a in arrays.items()]
    args.append(nc.dram_tensor("out_yT", (KD, P, SEQ), F32, kind="ExternalOutput").ap())
    build(nc, *args)
    r = _run(nc, [{f"in_{name}": a for name, a in arrays.items()}], core_ids=[0])
    y = np.asarray(r.results[0]["out_yT"])
    return np.ascontiguousarray(y.reshape(D_MODEL, SEQ).T).reshape(1, SEQ, D_MODEL)
```
